# Optimizing a Trainium2 kernel written in Bass

```python
import jax, jax.numpy as jnp
from jax import lax
import numpy as np

D_MODEL = 1024
BATCH = 1
SEQ = 512
DEPTH = 2

BLOCK_Q = 128
EPS = 1e-6
NEG_INF = -1e30
ROPE_THETA = 10000.0

MLA_HEADS = 8
MLA_Q_RANK = 256
MLA_KV_RANK = 128
MLA_NOPE = 64
MLA_ROPE = 32
MLA_QK = MLA_NOPE + MLA_ROPE
MLA_V = 64
SB_HEADS = 8
SB_DIM = 64
SB_WIDTH = SB_HEADS * SB_DIM
FOX_HEADS = 16
FOX_DIM = 64
FOX_WIDTH = FOX_HEADS * FOX_DIM
D_FF = ((8 * D_MODEL // 3 + 255) // 256) * 256

EVEN_IN = MLA_Q_RANK + MLA_KV_RANK + MLA_ROPE + 3 * SB_WIDTH
EVEN_OUT = MLA_HEADS * MLA_V + SB_WIDTH
ODD_IN = 3 * FOX_WIDTH + FOX_HEADS
ODD_OUT = FOX_WIDTH


def rms_norm(x, g):
    xf = x.astype(jnp.float32)
    y = xf * lax.rsqrt(jnp.mean(xf * xf, axis=-1, keepdims=True) + EPS)
    return (y * g.astype(jnp.float32)).astype(x.dtype)

def split_last(x, sizes):
    return jnp.split(x, [int(v) for v in np.cumsum(sizes)[:-1]], axis=-1)

def heads_first(x):
    return x.transpose(0, 2, 1, 3)

def merge_heads(x):
    b, h, s, d = x.shape
    return x.transpose(0, 2, 1, 3).reshape(b, s, h * d)

def rope_tail(x, positions):
    nope, r = x[..., :-MLA_ROPE], x[..., -MLA_ROPE:]
    half = MLA_ROPE // 2
    inv_freq = ROPE_THETA ** (-jnp.arange(half, dtype=jnp.float32) / half)
    ang = positions.astype(jnp.float32)[..., None] * inv_freq
    cos, sin = jnp.cos(ang)[:, :, None, :], jnp.sin(ang)[:, :, None, :]
    r1, r2 = r[..., :half].astype(jnp.float32), r[..., half:].astype(jnp.float32)
    rot = jnp.concatenate([r1 * cos - r2 * sin, r2 * cos + r1 * sin], axis=-1)
    return jnp.concatenate([nope, rot.astype(x.dtype)], axis=-1)

def sweep_query_blocks(block_fn, q):
    b, h, s, _ = q.shape
    out = lax.map(block_fn, jnp.arange(s // BLOCK_Q))
    nb, _, _, bq, dv = out.shape
    return out.transpose(1, 2, 0, 3, 4).reshape(b, h, nb * bq, dv)

def causal_softmax_attention(q, k, v, scale, decay=None):
    s = k.shape[2]
    k_idx = jnp.arange(s)

    def block(i):
        start = i * BLOCK_Q
        qb = lax.dynamic_slice_in_dim(q, start, BLOCK_Q, axis=2)
        logits = jnp.einsum('bhqd,bhkd->bhqk', qb, k).astype(jnp.float32) * scale
        if decay is not None:
            cq = lax.dynamic_slice_in_dim(decay, start, BLOCK_Q, axis=2)
            logits = logits + cq[..., :, None] - decay[..., None, :]
        q_idx = start + jnp.arange(BLOCK_Q)
        mask = k_idx[None, :] <= q_idx[:, None]
        p = jax.nn.softmax(jnp.where(mask, logits, NEG_INF), axis=-1)
        return jnp.einsum('bhqk,bhkd->bhqd', p.astype(v.dtype), v)

    return sweep_query_blocks(block, q)

def stick_breaking_attention(q, k, v):
    s = k.shape[2]
    scale = q.shape[-1] ** -0.5
    k_idx = jnp.arange(s)

    def block(i):
        start = i * BLOCK_Q
        qb = lax.dynamic_slice_in_dim(q, start, BLOCK_Q, axis=2)
        z = jnp.einsum('bhqd,bhkd->bhqk', qb, k).astype(jnp.float32) * scale
        q_idx = start + jnp.arange(BLOCK_Q)
        mask = k_idx[None, :] < q_idx[:, None]
        log_beta = jax.nn.log_sigmoid(z)
        log_1m_beta = jnp.where(mask, jax.nn.log_sigmoid(-z), 0.0)
        suffix = lax.cumsum(log_1m_beta, axis=3, reverse=True) - log_1m_beta
        a = jnp.where(mask, jnp.exp(log_beta + suffix), 0.0)
        return jnp.einsum('bhqk,bhkd->bhqd', a.astype(v.dtype), v)

    return sweep_query_blocks(block, q)

def even_mixer(h, positions, w_in, q_a_norm, w_q_up, kv_a_norm, w_kv_up, q_norm, k_norm, w_o):
    b, s, _ = h.shape
    proj = h @ w_in
    cq, ckv, k_rope, sb_qkv = split_last(proj, [MLA_Q_RANK, MLA_KV_RANK, MLA_ROPE, 3 * SB_WIDTH])
    q = (rms_norm(cq, q_a_norm) @ w_q_up).reshape(b, s, MLA_HEADS, MLA_QK)
    kv = (rms_norm(ckv, kv_a_norm) @ w_kv_up).reshape(b, s, MLA_HEADS, MLA_NOPE + MLA_V)
    k_nope, v = kv[..., :MLA_NOPE], kv[..., MLA_NOPE:]
    k_rope = jnp.broadcast_to(k_rope[:, :, None, :], (b, s, MLA_HEADS, MLA_ROPE))
    k = jnp.concatenate([k_nope, k_rope], axis=-1)
    q = rope_tail(rms_norm(q, q_norm), positions)
    k = rope_tail(rms_norm(k, k_norm), positions)
    mla = causal_softmax_attention(heads_first(q), heads_first(k), heads_first(v), MLA_QK ** -0.5)
    sq, sk, sv = [heads_first(t.reshape(b, s, SB_HEADS, SB_DIM)) for t in jnp.split(sb_qkv, 3, axis=-1)]
    sb = stick_breaking_attention(sq, sk, sv)
    o = jnp.concatenate([merge_heads(mla), merge_heads(sb)], axis=-1)
    return o @ w_o

def odd_mixer(h, w_in, f_bias, q_norm, k_norm, w_o):
    b, s, _ = h.shape
    proj = h @ w_in
    q, k, v, f_logit = split_last(proj, [FOX_WIDTH, FOX_WIDTH, FOX_WIDTH, FOX_HEADS])
    q = rms_norm(q.reshape(b, s, FOX_HEADS, FOX_DIM), q_norm)
    k = rms_norm(k.reshape(b, s, FOX_HEADS, FOX_DIM), k_norm)
    v = v.reshape(b, s, FOX_HEADS, FOX_DIM)
    log_f = jax.nn.log_sigmoid(f_logit.astype(jnp.float32) + f_bias.astype(jnp.float32))
    decay = lax.cumsum(log_f, axis=1).transpose(0, 2, 1)
    o = causal_softmax_attention(heads_first(q), heads_first(k), heads_first(v), FOX_DIM ** -0.5, decay)
    return merge_heads(o) @ w_o

def swiglu(h, w_gate, w_up, w_down):
    return (jax.nn.silu(h @ w_gate) * (h @ w_up)) @ w_down

def first_inputs(seed: int = 0) -> dict:
    key = jax.random.key(seed)
    ks = iter(jax.random.split(key, 32))

    def dense(shape):
        return jax.random.normal(next(ks), shape, jnp.float32) * shape[0] ** -0.5

    def gain(n):
        return 1.0 + 0.1 * jax.random.normal(next(ks), (n,), jnp.float32)

    x = jax.random.normal(next(ks), (BATCH, SEQ, D_MODEL), jnp.float32)
    offsets = jax.random.randint(next(ks), (BATCH, 1), 0, SEQ, dtype=jnp.int32)
    positions = (offsets + jnp.arange(SEQ, dtype=jnp.int32)[None, :]).astype(jnp.int32)
    return {
        'x': x,
        'positions': positions,
        'l0_attn_norm': gain(D_MODEL),
        'l0_w_in': dense((D_MODEL, EVEN_IN)),
        'l0_mla_q_a_norm': gain(MLA_Q_RANK),
        'l0_mla_w_q_up': dense((MLA_Q_RANK, MLA_HEADS * MLA_QK)),
        'l0_mla_kv_a_norm': gain(MLA_KV_RANK),
        'l0_mla_w_kv_up': dense((MLA_KV_RANK, MLA_HEADS * (MLA_NOPE + MLA_V))),
        'l0_mla_q_norm': gain(MLA_QK),
        'l0_mla_k_norm': gain(MLA_QK),
        'l0_w_o': dense((EVEN_OUT, D_MODEL)),
        'l0_ffn_norm': gain(D_MODEL),
        'l0_w_gate': dense((D_MODEL, D_FF)),
        'l0_w_up': dense((D_MODEL, D_FF)),
        'l0_w_down': dense((D_FF, D_MODEL)),
        'l1_attn_norm': gain(D_MODEL),
        'l1_w_in': dense((D_MODEL, ODD_IN)),
        'l1_fox_f_bias': 3.0 + 0.5 * jax.random.normal(next(ks), (FOX_HEADS,), jnp.float32),
        'l1_fox_q_norm': gain(FOX_DIM),
        'l1_fox_k_norm': gain(FOX_DIM),
        'l1_w_o': dense((ODD_OUT, D_MODEL)),
        'l1_ffn_norm': gain(D_MODEL),
        'l1_w_gate': dense((D_MODEL, D_FF)),
        'l1_w_up': dense((D_MODEL, D_FF)),
        'l1_w_down': dense((D_FF, D_MODEL)),
    }

def first_block(x, positions,
              l0_attn_norm, l0_w_in, l0_mla_q_a_norm, l0_mla_w_q_up, l0_mla_kv_a_norm,
              l0_mla_w_kv_up, l0_mla_q_norm, l0_mla_k_norm, l0_w_o,
              l0_ffn_norm, l0_w_gate, l0_w_up, l0_w_down,
              l1_attn_norm, l1_w_in, l1_fox_f_bias, l1_fox_q_norm, l1_fox_k_norm, l1_w_o,
              l1_ffn_norm, l1_w_gate, l1_w_up, l1_w_down):
    mixer_params = (
        (l0_attn_norm, l0_w_in, l0_mla_q_a_norm, l0_mla_w_q_up, l0_mla_kv_a_norm,
         l0_mla_w_kv_up, l0_mla_q_norm, l0_mla_k_norm, l0_w_o),
        (l1_attn_norm, l1_w_in, l1_fox_f_bias, l1_fox_q_norm, l1_fox_k_norm, l1_w_o),
    )
    ffn_params = (
        (l0_ffn_norm, l0_w_gate, l0_w_up, l0_w_down),
        (l1_ffn_norm, l1_w_gate, l1_w_up, l1_w_down),
    )
    for layer in range(DEPTH):
        norm_g, *mp = mixer_params[layer]
        h = rms_norm(x, norm_g)
        if layer % 2 == 0:
            x = x + even_mixer(h, positions, *mp)
        else:
            x = x + odd_mixer(h, *mp)
        f_norm, w_gate, w_up, w_down = ffn_params[layer]
        x = x + swiglu(rms_norm(x, f_norm), w_gate, w_up, w_down)
    return x


DEPTH_2 = 1

N_MEM = 256
MLSTM_HEADS = 4
MLSTM_HEAD_DIM = D_MODEL // MLSTM_HEADS
MLSTM_DIM = MLSTM_HEADS * MLSTM_HEAD_DIM
MLSTM_CHUNK = 128
CONV_WIDTH = 4
SGU_GROUPS = 8
SGU_GROUP_DIM = D_MODEL // SGU_GROUPS
SGU_DIM = SGU_GROUPS * SGU_GROUP_DIM
SGU_CHUNK = 128
N_BRANCH = 2
IN_WIDTHS = (2 * MLSTM_DIM, MLSTM_DIM, MLSTM_DIM, MLSTM_HEADS, MLSTM_HEADS, SGU_DIM, SGU_DIM, N_BRANCH * D_MODEL)
IN_DIM = sum(IN_WIDTHS)
SPLIT_POINTS = tuple(int(s) for s in np.cumsum(IN_WIDTHS)[:-1])
XATTN_HEADS = 4
XATTN_HEAD_DIM = D_MODEL // XATTN_HEADS
XATTN_DIM = XATTN_HEADS * XATTN_HEAD_DIM
MOE_GROUPS = 4
EXPERTS_PER_GROUP = 8
N_EXPERTS = MOE_GROUPS * EXPERTS_PER_GROUP
MOE_TOPK = 2
EXPERT_FF = D_MODEL // 2
MOE_BLOCK = 128


def rmsnorm(x, g):
    x32 = x.astype(jnp.float32)
    y = x32 * lax.rsqrt(jnp.mean(x32 * x32, axis=-1, keepdims=True) + EPS)
    return (y * g.astype(jnp.float32)).astype(x.dtype)

def causal_depthwise_conv(x, w, b):
    c = x.shape[-1]
    y = lax.conv_general_dilated(x, w[:, None, :].astype(x.dtype), window_strides=(1,),
                                 padding=[(CONV_WIDTH - 1, 0)],
                                 dimension_numbers=('NWC', 'WIO', 'NWC'),
                                 feature_group_count=c)
    return y + b.astype(x.dtype)

def mlstm_chunkwise(q, k, v, i_pre, f_pre):
    B, S, H, dh = q.shape
    L = MLSTM_CHUNK
    nc = S // L
    f32 = jnp.float32

    def to_chunks(a):
        return a.astype(f32).reshape(B, nc, L, H, dh).transpose(1, 0, 3, 2, 4)

    qc = to_chunks(q)
    kc = to_chunks(k) * (dh ** -0.5)
    vc = to_chunks(v)
    logf = jax.nn.log_sigmoid(f_pre.astype(f32)).reshape(B, nc, L, H).transpose(1, 0, 3, 2)
    ig = i_pre.astype(f32).reshape(B, nc, L, H).transpose(1, 0, 3, 2)
    causal = jnp.tril(jnp.ones((L, L), dtype=bool))

    def step(carry, inp):
        C, n, m = carry
        q_, k_, v_, lf, ic = inp
        b = jnp.cumsum(lf, axis=-1)
        dmat = jnp.where(causal, b[..., :, None] - b[..., None, :] + ic[..., None, :], -jnp.inf)
        inter = b + m[..., None]
        m_t = jnp.maximum(inter, jnp.max(dmat, axis=-1))
        dexp = jnp.exp(dmat - m_t[..., None])
        inter_w = jnp.exp(inter - m_t)
        s = jnp.einsum('bhtd,bhsd->bhts', q_, k_) * dexp
        num = jnp.einsum('bhts,bhsd->bhtd', s, v_) + inter_w[..., None] * jnp.einsum('bhtd,bhde->bhte', q_, C)
        den = jnp.sum(s, axis=-1) + inter_w * jnp.einsum('bhtd,bhd->bht', q_, n)
        h = num / jnp.maximum(jnp.abs(den), jnp.exp(-m_t))[..., None]
        b_last = b[..., -1]
        w_log = b_last[..., None] - b + ic
        m_new = jnp.maximum(b_last + m, jnp.max(w_log, axis=-1))
        decay = jnp.exp(b_last + m - m_new)
        ws = jnp.exp(w_log - m_new[..., None])
        C_new = decay[..., None, None] * C + jnp.einsum('bhs,bhsd,bhse->bhde', ws, k_, v_)
        n_new = decay[..., None] * n + jnp.einsum('bhs,bhsd->bhd', ws, k_)
        return (C_new, n_new, m_new), h

    init = (jnp.zeros((B, H, dh, dh), f32), jnp.zeros((B, H, dh), f32), jnp.zeros((B, H), f32))
    _, hs = lax.scan(step, init, (qc, kc, vc, logf, ig))
    return hs.transpose(1, 0, 3, 2, 4).reshape(B, S, H, dh).astype(q.dtype)

def spatial_gating(u, v, sgu_norm_g, w_s, b_s):
    B, S, _ = u.shape
    nc = S // SGU_CHUNK
    u = jax.nn.gelu(u)
    v = rmsnorm(jax.nn.gelu(v), sgu_norm_g)
    vb = v.reshape(B, nc, SGU_CHUNK, SGU_GROUPS, SGU_GROUP_DIM)
    w_causal = jnp.tril(w_s).astype(v.dtype)
    mixed = jnp.einsum('gts,bcsgd->bctgd', w_causal, vb) + b_s.T.astype(v.dtype)[:, :, None]
    return u * mixed.reshape(B, S, SGU_DIM)

def hybrid_mixer(xn, w_in, b_gate, b_if, conv_w, conv_b, mh_norm_g, sgu_norm_g, w_s, b_s, w_out):
    B, S, _ = xn.shape
    proj = xn @ w_in
    qk, v, o, i_pre, f_pre, u, sv, gates = jnp.split(proj, SPLIT_POINTS, axis=-1)
    qk = jax.nn.silu(causal_depthwise_conv(qk, conv_w, conv_b))
    q, k = jnp.split(qk, 2, axis=-1)
    b_i, b_f = jnp.split(b_if, 2)
    hd = (B, S, MLSTM_HEADS, MLSTM_HEAD_DIM)
    h = mlstm_chunkwise(q.reshape(hd), k.reshape(hd), v.reshape(hd), i_pre + b_i, f_pre + b_f)
    y_a = rmsnorm(h, mh_norm_g.reshape(MLSTM_HEADS, MLSTM_HEAD_DIM)).reshape(B, S, MLSTM_DIM) * jax.nn.sigmoid(o)
    y_b = spatial_gating(u, sv, sgu_norm_g, w_s, b_s)
    g_a, g_b = jnp.split(jax.nn.sigmoid(gates + b_gate), 2, axis=-1)
    return (g_a * y_a + g_b * y_b) @ w_out

def memory_cross_attention(xn, mn, w_xq, w_xkv, w_xo):
    B, S, _ = xn.shape
    M = mn.shape[1]
    q = (xn @ w_xq).reshape(B, S, XATTN_HEADS, XATTN_HEAD_DIM)
    k, v = jnp.split(mn @ w_xkv, 2, axis=-1)
    k = k.reshape(B, M, XATTN_HEADS, XATTN_HEAD_DIM)
    v = v.reshape(B, M, XATTN_HEADS, XATTN_HEAD_DIM)
    scores = jnp.einsum('bshd,bmhd->bhsm', q, k).astype(jnp.float32) * (XATTN_HEAD_DIM ** -0.5)
    p = jax.nn.softmax(scores, axis=-1).astype(v.dtype)
    out = jnp.einsum('bhsm,bmhd->bshd', p, v).reshape(B, S, XATTN_DIM)
    return out @ w_xo

def hierarchical_moe(xn, w_rg, b_rg, w_re, b_re, w1, w3, w2):
    B, S, D = xn.shape
    N = B * S
    xt = xn.reshape(N, D)
    g_logits = (xt @ w_rg + b_rg).astype(jnp.float32)
    g_idx = jnp.argmax(g_logits, axis=-1)
    p_g = jnp.take_along_axis(jax.nn.softmax(g_logits, axis=-1), g_idx[:, None], axis=1)
    e_logits = (xt @ w_re + b_re).astype(jnp.float32).reshape(N, MOE_GROUPS, EXPERTS_PER_GROUP)
    e_in_group = jnp.take_along_axis(e_logits, g_idx[:, None, None], axis=1)[:, 0]
    top_v, top_i = lax.top_k(e_in_group, MOE_TOPK)
    gate = p_g * jax.nn.softmax(top_v, axis=-1)
    expert = g_idx[:, None].astype(jnp.int32) * EXPERTS_PER_GROUP + top_i.astype(jnp.int32)

    A = N * MOE_TOPK
    e_flat = expert.reshape(A)
    tok_flat = jnp.repeat(jnp.arange(N, dtype=jnp.int32), MOE_TOPK)
    order = jnp.argsort(e_flat)
    e_sorted = e_flat[order]
    counts = jnp.bincount(e_flat, length=N_EXPERTS)
    starts = jnp.cumsum(counts) - counts
    padded = (counts + MOE_BLOCK - 1) // MOE_BLOCK * MOE_BLOCK
    pends = jnp.cumsum(padded)
    pstarts = pends - padded
    dest_sorted = (pstarts[e_sorted] + jnp.arange(A, dtype=jnp.int32) - starts[e_sorted]).astype(jnp.int32)
    n_blocks = -(-A // MOE_BLOCK) + N_EXPERTS
    P = n_blocks * MOE_BLOCK
    buf_tok = jnp.zeros((P,), jnp.int32).at[dest_sorted].set(tok_flat[order])
    block_expert = jnp.minimum(
        jnp.searchsorted(pends, jnp.arange(n_blocks, dtype=jnp.int32) * MOE_BLOCK, side='right'),
        N_EXPERTS - 1).astype(jnp.int32)

    def block_ffn(args):
        tok, e = args
        xb = xt[tok]
        hb = jax.nn.silu(xb @ w1[e]) * (xb @ w3[e])
        return hb @ w2[e]

    out_buf = lax.map(block_ffn, (buf_tok.reshape(n_blocks, MOE_BLOCK), block_expert)).reshape(P, D)
    dest = jnp.zeros((A,), jnp.int32).at[order].set(dest_sorted)
    y_assign = out_buf[dest].reshape(N, MOE_TOPK, D)
    y = jnp.einsum('nk,nkd->nd', gate.astype(xt.dtype), y_assign)
    return y.reshape(B, S, D)

def second_inputs(seed: int = 0) -> dict:
    key = jax.random.key(seed)
    ks = jax.random.split(key, 32)
    D, L = D_MODEL, DEPTH_2

    def nrm(k, shape, scale):
        return jax.random.normal(k, shape, jnp.float32) * scale

    def gain(k, shape):
        return 1.0 + 0.02 * jax.random.normal(k, shape, jnp.float32)

    b_i = nrm(ks[4], (L, MLSTM_HEADS), 0.1)
    b_f = jnp.linspace(3.0, 6.0, MLSTM_HEADS, dtype=jnp.float32)[None, :] + nrm(ks[5], (L, MLSTM_HEADS), 0.1)
    return {
        'x': nrm(ks[0], (BATCH, SEQ, D), 1.0),
        'mem': nrm(ks[1], (BATCH, N_MEM, D), 1.0),
        'norm_mix_g': gain(ks[2], (L, D)),
        'w_in': nrm(ks[3], (L, D, IN_DIM), D ** -0.5),
        'b_gate': nrm(ks[6], (L, N_BRANCH * D), 0.02),
        'b_if': jnp.concatenate([b_i, b_f], axis=-1),
        'conv_w': nrm(ks[7], (L, CONV_WIDTH, 2 * MLSTM_DIM), CONV_WIDTH ** -0.5),
        'conv_b': nrm(ks[8], (L, 2 * MLSTM_DIM), 0.02),
        'mh_norm_g': gain(ks[9], (L, MLSTM_DIM)),
        'sgu_norm_g': gain(ks[10], (L, SGU_DIM)),
        'w_s': nrm(ks[11], (L, SGU_GROUPS, SGU_CHUNK, SGU_CHUNK), SGU_CHUNK ** -0.5),
        'b_s': gain(ks[12], (L, SGU_GROUPS, SGU_CHUNK)),
        'w_out': nrm(ks[13], (L, D, D), D ** -0.5),
        'norm_x_g': gain(ks[14], (L, D)),
        'norm_mem_g': gain(ks[15], (L, D)),
        'w_xq': nrm(ks[16], (L, D, XATTN_DIM), D ** -0.5),
        'w_xkv': nrm(ks[17], (L, D, 2 * XATTN_DIM), D ** -0.5),
        'w_xo': nrm(ks[18], (L, XATTN_DIM, D), XATTN_DIM ** -0.5),
        'norm_moe_g': gain(ks[19], (L, D)),
        'w_rg': nrm(ks[20], (L, D, MOE_GROUPS), D ** -0.5),
        'b_rg': nrm(ks[21], (L, MOE_GROUPS), 0.01),
        'w_re': nrm(ks[22], (L, D, N_EXPERTS), D ** -0.5),
        'b_re': nrm(ks[23], (L, N_EXPERTS), 0.01),
        'w1': nrm(ks[24], (L, N_EXPERTS, D, EXPERT_FF), D ** -0.5),
        'w3': nrm(ks[25], (L, N_EXPERTS, D, EXPERT_FF), D ** -0.5),
        'w2': nrm(ks[26], (L, N_EXPERTS, EXPERT_FF, D), EXPERT_FF ** -0.5),
        'norm_f_g': gain(ks[27], (D,)),
    }

def second_block(x, mem, norm_mix_g, w_in, b_gate, b_if, conv_w, conv_b, mh_norm_g, sgu_norm_g, w_s, b_s, w_out,
              norm_x_g, norm_mem_g, w_xq, w_xkv, w_xo, norm_moe_g, w_rg, b_rg, w_re, b_re, w1, w3, w2, norm_f_g):
    for l in range(DEPTH_2):
        x = x + hybrid_mixer(rmsnorm(x, norm_mix_g[l]), w_in[l], b_gate[l], b_if[l], conv_w[l], conv_b[l],
                             mh_norm_g[l], sgu_norm_g[l], w_s[l], b_s[l], w_out[l])
        x = x + memory_cross_attention(rmsnorm(x, norm_x_g[l]), rmsnorm(mem, norm_mem_g[l]),
                                       w_xq[l], w_xkv[l], w_xo[l])
        x = x + hierarchical_moe(rmsnorm(x, norm_moe_g[l]), w_rg[l], b_rg[l], w_re[l], b_re[l],
                                 w1[l], w3[l], w2[l])
    return rmsnorm(x, norm_f_g)


def setup_inputs(seed=0):
    out = dict(first_inputs(seed))
    for name, value in second_inputs(seed + 1).items():
        if name != "x":
            out[name + "_2"] = value
    return out


def reference(
    x, positions, l0_attn_norm, l0_w_in, l0_mla_q_a_norm, l0_mla_w_q_up, l0_mla_kv_a_norm,
    l0_mla_w_kv_up, l0_mla_q_norm, l0_mla_k_norm, l0_w_o, l0_ffn_norm, l0_w_gate, l0_w_up,
    l0_w_down, l1_attn_norm, l1_w_in, l1_fox_f_bias, l1_fox_q_norm, l1_fox_k_norm, l1_w_o,
    l1_ffn_norm, l1_w_gate, l1_w_up, l1_w_down, mem_2, norm_mix_g_2, w_in_2, b_gate_2, b_if_2,
    conv_w_2, conv_b_2, mh_norm_g_2, sgu_norm_g_2, w_s_2, b_s_2, w_out_2, norm_x_g_2,
    norm_mem_g_2, w_xq_2, w_xkv_2, w_xo_2, norm_moe_g_2, w_rg_2, b_rg_2, w_re_2, b_re_2, w1_2,
    w3_2, w2_2, norm_f_g_2,
):
    x = first_block(
        x, positions, l0_attn_norm, l0_w_in, l0_mla_q_a_norm, l0_mla_w_q_up, l0_mla_kv_a_norm,
        l0_mla_w_kv_up, l0_mla_q_norm, l0_mla_k_norm, l0_w_o, l0_ffn_norm, l0_w_gate, l0_w_up,
        l0_w_down, l1_attn_norm, l1_w_in, l1_fox_f_bias, l1_fox_q_norm, l1_fox_k_norm, l1_w_o,
        l1_ffn_norm, l1_w_gate, l1_w_up, l1_w_down,
    )
    return second_block(
        x, mem_2, norm_mix_g_2, w_in_2, b_gate_2, b_if_2, conv_w_2, conv_b_2, mh_norm_g_2,
        sgu_norm_g_2, w_s_2, b_s_2, w_out_2, norm_x_g_2, norm_mem_g_2, w_xq_2, w_xkv_2, w_xo_2,
        norm_moe_g_2, w_rg_2, b_rg_2, w_re_2, b_re_2, w1_2, w3_2, w2_2, norm_f_g_2,
    )


_drawn_inputs = setup_inputs


def setup_inputs(seed=0):
    import zlib

    import numpy as np

    out = dict(_drawn_inputs(seed))
    spreads = {}
    factors = {'l0_mla_q_a_norm': 3.482,
     'l0_mla_q_norm': 2.677,
     'l0_mla_k_norm': 2.927,
     'norm_mix_g_2': 4.083,
     'b_gate_2': 8.0,
     'conv_b_2': 35.214,
     'mh_norm_g_2': 8.0,
     'sgu_norm_g_2': 5.923,
     'b_s_2': 5.2,
     'norm_x_g_2': 8.0,
     'norm_mem_g_2': 8.0,
     'norm_moe_g_2': 3.078,
     'b_rg_2': 29.988,
     'b_re_2': 19.912,
     'norm_f_g_2': 7.947}
    for name, (base, spread) in spreads.items():
        noise = np.random.default_rng([zlib.crc32(name.encode()), seed]).standard_normal(out[name].shape)
        drawn = base * np.exp(spread * noise) if base else spread * noise
        out[name] = __import__('jax').numpy.asarray(drawn.astype(out[name].dtype))
    for name, factor in factors.items():
        out[name] = (out[name] * factor).astype(out[name].dtype)
    return out
```

```python
from contextlib import ExitStack

import numpy as np

import concourse.bass as bass
from concourse import mybir

F32 = mybir.dt.float32
I32 = mybir.dt.int32
U32 = mybir.dt.uint32
ALU = mybir.AluOpType
ACT = mybir.ActivationFunctionType
AX = mybir.AxisListType.X

P = 128
S = 512
NT = S // P
D = 1024
KD = D // P
EPS = 1e-6
NEG = -1e30
BANK = 512
NBANK = 8
SLOT = 4096
NS = 4
NSM = 6
QR, KVR, RO, NOPE, MV = 256, 128, 32, 64, 64
QK = NOPE + RO
MH = 8
HALF = RO // 2
C0 = QR + KVR + RO
SBW = 512
FF = 2816
FT = FF // P
FC = FF // 256
FH = 16
LH = 4
DH = 256
NM = 256
MT = NM // P
G8 = 8
NE = 32
NGR = 4
EPG = NE // NGR
EF = 512
NOVER = 7

START, END = 1, 7


class Chain:

    def __init__(self, eng, sem):
        self.eng, self.sem, self.n = eng, sem, 0

    def mark(self, ins):
        self.n += 1
        ins.then_inc(self.sem, 1)

    def wait(self):
        self.eng.wait_ge(self.sem, self.n)

    def __call__(self, ins):
        self.mark(ins)
        self.wait()


def two_pi():
    c1 = 201.0 / 32.0
    c2 = float(np.round((2.0 * np.pi - c1) * 2.0**20) / 2.0**20)
    return c1, c2, float(np.float32(2.0 * np.pi - c1 - c2))


def bass_two_blocks_kernel(nc, I, out):
    def on(n):
        return START <= n <= END

    ctx = ExitStack()

    def sb(name, shape, dt=F32):
        return ctx.enter_context(nc.sbuf_tensor(name, shape, dt))

    def sem(name):
        return ctx.enter_context(nc.semaphore(name))

    with ctx:
        x = sb("x", [P, NT, D])
        actT = sb("actT", [P, KD, S])
        orow = actT[:, :, :].rearrange("p (t a) s -> p t (a s)", t=NT)
        ident = sb("ident", [P, P])
        tri = sb("tri", [P, P])
        ones = sb("ones", [P, P])
        maskz = sb("maskz", [P, S])
        rank1 = sb("rank1", [P, P])
        gains = sb("gains", [P, 64])
        cols2 = sb("cols2", [P, 96])
        nhalf = sb("nhalf", [P, 1])
        desc = sb("desc", [P, NE])
        eidx = sb("eidx", [P, NE])
        ss = sb("ss", [P, 8])
        rs = sb("rs", [P, 4])
        mx = sb("mx", [P, 4])
        bi = sb("bi", [P, 4])
        rinv = sb("rinv", [P, 4])
        em = sb("em", [P, 4])
        ffb = sb("ffb", [P, FH])
        bif = sb("bif", [P, 8])
        rbias = sb("rbias", [P, NGR + NE])
        qg = sb("qg", [P, 2, QK])
        ropec = sb("ropec", [P, NT, HALF])
        ropes = sb("ropes", [P, NT, HALF])
        posi = sb("posi", [P, NT], I32)
        CS = sb("CS", [P, NT, FH])
        FG = sb("FG", [P, 2, NT, FH])
        st = sb("st", [P, 128])
        ft = sb("ft", [1, 16], I32)
        free = (nc.sbuf_bytes_remaining // 4 - 64) // 64 * 64
        big = sb("big", [P, free])
        ring = [big[:, i * SLOT:(i + 1) * SLOT] for i in range(NSM)]

        def area(base, off, *shape):
            n = int(np.prod(shape))
            assert base + off + n <= free, (off, n, free - base)
            v = big[:, base + off:base + off + n]
            if len(shape) == 2:
                v = v.rearrange("p (a b) -> p a b", b=shape[1])
            if len(shape) == 3:
                v = v.rearrange("p (a b c) -> p a b c", b=shape[1], c=shape[2])
            return v

        def work(off, *shape):
            return area(NS * SLOT, off, *shape)

        def moe(off, *shape):
            return area(NSM * SLOT, off, *shape)

        ps = ctx.enter_context(nc.psum_tensor("ps", [P, NBANK, BANK], F32))
        G_A0, G_F0, G_A1, G_F1, G_MIX, G_X, G_MEM, G_MOE = range(8)
        norm_names = ["l0_attn_norm", "l0_ffn_norm", "l1_attn_norm", "l1_ffn_norm",
                      "norm_mix_g_2", "norm_x_g_2", "norm_mem_g_2", "norm_moe_g_2"]
        CW, CB, QA, BS, FQ, FK = 0, 64, 80, 83, 91, 92

        w_full = [sem(f"w_full{i}") for i in range(NS)]
        w_moe = [sem(f"w_moe{i}") for i in range(NSM)]
        mm = sem("mm")
        tr = sem("tr")
        ea = sem("ea")
        ev = sem("ev")
        mida = sem("mida")
        midv = sem("midv")
        ssd = sem("ssd")
        rsd = sem("rsd")
        xsd = sem("xsd")
        phase = sem("phase")
        vch, ach, pch = sem("vch"), sem("ach"), sem("pch")
        cst = sem("cst")
        xin = sem("xin")
        s_sc, s_mx, s_ex = sem("s_sc"), sem("s_mx"), sem("s_ex")
        s_pt, s_pe = sem("s_pt"), sem("s_pe")
        s_o, s_on = sem("s_o"), sem("s_on")
        s_pr, s_pre = sem("s_pr"), sem("s_pre")
        s_t1, s_sp, s_m1, s_w, s_m2 = sem("s_t1"), sem("s_sp"), sem("s_m1"), sem("s_w"), sem("s_m2")
        out_s = sem("out_s")
        m_oh, m_gx, m_gxa, m_gxv = sem("m_oh"), sem("m_gx"), sem("m_gxa"), sem("m_gxv")
        m_up, m_si, m_hb, m_tr, m_hT = sem("m_up"), sem("m_si"), sem("m_hb"), sem("m_tr"), sem("m_hT")
        m_dn, m_oa, m_ov, m_st = sem("m_dn"), sem("m_oa"), sem("m_ov"), sem("m_st")
        g_in = [sem(f"g_in{j}") for j in range(4)]
        g_use = sem("g_use")

        if on(7):
            obuf = nc.dram_tensor("expert_rows", [(NE + NOVER) * P, D], F32, kind="Internal").ap()

        counts = {}

        def use(s, n):
            b = counts.get(s.name, 0)
            counts[s.name] = b + n
            return b

        stages = []

        def stage(pe=None, act=None, dve=None, po=None):
            stages.append((pe, act, dve, po))

        chunks = []
        loads_at = [0] * NS

        def chunk(loads, kt, n, runs):
            c = len(chunks)
            slot = c % NS
            loads_at[slot] += len(loads)
            b = use(mm, runs)
            chunks.append((loads, kt, n, b + runs))
            v = ring[slot][:, :kt * n].rearrange("p (k c) -> p k c", c=n)
            return v, (w_full[slot], 16 * loads_at[slot]), b

        def kpc(w):
            return w.rearrange("(k p) c -> p k c", p=P)

        class Groups:

            def __init__(self, n, who):
                self.who = [who[g % len(who)] for g in range(n)]
                sems = {"A": ea, "V": ev, "C": midv}
                base = {k: use(s, self.who.count(k)) for k, s in sems.items()}
                base["X"], sems["X"] = 0, None
                self.freed = []
                for k in self.who:
                    base[k] += 1
                    self.freed.append((sems[k], base[k]))

            def bank(self, g):
                return g % NBANK

            def wait_free(self, eng, g):
                if g >= NBANK:
                    eng.wait_ge(*self.freed[g - NBANK])

            def wait_taken(self, eng, g):
                eng.wait_ge(*self.freed[g])

        xs = work(0, 2, D)
        junk = work(2048, D)

        def norm_stage(src, dst, gain, tiles):
            ss0, rs0, xs0, tr0 = use(ssd, tiles), use(rsd, tiles), use(xsd, tiles), use(tr, 2 * tiles)
            gr = Groups(2 * tiles, "V")

            def act(act, ch):
                for t in range(tiles):
                    if t:
                        act.wait_ge(ssd, ss0 + t)
                    act.activation(junk, src[:, t, :], ACT.Square, accum_out=ss[:, t:t + 1]).then_inc(ssd, 1)
                for t in range(tiles):
                    act.wait_ge(rsd, rs0 + t + 1)
                    if t >= 2:
                        act.wait_ge(tr, tr0 + 2 * (t - 1))
                    act.mul(xs[:, t % 2, :], src[:, t, :], ss[:, t:t + 1]).then_inc(xsd, 1)

            def po(po, ch):
                for t in range(tiles):
                    po.wait_ge(ssd, ss0 + t + 1)
                    v = ss[:, t:t + 1]
                    ch(po.tensor_scalar(v, v, 1.0 / D, EPS, ALU.mult, ALU.add))
                    po.tensor_tensor(v, v, nhalf[:, :], ALU.pow).then_inc(rsd, 1)

            def pe(pe, ch):
                for t in range(tiles):
                    pe.wait_ge(xsd, xs0 + t + 1)
                    for h in range(2):
                        g = 2 * t + h
                        gr.wait_free(pe, g)
                        for j in range(4):
                            m = pe.transpose(ps[:, gr.bank(g), j * P:j * P + P],
                                             xs[:, t % 2, (4 * h + j) * P:(4 * h + j + 1) * P], ident[:, :])
                        m.then_inc(tr, 1)

            def dve(dve, ch):
                for g in range(2 * tiles):
                    t, h = divmod(g, 2)
                    dve.wait_ge(tr, tr0 + g + 1)
                    dve.tensor_tensor(dst[:, 4 * h:4 * h + 4, t * P:t * P + P],
                                      ps[:, gr.bank(g), :].rearrange("p (k s) -> p k s", k=4),
                                      gains[:, 8 * gain + 4 * h:8 * gain + 4 * h + 4].rearrange(
                                          "p (k o) -> p k o", o=1).to_broadcast([P, 4, P]),
                                      ALU.mult).then_inc(ev, 1)
            stage(pe, act, dve, po)

        def pe_run(pe, gr, g, pairs, dst, s, lead=()):
            gr.wait_free(pe, g)
            for k, (lhs, rhs) in enumerate(pairs):
                m = pe.matmul(dst, lhs, rhs, start=(k == 0), stop=(k == len(pairs) - 1))
            m.then_inc(s, 1)

        class Rows:

            def __init__(self, gr, g0, lhs, tiles, loads, n, kt=KD, parts=1):
                self.gr, self.g0, self.lhs, self.tiles, self.n, self.kt, self.parts = gr, g0, lhs, tiles, n, kt, parts
                self.W, self.full, self.m0 = chunk(loads, kt, n * parts, tiles * parts)

            def pe(self, pe):
                pe.wait_ge(*self.full)
                for r in range(self.tiles * self.parts):
                    t, h = divmod(r, self.parts)
                    pe_run(pe, self.gr, self.g0 + r,
                           [(self.lhs[:, k, t * P:t * P + P], self.W[:, k, h * self.n:(h + 1) * self.n])
                            for k in range(self.kt)], ps[:, self.gr.bank(self.g0 + r), 0:self.n], mm)

            def ready(self, eng, r):
                eng.wait_ge(mm, self.m0 + r + 1)

            def src(self, r):
                return ps[:, self.gr.bank(self.g0 + r), 0:self.n]

        class Cols(Rows):

            def __init__(self, gr, g0, rhs, n, loads):
                self.gr, self.g0, self.rhs, self.n, self.tiles = gr, g0, rhs, n, 4
                self.W, self.full, self.m0 = chunk(loads, KD, 512, 4)

            def pe(self, pe):
                pe.wait_ge(*self.full)
                for j in range(4):
                    pe_run(pe, self.gr, self.g0 + j,
                           [(self.W[:, k, j * P:j * P + P], self.rhs[:, k, :]) for k in range(KD)],
                           ps[:, self.gr.bank(self.g0 + j), 0:self.n], mm)

        def take_act(act, src, dst, scale=1.0):
            act.activation(dst, src, ACT.Copy, scale=scale).then_inc(ea, 1)

        def take_dve(dve, src, dst):
            dve.tensor_copy(dst, src).then_inc(ev, 1)

        def plain_stage(jobs, gr):
            def pe(pe, ch):
                for job, _, _ in jobs:
                    job.pe(pe)

            def act(act, ch):
                for job, dst, scale in jobs:
                    for r in range(job.tiles):
                        if gr.who[job.g0 + r] == "A":
                            job.ready(act, r)
                            take_act(act, job.src(r), dst(r), scale)

            def dve(dve, ch):
                for job, dst, scale in jobs:
                    for r in range(job.tiles):
                        if gr.who[job.g0 + r] == "V":
                            job.ready(dve, r)
                            dve.tensor_scalar(dst(r), job.src(r), scale, None, ALU.mult).then_inc(ev, 1)
            stage(pe, act, dve)

        def out_stage(src, oT, wts):
            gt = Groups(8, "AV")
            tr0 = use(tr, 8)

            def pe(pe, ch):
                for g in range(8):
                    t, h = divmod(g, 2)
                    for j in range(4):
                        m = pe.transpose(ps[:, g, j * P:j * P + P],
                                         src[:, t, (4 * h + j) * P:(4 * h + j + 1) * P], ident[:, :])
                    m.then_inc(tr, 1)

            def moves(eng, who):
                for g in range(8):
                    if gt.who[g] == who:
                        t, h = divmod(g, 2)
                        eng.wait_ge(tr, tr0 + g + 1)
                        d = oT[:, 4 * h:4 * h + 4, t * P:t * P + P]
                        s = ps[:, g, :].rearrange("p (k s) -> p k s", k=4)
                        (take_act if who == "A" else take_dve)(eng, s, d)
            stage(pe, lambda act, ch: moves(act, "A"), lambda dve, ch: moves(dve, "V"))
            gr = Groups(8, "V")
            jobs = [Rows(gr, 4 * c, oT, NT, [(kpc(wts[:, c * 512:c * 512 + 512]), 0)], 512) for c in range(2)]

            def pe2(pe, ch):
                for job in jobs:
                    job.pe(pe)

            def dve2(dve, ch):
                for c, job in enumerate(jobs):
                    for t in range(NT):
                        job.ready(dve, t)
                        xx = x[:, t, c * 512:c * 512 + 512]
                        dve.tensor_tensor(xx, xx, job.src(t), ALU.add).then_inc(ev, 1)
            stage(pe2, None, dve2)

        def ffn_stage(wg, wu, wd):
            guT = work(0, FT, S)
            sil = work(FT * S, 4, 512)
            gr = Groups(2 * FT, "V")
            si0 = use(mida, FT)
            ev0 = gr.freed[0][1] - 1
            jobs = [chunk([(kpc(wg[:, 256 * c:256 * c + 256]), 0), (kpc(wu[:, 256 * c:256 * c + 256]), 256)], KD, 512, 4)
                    for c in range(FC)]
            m0 = jobs[0][2]
            g2 = Groups(8, "V")
            parts = ((0, 8), (8, 16), (16, 22))
            down = [[chunk([(kpc(wd[k0 * P:k1 * P, h * 512:h * 512 + 512]), 0)], k1 - k0, 512, NT) for k0, k1 in parts]
                    for h in range(2)]

            def pe(pe, ch):
                for c, (W, full, _) in enumerate(jobs):
                    pe.wait_ge(*full)
                    for q in range(4):
                        f, o = 2 * c + q // 2, 256 * (q % 2) + P * (q // 2)
                        pe_run(pe, gr, 4 * c + q, [(W[:, k, o:o + P], actT[:, k, :]) for k in range(KD)],
                               ps[:, gr.bank(4 * c + q), :], mm)
                gr.wait_taken(pe, 2 * FT - 1)
                for h in range(2):
                    for (k0, k1), (W, full, _) in zip(parts, down[h]):
                        pe.wait_ge(*full)
                        for t in range(NT):
                            for k in range(k0, k1):
                                m = pe.matmul(ps[:, 4 * h + t, :], guT[:, k, t * P:t * P + P], W[:, k - k0, :],
                                              start=(k == 0), stop=(k == FT - 1))
                            m.then_inc(mm, 1)

            def act(act, ch):
                for f in range(FT):
                    act.wait_ge(mm, m0 + 2 * f + 1)
                    if f >= 4:
                        act.wait_ge(ev, ev0 + 2 * (f - 3))
                    act.activation(sil[:, f % 4, :], ps[:, 2 * f % NBANK, :], ACT.Silu).then_inc(mida, 1)

            def dve(dve, ch):
                for f in range(FT):
                    dve.wait_ge(mm, m0 + 2 * f + 2)
                    dve.wait_ge(mida, si0 + f + 1)
                    dve.tensor_tensor(guT[:, f, :], sil[:, f % 4, :], ps[:, (2 * f + 1) % NBANK, :],
                                      ALU.mult).then_inc(ev, 2)
                for h in range(2):
                    for t in range(NT):
                        dve.wait_ge(mm, down[h][2][2] + t + 1)
                        xx = x[:, t, h * 512:h * 512 + 512]
                        dve.tensor_tensor(xx, xx, ps[:, 4 * h + t, :], ALU.add).then_inc(ev, 1)
            stage(pe, act, dve)

        Pb = work(0, 4, 512)
        PT = work(2048, 2, 512)
        A0 = 3072

        def causal(v):
            return (v % NT + 1) * P

        def attention(units, length, scores, values, dv, dst, scale, preps=(), kind="soft", fox=False):
            sc0, mx0, ex0, pt0, pe0, o0, on0 = (use(s, units) for s in (s_sc, s_mx, s_ex, s_pt, s_pe, s_o, s_on))
            npr = sum(len(p[2]) for p in preps)
            pr0, pre0 = use(s_pr, npr), use(s_pre, npr)
            t10 = use(s_t1, units) if kind == "mlstm" else 0
            t2 = use(mida, units) if kind == "mlstm" else 0
            order, at = [], {}
            for p in preps:
                order.append((p, sum(len(q[2]) for q, _ in order)))
                at.setdefault(p[0], []).append(order[-1])

            def pe(pe, ch):
                def prep(p, n0):
                    for j, (blocks, _, _) in enumerate(p[2]):
                        if n0 >= 2:
                            pe.wait_ge(s_pre, pre0 + n0 - 1 + j)
                        for t, b in enumerate(blocks):
                            m = pe.transpose(ps[0:b.shape[1], 6 + j, t * P:t * P + P], b, ident[:, :])
                        m.then_inc(s_pr, 1)
                for v in range(units + 2):
                    for p in at.get(v, ()):
                        prep(*p)
                    if v < units:
                        if v >= 2:
                            pe.wait_ge(s_ex, ex0 + v - 1)
                        scores(pe, v, v % 2, pre0).then_inc(s_sc, 1)
                    if 1 <= v <= units:
                        u = v - 1
                        pe.wait_ge(s_ex, ex0 + u + 1)
                        if u >= 2:
                            pe.wait_ge(s_pe, pe0 + u - 1)
                        for j in range(length(u) // P):
                            m = pe.transpose(ps[:, 2 + u % 2, j * P:j * P + P],
                                             Pb[:, u % 4, j * P:j * P + P], ident[:, :])
                        m.then_inc(s_pt, 1)
                    if v >= 2:
                        u = v - 2
                        pe.wait_ge(s_pe, pe0 + u + 1)
                        if u >= 2:
                            pe.wait_ge(s_on, on0 + u - 1)
                        nb = length(u) // P
                        for j in range(nb):
                            m = pe.matmul(ps[:, 4 + u % 2, 0:dv], PT[:, u % 2, j * P:j * P + P], values(u, j),
                                          start=(j == 0), stop=(j == nb - 1))
                        m.then_inc(s_o, 1)

            def act(act, ch):
                def prep(p, n0):
                    for j, (_, d, gain) in enumerate(p[2]):
                        act.wait_ge(s_pr, pr0 + n0 + j + 1)
                        if p[1]:
                            act.wait_ge(s_sc, sc0 + p[1])
                        act.activation(d, ps[0:d.shape[0], 6 + j, :], ACT.Copy, scale=gain).then_inc(s_pre, 1)
                for v in range(units + 1):
                    for p in at.get(v, ()):
                        prep(*p)
                    if v < units:
                        L = length(v)
                        act.wait_ge(s_mx, mx0 + v + 1)
                        b = bi[:, v % 4:v % 4 + 1]
                        if kind == "soft":
                            if v >= 4:
                                act.wait_ge(s_pt, pt0 + v - 3)
                                act.wait_ge(s_on, on0 + v - 3)
                            act.activation(Pb[:, v % 4, 0:L], ps[:, v % 2, 0:L], ACT.Exp, bias=b, scale=scale,
                                           accum_out=rs[:, v % 4:v % 4 + 1]).then_inc(s_ex, 1)
                        else:
                            if v >= 2:
                                act.wait_ge(s_ex, ex0 + v - 1)
                            act.activation(E[:, v % 2, 0:L], ps[:, 6 + v % 2, 0:L], ACT.Exp, bias=b).then_inc(s_t1, 1)
                            if v >= 4:
                                act.wait_ge(s_on, on0 + v - 3)
                            h, i = divmod(v, NT)
                            act.activation(em[:, v % 4:v % 4 + 1], b, ACT.Exp, bias=CS[:, i, h:h + 1]).then_inc(mida, 1)
                    if v >= 1:
                        u = v - 1
                        act.wait_ge(s_pt, pt0 + u + 1)
                        if u >= 2:
                            act.wait_ge(s_o, o0 + u - 1)
                        L = length(u)
                        act.activation(PT[:, u % 2, 0:L], ps[:, 2 + u % 2, 0:L], ACT.Copy).then_inc(s_pe, 1)

            def dve(dve, ch):
                for v in range(units + 2):
                    if v < units:
                        L = length(v)
                        h, i = divmod(v, NT)
                        dve.wait_ge(s_sc, sc0 + v + 1)
                        m1 = mx[:, v % 4:v % 4 + 1]
                        bank = ps[:, (v % 2) + (6 if kind == "mlstm" else 0), 0:L]
                        if kind == "mlstm" or length is causal:
                            ch(dve.tensor_tensor_reduce(bank, bank, maskz[:, S - L:S], 1.0, -3e38,
                                                        ALU.add, ALU.max, m1))
                        else:
                            ch(dve.tensor_reduce(m1, bank, AX, ALU.max))
                        if v >= 4 and kind != "mlstm":
                            dve.wait_ge(s_ex, ex0 + v - 3)
                        if v >= 4 and kind == "mlstm":
                            dve.wait_ge(mida, t2 + v - 3)
                        b = bi[:, v % 4:v % 4 + 1]
                        if kind == "mlstm":
                            dve.tensor_scalar(b, m1, 0.0, -1.0, ALU.max, ALU.mult).then_inc(s_mx, 1)
                        elif fox:
                            ch(dve.tensor_scalar(m1, m1, scale, CS[:, i, h:h + 1], ALU.mult, ALU.subtract))
                            dve.tensor_scalar(b, m1, -1.0, CS[:, i, h:h + 1], ALU.mult, ALU.subtract).then_inc(s_mx, 1)
                        else:
                            dve.tensor_scalar(b, m1, -scale, None, ALU.mult).then_inc(s_mx, 1)
                    if kind == "mlstm" and 1 <= v <= units:
                        u = v - 1
                        L = length(u)
                        dve.wait_ge(s_t1, t10 + u + 1)
                        if u >= 4:
                            dve.wait_ge(s_pt, pt0 + u - 3)
                        dve.tensor_tensor_reduce(Pb[:, u % 4, 0:L], ps[:, u % 2, 0:L], E[:, u % 2, 0:L],
                                                 DH ** -0.5, 0.0, ALU.mult, ALU.add,
                                                 rs[:, u % 4:u % 4 + 1]).then_inc(s_ex, 1)
                    if v >= 2:
                        u = v - 2
                        h, i = divmod(u, NT)
                        r, q = rinv[:, u % 4:u % 4 + 1], rs[:, u % 4:u % 4 + 1]
                        if kind == "mlstm":
                            dve.wait_ge(s_ex, ex0 + u + 1)
                            dve.wait_ge(mida, t2 + u + 1)
                            ch(dve.scalar_tensor_tensor(out=q, in0=q, scalar=-1.0, in1=q, op0=ALU.mult, op1=ALU.max))
                            ch(dve.tensor_scalar(q, q, em[:, u % 4:u % 4 + 1], None, ALU.max))
                        else:
                            dve.wait_ge(s_ex, ex0 + u + 1)
                        ch(dve.reciprocal(r, q))
                        dve.wait_ge(s_o, o0 + u + 1)
                        dve.tensor_scalar(dst(h, i), ps[:, 4 + u % 2, 0:dv], r, None, ALU.mult).then_inc(s_on, 1)
            stage(pe, act, dve)

        crow = work(0, 256)
        freq = work(256, HALF)
        ang = work(320, NT, HALF)
        angk = work(384, NT, HALF)
        posf = work(448, NT)
        crows = []
        for k, name in enumerate(norm_names):
            v = I[name] if len(I[name].shape) == 1 else I[name][0]
            crows.append((crow[8 * k:8 * k + 8, 0:P], v.rearrange("(k p) -> k p", p=P)))
        crows += [(crow[0:64, P:2 * P], I["conv_w_2"][0].rearrange("w (k p) -> (w k) p", p=P)),
                  (crow[CB:CB + 16, P:2 * P], I["conv_b_2"][0].rearrange("(k p) -> k p", p=P)),
                  (crow[QA:QA + 2, P:2 * P], I["l0_mla_q_a_norm"].rearrange("(k p) -> k p", p=P)),
                  (crow[QA + 2:QA + 3, P:2 * P], I["l0_mla_kv_a_norm"].rearrange("(k p) -> k p", p=P)),
                  (crow[BS:BS + 8, P:2 * P], I["b_s_2"][0])]
        for r, name in ((FQ, "l1_fox_q_norm"), (FK, "l1_fox_k_norm")):
            for h in range(2):
                crows.append((crow[r:r + 1, P + 64 * h:P + 64 * h + 64], I[name].rearrange("(k p) -> k p", p=64)))

        def every(v):
            return v.rearrange("(a n) -> a n", a=1).to_broadcast([P, v.shape[0]])

        crows += [(ffb[:, :], every(I["l1_fox_f_bias"])), (qg[:, 0, :], every(I["l0_mla_q_norm"])),
                  (qg[:, 1, :], every(I["l0_mla_k_norm"])), (bif[:, :], every(I["b_if_2"][0])),
                  (rbias[:, 0:NGR], every(I["b_rg_2"][0])), (rbias[:, NGR:], every(I["b_re_2"][0]))]

        def consts_po(po, ch):
            for m, val in ((ident, 0.0), (tri, 1.0), (ones, 1.0), (maskz, 0.0), (nhalf, -0.5)):
                ch.mark(po.memset(m[:, :], val))
            for j in range(HALF):
                ch.mark(po.memset(freq[:, j:j + 1], float(np.float32(10000.0) ** (-np.float32(j) / np.float32(HALF)))))
            ch.wait()
            ch.mark(po.affine_select(out=ident[:, :], in_=ident[:, :], compare_op=ALU.not_equal, fill=1.0,
                                     base=0, pattern=[[-1, P]], channel_multiplier=1))
            ch.mark(po.affine_select(out=tri[:, :], in_=tri[:, :], compare_op=ALU.is_ge, fill=0.0,
                                     base=0, pattern=[[1, P]], channel_multiplier=-1))
            ch.mark(po.affine_select(out=maskz[:, S - P:S], in_=maskz[:, S - P:S], compare_op=ALU.is_ge, fill=NEG,
                                     base=0, pattern=[[-1, P]], channel_multiplier=1))
            for v, step, n, b in ((rank1, 1, P, 1), (desc, -1, NE, NE), (eidx, 1, NE, 0)):
                ch.mark(po.iota(v[:, :], pattern=[[step, n]], base=b, channel_multiplier=0,
                                allow_small_or_imprecise_dtypes=True))
            ch.wait()
        stage(None, None, None, consts_po)

        tr_c, mv_c = use(tr, 1), use(midv, 1)

        def cols_pe(pe, ch):
            pe.wait_ge(cst, 16 * (len(crows) + 1))
            pe.transpose(ps[0:P, 0, 0:64], crow[0:64, 0:P], ident[0:64, 0:64])
            pe.transpose(ps[0:P, 1, 0:93], crow[0:93, P:2 * P], ident[0:93, 0:93]).then_inc(tr, 1)

        def cols_act(act, ch):
            act.wait_ge(midv, mv_c + 1)
            ch.mark(act.activation(ropes[:, :, :], ropes[:, :, :], ACT.Sin))
            ch(act.activation(ropec[:, :, :], ropec[:, :, :], ACT.Sin))

        def cols_dve(dve, ch):
            dve.wait_ge(cst, 16 * (len(crows) + 1))
            ch(dve.tensor_copy(posf, posi[:, :]))
            c1, c2, c3 = two_pi()
            ch(dve.tensor_tensor(ang, posf.rearrange("p (t o) -> p t o", o=1).to_broadcast([P, NT, HALF]),
                                 freq.rearrange("p (o h) -> p o h", o=1).to_broadcast([P, NT, HALF]), ALU.mult))
            magic = 1.5 * 2.0 ** 23
            ch(dve.tensor_scalar(angk, ang, float(np.float32(1 / (2 * np.pi))), magic, ALU.mult, ALU.add))
            ch(dve.tensor_scalar(angk, angk, magic, None, ALU.subtract))
            for c in (c1, c2, c3):
                ch(dve.scalar_tensor_tensor(out=ang, in0=angk, scalar=-c, in1=ang, op0=ALU.mult, op1=ALU.add))
            lim = 3.1415925
            ch(dve.tensor_scalar(ropes[:, :, :], ang, lim, -lim, ALU.min, ALU.max))
            ch(dve.scalar_tensor_tensor(out=ropec[:, :, :], in0=ropes[:, :, :], scalar=-1.0, in1=ropes[:, :, :],
                                        op0=ALU.mult, op1=ALU.max))
            dve.tensor_scalar(ropec[:, :, :], ropec[:, :, :], -1.0, float(np.float32(np.pi / 2)),
                              ALU.mult, ALU.add).then_inc(midv, 1)
            dve.wait_ge(tr, tr_c + 1)
            ch.mark(dve.tensor_copy(gains[:, :], ps[:, 0, 0:64]))
            ch.mark(dve.tensor_copy(cols2[:, 0:93], ps[:, 1, 0:93]))
            dve.wait_ge(xin, 16)
            ch.wait()
        stage(cols_pe, cols_act, cols_dve)

        def softplus_stages(n, cs_cols, extra=None):
            f, a = FG[:, 0, :, 0:n], FG[:, 1, :, 0:n]
            v0, a0, t0 = use(midv, 2), use(mida, 1), use(tr, 2)

            def dve(dve, ch):
                dve.scalar_tensor_tensor(out=a, in0=f, scalar=-1.0, in1=f, op0=ALU.mult, op1=ALU.max).then_inc(midv, 1)
                ch(dve.tensor_scalar(f, f, -1.0, 0.0, ALU.mult, ALU.max))
                dve.wait_ge(mida, a0 + 1)
                dve.tensor_tensor(f, f, a, ALU.add).then_inc(midv, 1)
                dve.wait_ge(tr, t0 + 1)
                ch(dve.tensor_copy(CS[:, :, 0:n], ps[:, 0, 0:NT * n].rearrange("p (t a) -> p t a", t=NT)))
                if extra:
                    extra(dve, ch)

            def act(act, ch):
                act.wait_ge(midv, v0 + 1)
                ch(act.activation(a, a, ACT.Exp, scale=-1.0))
                act.activation(a, a, ACT.Ln, bias=1.0).then_inc(mida, 1)

            def pe(pe, ch):
                pe.wait_ge(midv, v0 + 2)
                for t in range(NT):
                    for j in range(t + 1):
                        m = pe.matmul(ps[:, 0, t * n:t * n + n], (tri if j == t else ones)[:, :], FG[:, 0, j, 0:n],
                                      start=(j == 0), stop=(j == t))
                m.then_inc(tr, 1)
            stage(pe, act, dve)
            src, dst, scale = cs_cols

            def pe2(pe, ch):
                for t in range(NT):
                    m = pe.transpose(ps[0:n, 1, t * P:t * P + P], src[:, t, 0:n], ident[:, :])
                m.then_inc(tr, 1)

            def act2(act, ch):
                act.wait_ge(tr, t0 + 2)
                ch(act.activation(dst, ps[0:n, 1, :], ACT.Copy, scale=scale))
            stage(pe2, act2)

        if on(1):
            cq0 = work(A0, NT, C0)
            sbq = work(A0 + 1664, NT, S)
            sbk = work(A0 + 3712, NT, S)
            sbv = work(A0 + 5760, NT, SBW)
            Qr = work(A0 + 7808, NT, MH * QK)
            Kr = work(A0 + 10880, NT, MH * QK)
            Vr = work(A0 + 13952, NT, MH * MV)
            QT = work(A0 + 16000, 2, 512)
            KT = work(A0 + 17024, 2, 512)
            cqT = work(A0 + 7808, 3, S)
            sqq = work(0, NT * MH, QK)
            sqk = work(A0 + 16000 + 3072, NT * MH, HALF)
            norm_stage(x, actT, G_A0, NT)
            gr = Groups(16, "AV")
            w = I["l0_w_in"]
            plain_stage([
                (Rows(gr, 0, actT, NT, [(kpc(w[:, 0:C0]), 0)], C0), lambda t: cq0[:, t, :], 1.0),
                (Cols(gr, 4, actT, S, [(kpc(w[:, C0:C0 + SBW]), 0)]), lambda t: sbq[:, t, :], 64 ** -0.5),
                (Cols(gr, 8, actT, S, [(kpc(w[:, C0 + SBW:C0 + 2 * SBW]), 0)]), lambda t: sbk[:, t, :], 1.0),
                (Rows(gr, 12, actT, NT, [(kpc(w[:, C0 + 2 * SBW:C0 + 3 * SBW]), 0)], SBW),
                 lambda t: sbv[:, t, :], 1.0)], gr)

            ss0, rs0, xs0, tr0 = use(ssd, 1), use(rsd, 1), use(xsd, 4), use(tr, 4)
            gr1 = Groups(4, "V")

            def rank_act(act, ch):
                for t in range(NT):
                    ch(act.activation(junk[:, 0:QR], cq0[:, t, 0:QR], ACT.Square, accum_out=ss[:, t:t + 1]))
                    last = act.activation(junk[:, QR:QR + KVR], cq0[:, t, QR:QR + KVR], ACT.Square,
                                          accum_out=ss[:, 4 + t:5 + t])
                    if t < NT - 1:
                        ch(last)
                last.then_inc(ssd, 1)

            def rank_po(po, ch):
                po.wait_ge(ssd, ss0 + 1)
                ch.mark(po.tensor_scalar(ss[:, 0:4], ss[:, 0:4], 1.0 / QR, EPS, ALU.mult, ALU.add))
                ch(po.tensor_scalar(ss[:, 4:8], ss[:, 4:8], 1.0 / KVR, EPS, ALU.mult, ALU.add))
                po.tensor_tensor(ss[:, :], ss[:, :], nhalf[:, :].to_broadcast([P, 8]), ALU.pow).then_inc(rsd, 1)

            def rank_dve(dve, ch):
                dve.wait_ge(rsd, rs0 + 1)
                for t in range(NT):
                    ch(dve.tensor_scalar(cq0[:, t, 0:QR], cq0[:, t, 0:QR], ss[:, t:t + 1], None, ALU.mult))
                    dve.tensor_scalar(cq0[:, t, QR:QR + KVR], cq0[:, t, QR:QR + KVR], ss[:, 4 + t:5 + t], None,
                                      ALU.mult).then_inc(xsd, 1)
                for t in range(NT):
                    dve.wait_ge(tr, tr0 + t + 1)
                    dve.tensor_tensor(cqT[:, :, t * P:t * P + P],
                                      ps[:, t, 0:3 * P].rearrange("p (k s) -> p k s", k=3),
                                      cols2[:, QA:QA + 3].rearrange("p (k o) -> p k o", o=1).to_broadcast([P, 3, P]),
                                      ALU.mult).then_inc(ev, 1)

            def rank_pe(pe, ch):
                for t in range(NT):
                    pe.wait_ge(xsd, xs0 + t + 1)
                    for j in range(3):
                        m = pe.transpose(ps[:, t, j * P:j * P + P], cq0[:, t, j * P:j * P + P], ident[:, :])
                    m.then_inc(tr, 1)
            stage(rank_pe, rank_act, rank_dve, rank_po)

            gr2 = Groups(16, "AV")
            up_q = Rows(gr2, 0, cqT, NT, [(kpc(I["l0_mla_w_q_up"]), 0)], 384, 2, 2)
            up_kv = Rows(gr2, 8, cqT[:, 2:3, :], NT, [(kpc(I["l0_mla_w_kv_up"]), 0)], 512, 1, 2)

            def up_pe(pe, ch):
                up_q.pe(pe)
                up_kv.pe(pe)

            def kv_views(r):
                t, h = divmod(r, 2)
                s = up_kv.src(r).rearrange("p (h c) -> p h c", c=P)
                k = Kr[:, t, :].rearrange("p (h c) -> p h c", c=QK)[:, 4 * h:4 * h + 4, 0:NOPE]
                v = Vr[:, t, :].rearrange("p (h c) -> p h c", c=MV)[:, 4 * h:4 * h + 4, :]
                return s, k, v

            QrT = area(NS * SLOT, A0 + 16000, NT, MH * QK)

            def up_act(act, ch):
                for r in range(0, 8, 2):
                    up_q.ready(act, r)
                    take_act(act, up_q.src(r), QrT[:, r // 2, 0:384])
                for r in range(0, 8, 2):
                    up_kv.ready(act, r)
                    s, k, v = kv_views(r)
                    ch(act.activation(k, s[:, :, 0:NOPE], ACT.Copy))
                    take_act(act, s[:, :, NOPE:P], v)

            def up_dve(dve, ch):
                for r in range(1, 8, 2):
                    up_q.ready(dve, r)
                    take_dve(dve, up_q.src(r), QrT[:, r // 2, 384:768])
                for r in range(1, 8, 2):
                    up_kv.ready(dve, r)
                    s, k, v = kv_views(r)
                    ch(dve.tensor_copy(k, s[:, :, 0:NOPE]))
                    take_dve(dve, s[:, :, NOPE:P], v)
            stage(up_pe, up_act, up_dve)

            ss1, rs1 = use(ssd, 2), use(rsd, 1)

            def heads(v):
                return v.rearrange("p t (h c) -> p (t h) c", c=QK)

            def head_norm(eng, ch, src, dst, which, stat):
                b = [P, NT * MH, QK]
                ch(eng.tensor_tensor(heads(dst), heads(src), stat.rearrange("p (n o) -> p n o", o=1).to_broadcast(b),
                                     ALU.mult))
                ch(eng.tensor_tensor(heads(dst), heads(dst), qg[:, which:which + 1, :].to_broadcast(b), ALU.mult))
                tmp = (sqq, sqk)[which]
                for t in range(NT):
                    d = dst[:, t, :].rearrange("p (h c) -> p h c", c=QK)
                    r1, r2 = d[:, :, NOPE:NOPE + HALF], d[:, :, NOPE + HALF:QK]
                    cs_, sn = (v[:, t:t + 1, :].to_broadcast([P, MH, HALF]) for v in (ropec, ropes))
                    a = [tmp[:, 8 * q:8 * q + 8, 0:HALF] for q in range(4)]
                    ch.mark(eng.tensor_tensor(a[0], r1, cs_, ALU.mult))
                    ch.mark(eng.tensor_tensor(a[1], r2, sn, ALU.mult))
                    ch.mark(eng.tensor_tensor(a[2], r2, cs_, ALU.mult))
                    ch(eng.tensor_tensor(a[3], r1, sn, ALU.mult))
                    ch.mark(eng.tensor_tensor(r1, a[0], a[1], ALU.subtract))
                    ch(eng.tensor_tensor(r2, a[2], a[3], ALU.add))

            def hn_act(act, ch):
                act.activation(sqq, heads(QrT), ACT.Square).then_inc(ssd, 1)

            def hn_dve(dve, ch):
                for t in range(NT):
                    ch.mark(dve.tensor_copy(
                        Kr[:, t, :].rearrange("p (h c) -> p h c", c=QK)[:, :, NOPE:QK],
                        cq0[:, t:t + 1, QR + KVR:C0].to_broadcast([P, MH, RO])))
                ch.wait()
                dve.wait_ge(ssd, ss1 + 1)
                ch(dve.tensor_reduce(st[:, 0:32], sqq, AX, ALU.add))
                ch(dve.tensor_tensor(sqq, heads(Kr), heads(Kr), ALU.mult))
                dve.tensor_reduce(st[:, 32:64], sqq, AX, ALU.add).then_inc(ssd, 1)
                dve.wait_ge(rsd, rs1 + 1)
                head_norm(dve, ch, QrT, Qr, 0, st[:, 0:32])

            def hn_po(po, ch):
                po.wait_ge(ssd, ss1 + 2)
                ch(po.tensor_scalar(st[:, 0:64], st[:, 0:64], 1.0 / QK, EPS, ALU.mult, ALU.add))
                po.tensor_tensor(st[:, 0:64], st[:, 0:64], nhalf[:, :].to_broadcast([P, 64]), ALU.pow).then_inc(rsd, 1)
                po.wait_ge(rsd, rs1 + 1)
                head_norm(po, ch, Kr, Kr, 1, st[:, 32:64])
            stage(None, hn_act, hn_dve, hn_po)

            preps = []
            for h in range(MH):
                srcs = [[R[:, t, h * QK:h * QK + QK] for t in range(NT)] for R in (Qr, Kr)]
                preps.append((max(0, 4 * h - 2), max(0, 4 * (h - 1)),
                              [(srcs[0], QT[0:QK, h % 2, :], 1.0), (srcs[1], KT[0:QK, h % 2, :], 1.0)]))

            def sc_mla(pe, v, b, pre0):
                h, i = divmod(v, NT)
                pe.wait_ge(s_pre, pre0 + 2 * h + 2)
                L = causal(v)
                return pe.matmul(ps[:, b, 0:L], QT[0:QK, h % 2, i * P:i * P + P], KT[0:QK, h % 2, 0:L],
                                 start=True, stop=True)
            attention(MH * NT, causal, sc_mla,
                      lambda u, j: Vr[:, j, (u // NT) * MV:(u // NT) * MV + MV], MV,
                      lambda h, i: orow[:, i, h * MV:h * MV + MV], QK ** -0.5, preps)

            T1 = work(A0 + 7808, 4, 512)
            U0 = MH * NT
            sc0, t10, sp0, m10, w0, m20, ex0, pt0, pe0, o0, on0 = (
                use(s, U0) for s in (s_sc, s_t1, s_sp, s_m1, s_w, s_m2, s_ex, s_pt, s_pe, s_o, s_on))
            SBK = (0, 1, 6, 7)

            def sb_pe(pe, ch):
                for v in range(U0 + 4):
                    if v < U0:
                        h, i = divmod(v, NT)
                        L = causal(v)
                        if v >= 4:
                            pe.wait_ge(s_w, w0 + v - 3)
                        r = slice(64 * (h % 2), 64 * (h % 2) + 64)
                        pe.matmul(ps[:, SBK[v % 4], 0:L], sbq[r, h // 2, i * P:i * P + P], sbk[r, h // 2, 0:L],
                                  start=True, stop=True).then_inc(s_sc, 1)
                    if 3 <= v < U0 + 3:
                        u = v - 3
                        pe.wait_ge(s_ex, ex0 + u + 1)
                        if u >= 2:
                            pe.wait_ge(s_pe, pe0 + u - 1)
                        for j in range(causal(u) // P):
                            m = pe.transpose(ps[:, 2 + u % 2, j * P:j * P + P], Pb[:, u % 4, j * P:j * P + P],
                                             ident[:, :])
                        m.then_inc(s_pt, 1)
                    if v >= 4:
                        u = v - 4
                        h = u // NT
                        pe.wait_ge(s_pe, pe0 + u + 1)
                        if u >= 2:
                            pe.wait_ge(s_on, on0 + u - 1)
                        nb = causal(u) // P
                        for j in range(nb):
                            m = pe.matmul(ps[:, 4 + u % 2, 0:64], PT[:, u % 2, j * P:j * P + P],
                                          sbv[:, j, h * 64:h * 64 + 64], start=(j == 0), stop=(j == nb - 1))
                        m.then_inc(s_o, 1)

            def sb_act(act, ch):
                for v in range(U0 + 3):
                    if v < U0:
                        act.wait_ge(s_sc, sc0 + v + 1)
                        if v >= 4:
                            act.wait_ge(s_w, w0 + v - 3)
                        t1 = T1[:, v % 4, 0:causal(v)]
                        ch(act.activation(t1, ps[:, SBK[v % 4], 0:causal(v)], ACT.Abs))
                        ch(act.activation(t1, t1, ACT.Exp, scale=-1.0))
                        act.activation(t1, t1, ACT.Ln, bias=1.0).then_inc(s_t1, 1)
                    if 2 <= v < U0 + 2:
                        u = v - 2
                        act.wait_ge(s_m2, m20 + u + 1)
                        p = Pb[:, u % 4, 0:causal(u)]
                        act.activation(p, p, ACT.Exp).then_inc(s_ex, 1)
                    if v >= 3:
                        u = v - 3
                        L = causal(u)
                        act.wait_ge(s_pt, pt0 + u + 1)
                        if u >= 2:
                            act.wait_ge(s_o, o0 + u - 1)
                        act.activation(PT[:, u % 2, 0:L], ps[:, 2 + u % 2, 0:L], ACT.Copy).then_inc(s_pe, 1)

            def sb_dve(dve, ch):
                for v in range(U0 + 4):
                    if v < U0:
                        dve.wait_ge(s_t1, t10 + v + 1)
                        t1 = T1[:, v % 4, 0:causal(v)]
                        dve.scalar_tensor_tensor(out=t1, in0=ps[:, SBK[v % 4], 0:causal(v)], scalar=0.0, in1=t1,
                                                 op0=ALU.max, op1=ALU.add).then_inc(s_sp, 1)
                    if 1 <= v <= U0:
                        u = v - 1
                        L = causal(u)
                        t1 = T1[:, u % 4, 0:L]
                        p = Pb[:, u % 4, 0:L]
                        dve.wait_ge(s_m1, m10 + u + 1)
                        if u >= 4:
                            dve.wait_ge(s_pt, pt0 + u - 3)
                        ch(dve.tensor_tensor_scan(p[:, ::-1], ones[:, 0:1].to_broadcast([P, L]), t1[:, ::-1], 0.0,
                                                  ALU.mult, ALU.add))
                        dve.tensor_tensor(p, ps[:, SBK[u % 4], 0:L], p, ALU.subtract).then_inc(s_w, 1)
                    if v >= 4:
                        u = v - 4
                        h, i = divmod(u, NT)
                        dve.wait_ge(s_o, o0 + u + 1)
                        dve.tensor_copy(orow[:, i, 512 + h * 64:512 + h * 64 + 64],
                                        ps[:, 4 + u % 2, 0:64]).then_inc(s_on, 1)

            def sb_po(po, ch):
                for v in range(U0 + 1):
                    if v < U0:
                        dg = T1[:, v % 4, causal(v) - P:causal(v)]
                        po.wait_ge(s_sp, sp0 + v + 1)
                        po.affine_select(out=dg, in_=dg, compare_op=ALU.is_gt, fill=0.0,
                                         base=0, pattern=[[-1, P]], channel_multiplier=1).then_inc(s_m1, 1)
                    if v >= 1:
                        u = v - 1
                        dg = Pb[:, u % 4, causal(u) - P:causal(u)]
                        po.wait_ge(s_w, w0 + u + 1)
                        po.affine_select(out=dg, in_=dg, compare_op=ALU.is_gt, fill=NEG,
                                         base=0, pattern=[[-1, P]], channel_multiplier=1).then_inc(s_m2, 1)
            stage(sb_pe, sb_act, sb_dve, sb_po)
            out_stage(orow, work(A0, KD, S), I["l0_w_o"])
        if on(2):
            norm_stage(x, actT, G_F0, NT)
            ffn_stage(I["l0_w_gate"], I["l0_w_up"], I["l0_w_down"])

        if on(3):
            FQr = work(A0, NT, D)
            FKr = work(A0 + 4096, NT, D)
            FVr = work(A0 + 8192, NT, D)
            FQT = work(A0 + 12288, 2, 512)
            FKT = work(A0 + 13312, 2, 512)
            CT8 = work(A0 + 14336, S)
            sqf = work(A0 + 14848, NT, D)
            norm_stage(x, actT, G_A1, NT)
            gr = Groups(28, "VVVV" + "AV" * 12)
            w = I["l1_w_in"]
            fj = Rows(gr, 0, actT, NT, [(kpc(w[:, 3 * D:3 * D + FH]), 0)], FH)
            fjobs = [(Rows(gr, 4 + 4 * j, actT, NT, [(kpc(w[:, j * 512:j * 512 + 512]), 0)], 512),
                      (FQr, FKr, FVr)[j // 2], j % 2) for j in range(6)]

            def fp_pe(pe, ch):
                fj.pe(pe)
                for job, _, _ in fjobs:
                    job.pe(pe)

            def fp_act(act, ch):
                for job, dst, c in fjobs:
                    for t in range(0, NT, 2):
                        job.ready(act, t)
                        take_act(act, job.src(t), dst[:, t, c * 512:c * 512 + 512])

            def fp_dve(dve, ch):
                for t in range(NT):
                    fj.ready(dve, t)
                    dve.tensor_tensor(FG[:, 0, t, :], fj.src(t), ffb[:, :], ALU.add).then_inc(ev, 1)
                for job, dst, c in fjobs:
                    for t in range(1, NT, 2):
                        job.ready(dve, t)
                        take_dve(dve, job.src(t), dst[:, t, c * 512:c * 512 + 512])
            stage(fp_pe, fp_act, fp_dve)
            softplus_stages(FH, (CS, CT8[0:FH, :], 8.0))
            ss2, rs2 = use(ssd, 1), use(rsd, 1)
            nn = NT * FH

            def h64(v):
                return v[:, :, :].rearrange("p t (h c) -> p (t h) c", c=64)

            def fn_act(act, ch):
                act.activation(sqf, FQr, ACT.Square).then_inc(ssd, 1)

            def fn_dve(dve, ch):
                dve.wait_ge(ssd, ss2 + 1)
                ch(dve.tensor_reduce(st[:, 0:nn], h64(sqf), AX, ALU.add))
                ch(dve.tensor_tensor(sqf, FKr, FKr, ALU.mult))
                dve.tensor_reduce(st[:, nn:2 * nn], h64(sqf), AX, ALU.add).then_inc(midv, 1)
                dve.wait_ge(rsd, rs2 + 1)
                ch(dve.tensor_tensor(h64(FQr), h64(FQr),
                                     st[:, 0:nn].rearrange("p (n o) -> p n o", o=1).to_broadcast([P, nn, 64]),
                                     ALU.mult))
            mv2 = use(midv, 1)

            def fn_po(po, ch):
                po.wait_ge(midv, mv2 + 1)
                ch(po.tensor_scalar(st[:, :], st[:, :], 1.0 / 64, EPS, ALU.mult, ALU.add))
                po.tensor_tensor(st[:, :], st[:, :], nhalf[:, :].to_broadcast([P, 2 * nn]), ALU.pow).then_inc(rsd, 1)
                po.wait_ge(rsd, rs2 + 1)
                ch(po.tensor_tensor(h64(FKr), h64(FKr),
                                    st[:, nn:2 * nn].rearrange("p (n o) -> p n o", o=1).to_broadcast([P, nn, 64]),
                                    ALU.mult))
            stage(None, fn_act, fn_dve, fn_po)

            preps = []
            for hp in range(FH // 2):
                srcs = [[R[:, t, hp * P:hp * P + P] for t in range(NT)] for R in (FQr, FKr)]
                preps.append((max(0, 8 * hp - 3), max(0, 8 * (hp - 1)),
                              [(srcs[0], FQT[:, hp % 2, :], cols2[:, FQ:FQ + 1]),
                               (srcs[1], FKT[:, hp % 2, :], cols2[:, FK:FK + 1])]))

            def sc_fox(pe, v, b, pre0):
                h, i = divmod(v, NT)
                pe.wait_ge(s_pre, pre0 + 2 * (h // 2) + 2)
                L = causal(v)
                r = slice(64 * (h % 2), 64 * (h % 2) + 64)
                pe.matmul(ps[:, b, 0:L], FQT[r, (h // 2) % 2, i * P:i * P + P], FKT[r, (h // 2) % 2, 0:L],
                          start=True, stop=False)
                return pe.matmul(ps[:, b, 0:L], ident[0:FH, h:h + 1].to_broadcast([FH, P]), CT8[0:FH, 0:L],
                                 start=False, stop=True)
            attention(FH * NT, causal, sc_fox,
                      lambda u, j: FVr[:, j, (u // NT) * 64:(u // NT) * 64 + 64], 64,
                      lambda h, i: orow[:, i, h * 64:h * 64 + 64], 0.125, preps, fox=True)
            out_stage(orow, work(A0, KD, S), I["l1_w_o"])
        if on(4):
            norm_stage(x, actT, G_F1, NT)
            ffn_stage(I["l1_w_gate"], I["l1_w_up"], I["l1_w_down"])

        late = []

        def load_now(name, dst, src):
            s = sem(name)
            late.append((len(stages), dst, src, s))
            return s, 16

        if on(5):
            mqk = work(A0, 16, S)
            mv = work(A0 + 8192, NT, D)
            H = work(A0 + 12288, NT, D)
            acc = work(A0 + 16384, 2, 512)
            CTm = work(A0 + 17408, S)
            E = work(A0 + 17920, 2, 512)
            norm_stage(x, actT, G_MIX, NT)
            w = I["w_in_2"][0]
            gr = Groups(28, "V" * 4 + "C" * 16 + "AV" * 4)
            ij = Rows(gr, 0, actT, NT, [(kpc(w[:, 4096:4104]), 0)], 8)
            qkj = [Cols(gr, 4 + 4 * c, actT, S, [(kpc(w[:, c * 512:c * 512 + 512]), 0)]) for c in range(4)]
            vj = [Rows(gr, 20 + 4 * c, actT, NT, [(kpc(w[:, 2048 + c * 512:2560 + c * 512]), 0)], 512)
                  for c in range(2)]
            cv0, sl0 = gr.freed[4][1] - 1, use(mida, 16)

            def mp_pe(pe, ch):
                for job in [ij] + qkj + vj:
                    job.pe(pe)

            def mp_act(act, ch):
                for c in range(16):
                    act.wait_ge(midv, cv0 + c + 1)
                    act.activation(mqk[:, c, :], acc[:, c % 2, :], ACT.Silu,
                                   bias=cols2[:, CB + c:CB + c + 1]).then_inc(mida, 1)
                for c, job in enumerate(vj):
                    for t in range(0, NT, 2):
                        job.ready(act, t)
                        take_act(act, job.src(t), mv[:, t, c * 512:c * 512 + 512])

            def mp_dve(dve, ch):
                for t in range(NT):
                    ij.ready(dve, t)
                    b = ps[:, gr.bank(t), :]
                    ch(dve.tensor_tensor(FG[:, 1, t, 4:8], b[:, 0:4], bif[:, 0:4], ALU.add))
                    dve.tensor_tensor(FG[:, 0, t, 0:4], b[:, 4:8], bif[:, 4:8], ALU.add).then_inc(ev, 1)
                for c in range(16):
                    job = qkj[c // 4]
                    job.ready(dve, c % 4)
                    if c >= 2:
                        dve.wait_ge(mida, sl0 + c - 1)
                    p, a = job.src(c % 4), acc[:, c % 2, :]
                    tap = lambda i: cols2[:, CW + 16 * i + c:CW + 16 * i + c + 1]
                    ch(dve.tensor_scalar(a, p, tap(3), None, ALU.mult))
                    for s in (1, 2, 3):
                        ins = dve.scalar_tensor_tensor(out=a[:, s:S], in0=p[:, 0:S - s], scalar=tap(3 - s),
                                                       in1=a[:, s:S], op0=ALU.mult, op1=ALU.add)
                        if s < 3:
                            ch(ins)
                    ins.then_inc(midv, 1)
                for c, job in enumerate(vj):
                    for t in range(1, NT, 2):
                        job.ready(dve, t)
                        take_dve(dve, job.src(t), mv[:, t, c * 512:c * 512 + 512])
            stage(mp_pe, mp_act, mp_dve)

            def input_gates(dve, ch):
                ch(dve.tensor_tensor(FG[:, 1, :, 8:12], FG[:, 1, :, 4:8], CS[:, :, 0:4], ALU.add))
            softplus_stages(LH, (FG[:, 1, :, 8:12], CTm[0:LH, :], 1.0), input_gates)

            def sc_ml(pe, v, b, pre0):
                h, i = divmod(v, NT)
                L = causal(v)
                pe.matmul(ps[:, 6 + v % 2, 0:L], ident[0:LH, h:h + 1].to_broadcast([LH, P]), CTm[0:LH, 0:L],
                          start=True, stop=True)
                for k in range(2):
                    m = pe.matmul(ps[:, b, 0:L], mqk[:, 2 * h + k, i * P:i * P + P], mqk[:, 8 + 2 * h + k, 0:L],
                                  start=(k == 0), stop=(k == 1))
                return m
            attention(LH * NT, causal, sc_ml, lambda u, j: mv[:, j, (u // NT) * DH:(u // NT) * DH + DH], DH,
                      lambda h, i: H[:, i, h * DH:h * DH + DH], 1.0, kind="mlstm")

            sqm = work(A0, NT, D)
            mhb = work(A0 + 4096, D)
            mhb_in = load_now("mhb_in", mhb, every(I["mh_norm_g_2"][0]))
            sgb = work(A0 + 5120, D)
            sgb_in = load_now("sgb_in", sgb, every(I["sgu_norm_g_2"][0]))
            gb = work(A0 + 6144, 2 * D)
            gb_in = load_now("gb_in", gb, every(I["b_gate_2"][0]))
            wsr = work(0, G8, P)
            wsr_in = load_now("wsr_in", wsr, I["w_s_2"][0].rearrange("g t s -> t g s"))
            ss3, rs3 = use(ssd, 1), use(rsd, 1)

            def d256(v):
                return v[:, :, :].rearrange("p t (h c) -> p (t h) c", c=DH)

            def hm_act(act, ch):
                act.activation(sqm, H, ACT.Square).then_inc(ssd, 1)
            mv3 = use(midv, 1)

            def hm_dve(dve, ch):
                dve.wait_ge(ssd, ss3 + 1)
                dve.tensor_reduce(st[:, 0:16], d256(sqm), AX, ALU.add).then_inc(midv, 1)
                dve.wait_ge(rsd, rs3 + 1)
                ch(dve.tensor_tensor(d256(H), d256(H),
                                     st[:, 0:16].rearrange("p (n o) -> p n o", o=1).to_broadcast([P, 16, DH]),
                                     ALU.mult))
                dve.wait_ge(*mhb_in)
                ch(dve.tensor_tensor(H, H, mhb.rearrange("p (o c) -> p o c", o=1).to_broadcast([P, NT, D]), ALU.mult))

            def hm_po(po, ch):
                po.wait_ge(midv, mv3 + 1)
                ch(po.tensor_scalar(st[:, 0:16], st[:, 0:16], 1.0 / DH, EPS, ALU.mult, ALU.add))
                po.tensor_tensor(st[:, 0:16], st[:, 0:16], nhalf[:, :].to_broadcast([P, 16]), ALU.pow).then_inc(rsd, 1)
            stage(None, hm_act, hm_dve, hm_po)

            tmp = work(A0 + 16384, 4, 512)
            Vs = work(A0 + 8192, NT, D)
            Mx = work(A0, NT, D)
            wsT = work(1024, G8, P)

            def gated_stage(spec, dst_of):
                kinds = [kind for _, kind, _, _ in spec for t in range(NT)]
                gr = Groups(len(kinds), ["A" if k == "gelu" else "C" if k == "bias" else "X" for k in kinds])
                jobs = [(Rows(gr, NT * n, actT, NT, [(kpc(w[:, c0:c0 + 512]), 0)], 512), kind, half, bcol)
                        for n, (c0, kind, half, bcol) in enumerate(spec)]
                order = [k for k in range(len(kinds)) if kinds[k] != "gelu"]
                a0, u0 = use(mida, len(order)), use(xsd, len(order))
                for n, g in enumerate(order):
                    if gr.who[g] == "X":
                        gr.freed[g] = (mida, a0 + n + 1)

                def steps():
                    n = 0
                    for j, (job, kind, half, bcol) in enumerate(jobs):
                        for t in range(NT):
                            yield n, job, kind, half, bcol, t, NT * j + t
                            n += kind != "gelu"

                def pe(pe, ch):
                    for job, _, _, _ in jobs:
                        job.pe(pe)

                def act(act, ch):
                    for n, job, kind, half, _, t, g in steps():
                        b = tmp[:, n % 4, :]
                        if kind == "gelu":
                            job.ready(act, t)
                            act.activation(Vs[:, t, half * 512:half * 512 + 512], job.src(t),
                                           ACT.Gelu_apprx_tanh).then_inc(ea, 1)
                        elif kind == "bias":
                            act.wait_ge(*gr.freed[g])
                            act.activation(b, b, ACT.Sigmoid).then_inc(mida, 1)
                        else:
                            job.ready(act, t)
                            if n >= 4:
                                act.wait_ge(xsd, u0 + n - 3)
                            act.activation(b, job.src(t), kind).then_inc(mida, 1)

                def dve(dve, ch):
                    dve.wait_ge(*gb_in)
                    todo = []

                    def finish(n, half, bcol, t):
                        dve.wait_ge(mida, a0 + n + 1)
                        dst, add = dst_of(bcol)
                        d = dst[:, t, half * 512:half * 512 + 512]
                        ins = dve.tensor_tensor(d, d, tmp[:, n % 4, :], ALU.mult)
                        if add:
                            ch(ins)
                            y = H[:, t, half * 512:half * 512 + 512]
                            ins = dve.tensor_tensor(y, y, d, ALU.add)
                        ins.then_inc(xsd, 1)
                    for n, job, kind, half, bcol, t, g in steps():
                        if kind == "gelu":
                            continue
                        if kind == "bias":
                            job.ready(dve, t)
                            if n >= 4:
                                dve.wait_ge(xsd, u0 + n - 3)
                            dve.tensor_tensor(tmp[:, n % 4, :], job.src(t), gb[:, bcol:bcol + 512],
                                              ALU.add).then_inc(midv, 1)
                        todo.append((n, half, bcol, t))
                        if len(todo) > 1:
                            finish(*todo.pop(0))
                    for q in todo:
                        finish(*q)
                stage(pe, act, dve)

            gated_stage([(3072, ACT.Sigmoid, 0, None), (3584, ACT.Sigmoid, 1, None),
                         (6152, "bias", 0, 0), (6664, "bias", 1, 512),
                         (5128, "gelu", 0, None), (5640, "gelu", 1, None)],
                        lambda bcol: (H, False))

            ss4, rs4 = use(ssd, 1), use(rsd, 1)

            def sv_act(act, ch):
                for t in range(NT):
                    ins = act.activation(tmp[:, 0:2, :].rearrange("p a b -> p (a b)"), Vs[:, t, :], ACT.Square,
                                         accum_out=ss[:, t:t + 1])
                    if t < NT - 1:
                        ch(ins)
                ins.then_inc(ssd, 1)

            def sv_po(po, ch):
                po.wait_ge(ssd, ss4 + 1)
                ch(po.tensor_scalar(ss[:, 0:4], ss[:, 0:4], 1.0 / D, EPS, ALU.mult, ALU.add))
                po.tensor_tensor(ss[:, 0:4], ss[:, 0:4], nhalf[:, :].to_broadcast([P, 4]), ALU.pow).then_inc(rsd, 1)
            tr4 = use(tr, 2)

            def sv_pe(pe, ch):
                pe.wait_ge(*wsr_in)
                for g in range(G8):
                    m = pe.transpose(ps[:, g // 4, (g % 4) * P:(g % 4) * P + P], wsr[:, g, :], ident[:, :])
                    if g % 4 == 3:
                        m.then_inc(tr, 1)

            def sv_dve(dve, ch):
                dve.wait_ge(*sgb_in)
                for q in range(2):
                    dve.wait_ge(tr, tr4 + q + 1)
                    ch.mark(dve.tensor_tensor(wsT[:, 4 * q:4 * q + 4, :],
                                              ps[:, q, :].rearrange("p (g s) -> p g s", g=4),
                                              tri[:, :].rearrange("p (o s) -> p o s", o=1).to_broadcast([P, 4, P]),
                                              ALU.mult))
                dve.wait_ge(rsd, rs4 + 1)
                for t in range(NT):
                    ch(dve.scalar_tensor_tensor(out=Vs[:, t, :], in0=Vs[:, t, :], scalar=ss[:, t:t + 1],
                                                in1=sgb, op0=ALU.mult, op1=ALU.mult))
            stage(sv_pe, sv_act, sv_dve, sv_po)

            gm = Groups(8, "A")
            tr5 = use(tr, 8)

            def mix_pe(pe, ch):
                for g in range(G8):
                    for c in range(NT):
                        m = pe.matmul(ps[:, g, c * P:c * P + P], wsT[:, g, :], Vs[:, c, g * P:g * P + P],
                                      start=True, stop=True)
                    m.then_inc(tr, 1)

            def mix_act(act, ch):
                for g in range(G8):
                    act.wait_ge(tr, tr5 + g + 1)
                    act.activation(Mx[:, :, g * P:g * P + P], ps[:, g, :].rearrange("p (c s) -> p c s", c=NT),
                                   ACT.Identity, bias=cols2[:, BS + g:BS + g + 1]).then_inc(ea, 1)
            stage(mix_pe, mix_act)
            gated_stage([(4104, ACT.Gelu_apprx_tanh, 0, None), (4616, ACT.Gelu_apprx_tanh, 1, None),
                         (7176, "bias", 0, 1024), (7688, "bias", 1, 1536)],
                        lambda bcol: (Mx, bcol is not None))
            out_stage(H, work(A0, KD, S), I["w_out_2"][0])

        if on(6):
            memr = work(A0, MT, D)
            mem_in = load_now("mem_in", memr, I["mem_2"][0].rearrange("(t p) d -> p t d", p=P))
            memT = work(A0 + 2048, KD, NM)
            xk = work(A0 + 4096, KD, NM)
            xv = work(A0 + 6144, MT, D)
            xq = work(A0 + 8192, KD, S)

            def mem_dve(dve, ch):
                dve.wait_ge(*mem_in)
            stage(None, None, mem_dve)
            norm_stage(memr, memT, G_MEM, MT)
            norm_stage(x, actT, G_X, NT)
            gr = Groups(20, "AV")
            jobs = []
            wkv, wq = I["w_xkv_2"][0], I["w_xq_2"][0]

            def cols_to(v, c):
                return lambda r: v[:, 4 * c + r, :]

            def rows_to(v, c):
                return lambda r: v[:, r, c * 512:c * 512 + 512]
            for c in range(2):
                jobs.append((Cols(gr, 4 * c, memT, NM, [(kpc(wkv[:, c * 512:c * 512 + 512]), 0)]), cols_to(xk, c), 1.0))
            for c in range(2):
                jobs.append((Rows(gr, 8 + 2 * c, memT, MT, [(kpc(wkv[:, D + c * 512:D + c * 512 + 512]), 0)], 512),
                             rows_to(xv, c), 1.0))
            for c in range(2):
                jobs.append((Cols(gr, 12 + 4 * c, actT, S, [(kpc(wq[:, c * 512:c * 512 + 512]), 0)]),
                             cols_to(xq, c), 1.0))
            plain_stage(jobs, gr)

            def sc_x(pe, v, b, pre0):
                h, i = divmod(v, NT)
                for k in range(2):
                    m = pe.matmul(ps[:, b, 0:NM], xq[:, 2 * h + k, i * P:i * P + P], xk[:, 2 * h + k, :],
                                  start=(k == 0), stop=(k == 1))
                return m
            attention(LH * NT, lambda v: NM, sc_x, lambda u, j: xv[:, j, (u // NT) * DH:(u // NT) * DH + DH], DH,
                      lambda h, i: orow[:, i, h * DH:h * DH + DH], DH ** -0.5)
            out_stage(orow, work(A0 + 12288, KD, S), I["w_xo_2"][0])

        if on(7):
            norm_stage(x, actT, G_MOE, NT)
            moe_bar = len(stages)
            xn = moe(0, NT, D)
            LG = moe(4096, NT, NGR + NE)
            OB = moe(4240, D)
            XT = moe(5264, KD, P)
            OH = moe(6288, NT, P)
            HS = moe(6800, 512)
            HB = moe(7312, 512)
            HT = moe(7824, 4, P)
            gmoe = moe(8336, D)
            gfin = moe(9360, D)
            A2 = moe(10384, 2 * NT, NE)
            As = moe(10640, NT, NE)
            RK = moe(10768, NT, NE)
            T32 = moe(11280, NT, NE)
            T4 = moe(11408, NT, NGR)
            GO = moe(11424, NT, NGR)
            s1 = moe(11440, 16, NT)
            gate = moe(11504, 2, NT)
            rowi = moe(11512, 2, NT)
            rowu = sb("rowu", [P, 2 * NT], U32)
            cnt = moe(11520, NE)
            flg = moe(11552, 3, NE)
            pos = moe(11648, 3, NE)
            t96 = moe(11840, 3, NE)
            codee = moe(11936, 3, NE)
            codeb = moe(12032, 3, NE)
            val = moe(12128, 16)
            vsh = moe(12144, NOVER)
            rkq = moe(12152, NT, 1)
            rbase = moe(12160, 4, NE)
            zrow = moe(12288, D)
            gmoe_in = load_now("gmoe_in", gmoe, every(I["norm_moe_g_2"][0]))
            gfin_in = load_now("gfin_in", gfin, every(I["norm_f_g_2"]))
            gr = Groups(4, "V")
            rj = None
            loads = [(kpc(I["w_rg_2"][0]), 0), (kpc(I["w_re_2"][0]), NGR)]
            rj = Rows(gr, 0, actT, NT, loads, NGR + NE)
            v0, a0, t0 = use(midv, 2), use(mida, 1), use(tr, 1)

            def b3(v, n):
                return v.rearrange("p (a o) -> p a o", o=1).to_broadcast([P, v.shape[1], n])

            def first_of(dve, ch, oh, vals, m, n, tmpv):
                ch(dve.tensor_reduce(m, vals, AX, ALU.max))
                ch(dve.tensor_tensor(oh, vals, b3(m, n), ALU.is_equal))
                ch(dve.tensor_tensor(oh, oh, desc[:, NE - n:NE].rearrange("p (o c) -> p o c", o=1
                                                                          ).to_broadcast([P, NT, n]), ALU.mult))
                ch(dve.tensor_reduce(tmpv, oh, AX, ALU.max))
                ch(dve.tensor_tensor(oh, oh, b3(tmpv, n), ALU.is_equal))

            def rt_pe(pe, ch):
                rj.pe(pe)
                pe.wait_ge(midv, v0 + 2)
                for t in range(NT):
                    for j in range(t + 1):
                        m = pe.matmul(ps[:, 4, t * NE:t * NE + NE], (tri if j == t else ones)[:, :], As[:, j, :],
                                      start=(j == 0), stop=(j == t))
                for j in range(NT):
                    m = pe.matmul(ps[:, 5, 0:NE], ones[:, :], As[:, j, :], start=(j == 0), stop=(j == NT - 1))
                m.then_inc(tr, 1)

            def rt_act(act, ch):
                for t in range(NT):
                    act.mul(xn[:, t, :], x[:, t, :], ss[:, t:t + 1]).then_inc(xsd, 1)
                act.wait_ge(midv, v0 + 1)
                ch(act.activation(T4, T4, ACT.Exp))
                act.activation(s1[:, 5, :], s1[:, 5, :], ACT.Exp).then_inc(mida, 1)
            xn0 = use(xsd, NT)

            z_in = sem("z_in")

            def rt_po(po, ch):
                ch(po.memset(zrow, 0.0))
                for q in range(NOVER):
                    po.dma_start(obuf[(NE + q) * P:(NE + q + 1) * P, :], zrow).then_inc(z_in, 16)
                po.wait_ge(xsd, xn0 + NT)
                po.wait_ge(*gmoe_in)
                ch(po.tensor_tensor(xn, xn, gmoe.rearrange("p (o c) -> p o c", o=1).to_broadcast([P, NT, D]),
                                    ALU.mult))

            def rt_dve(dve, ch):
                for t in range(NT):
                    rj.ready(dve, t)
                    dve.tensor_tensor(LG[:, t, :], rj.src(t), rbias[:, :], ALU.add).then_inc(ev, 1)
                gr.wait_taken(dve, NT - 1)
                G, Ee = LG[:, :, 0:NGR], LG[:, :, NGR:NGR + NE]
                m1, m2, gm_, w_ = s1[:, 0, :], s1[:, 1, :], s1[:, 2, :], s1[:, 3, :]
                first_of(dve, ch, GO, G, gm_, NGR, w_)
                ch(dve.tensor_tensor(T4, G, b3(gm_, NGR), ALU.subtract))
                ch(dve.tensor_scalar(GO, GO, 1.0, 1e30, ALU.subtract, ALU.mult))
                Eg = Ee.rearrange("p t (g e) -> p t g e", e=EPG)
                for g in range(NGR):
                    ch(dve.tensor_tensor(Eg[:, :, g, :], Eg[:, :, g, :],
                                         GO[:, :, g:g + 1].to_broadcast([P, NT, EPG]), ALU.add))
                first_of(dve, ch, A2[:, 0:NT, :], Ee, m1, NE, w_)
                ch(dve.scalar_tensor_tensor(out=T32, in0=A2[:, 0:NT, :], scalar=-2e30, in1=Ee,
                                            op0=ALU.mult, op1=ALU.add))
                first_of(dve, ch, A2[:, NT:2 * NT, :], T32, m2, NE, w_)
                dve.tensor_tensor(s1[:, 5, :], m2, m1, ALU.subtract).then_inc(midv, 1)
                dve.tensor_tensor(As, A2[:, 0:NT, :], A2[:, NT:2 * NT, :], ALU.add).then_inc(midv, 1)
                dve.wait_ge(midv, v0 + 2)
                dve.wait_ge(mida, a0 + 1)
                ch(dve.tensor_reduce(s1[:, 6, :], T4, AX, ALU.add))
                ch(dve.tensor_scalar(s1[:, 7, :], s1[:, 5, :], 1.0, None, ALU.add))
                ch(dve.tensor_tensor(s1[:, 6, :], s1[:, 6, :], s1[:, 7, :], ALU.mult))
                ch(dve.reciprocal(gate[:, 0, :], s1[:, 6, :]))
                ch(dve.tensor_tensor(gate[:, 1, :], gate[:, 0, :], s1[:, 5, :], ALU.mult))
                dve.wait_ge(tr, t0 + 1)
                rk = ps[:, 4, 0:NT * NE].rearrange("p (t e) -> p t e", t=NT)
                ch(dve.tensor_tensor(RK, As, rk, ALU.mult))
                ch(dve.tensor_copy(cnt, ps[:, 5, 0:NE]))
                for b in range(3):
                    ch.mark(dve.tensor_scalar(flg[:, b, :], cnt, 128.0 * (b + 1) + 0.5, None, ALU.is_gt))
                    ch.mark(dve.tensor_copy(codee[:, b, :], eidx[:, :]))
                    ch.mark(dve.memset(codeb[:, b, :], 128.0 * (b + 1)))
                ch.mark(dve.memset(val, 0.0))
                ch.wait()
                f1, p1, q1, ce, cb = (v.rearrange("p b e -> p (b e)") for v in (flg, pos, t96, codee, codeb))
                ch(dve.tensor_tensor_scan(p1, ones[:, 0:96], f1, 0.0, ALU.mult, ALU.add))
                ch(dve.tensor_copy(val[:, 0:1], p1[:, 95:96]))
                ch(dve.tensor_tensor(p1, p1, f1, ALU.mult))
                for q in range(NOVER):
                    for c1, to in ((ce, val[:, 1 + q:2 + q]), (cb, vsh[:, q:q + 1])):
                        ch(dve.scalar_tensor_tensor(out=q1, in0=p1, scalar=float(q + 1), in1=c1,
                                                    op0=ALU.is_equal, op1=ALU.mult))
                        ch(dve.tensor_reduce(to, q1, AX, ALU.add))
                ch(dve.tensor_copy(ft[0:1, :], val[0:1, :]))
                ch.mark(dve.tensor_scalar(rbase[:, 0, :], eidx[:, :], float(P), None, ALU.mult))
                for b in range(3):
                    ch.mark(dve.tensor_scalar(rbase[:, 1 + b, :], pos[:, b, :], float(P),
                                              float((NE - 1) * P - P * (b + 1)), ALU.mult, ALU.add))
                ch.wait()
                for b in (3, 2, 1):
                    ch(dve.tensor_tensor(rbase[:, b, :], rbase[:, b, :], rbase[:, b - 1, :], ALU.subtract))
                for k in range(2):
                    A = A2[:, NT * k:NT * k + NT, :]
                    rank, part, row = s1[:, 9, :], s1[:, 8, :], rowi[:, k, :]
                    ch(dve.tensor_tensor(T32, A, RK, ALU.mult))
                    ch(dve.tensor_reduce(rank, T32, AX, ALU.add))
                    ch(dve.tensor_scalar(row, rank, 1.0, None, ALU.subtract))
                    for b in range(4):
                        ch(dve.tensor_tensor(T32, A, rbase[:, b:b + 1, :].to_broadcast([P, NT, NE]), ALU.mult))
                        ch(dve.tensor_reduce(part, T32, AX, ALU.add))
                        if b:
                            ch(dve.scalar_tensor_tensor(out=part, in0=rank, scalar=P * b + 0.5, in1=part,
                                                        op0=ALU.is_gt, op1=ALU.mult))
                        ch(dve.tensor_tensor(row, row, part, ALU.add))
                ch(dve.tensor_copy(rowu[:, :].rearrange("p (k t) -> p k t", k=2), rowi))
            stage(rt_pe, rt_act, rt_dve, rt_po)

            def w1v(s):
                return ring[s].rearrange("p (k c) -> p k c", c=EF)

            def w2v(s):
                return ring[s].rearrange("p (k c) -> p k c", c=D)

            def after(n):
                return not (isinstance(n, int) and n == 0)

            def onehot(dve, n, col):
                rk = RK[:, :, bass.ds(col, 1)]
                dve.tensor_tensor(OH, rank1[:, :].rearrange("p (o c) -> p o c", o=1).to_broadcast([P, NT, P]),
                                  rk.to_broadcast([P, NT, P]), ALU.is_equal).then_inc(m_oh, 1)
            def gather(pe, n):
                pe.wait_ge(m_oh, n + 1)
                for k in range(KD):
                    for t in range(NT):
                        m = pe.matmul(ps[:, k // 4, (k % 4) * P:(k % 4) * P + P], xn[:, t, k * P:k * P + P],
                                      OH[:, t, :], start=(t == 0), stop=(t == NT - 1))
                    if k % 4 == 3:
                        m.then_inc(m_gx, 1)

            def up(pe, n, par, load):
                pe.wait_ge(m_gxa, n + 1)
                pe.wait_ge(m_gxv, n + 1)
                if after(n):
                    pe.wait_ge(m_hb, n)
                for j in range(2):
                    pe.wait_ge(w_moe[3 * par + j], 16 * load)
                    for k in range(KD):
                        m = pe.matmul(ps[:, 2 + j, :], XT[:, k, :], w1v(3 * par + j)[:, k, :],
                                      start=(k == 0), stop=(k == KD - 1))
                    m.then_inc(m_up, 1)

            def down(pe, n, par, load):
                pe.wait_ge(m_hb, n + 1)
                for j in range(4):
                    m = pe.transpose(ps[:, 4, j * P:j * P + P], HB[:, j * P:j * P + P], ident[:, :])
                m.then_inc(m_tr, 1)
                pe.wait_ge(m_hT, n + 1)
                pe.wait_ge(w_moe[3 * par + 2], 16 * load)
                if after(n):
                    pe.wait_ge(m_oa, n)
                    pe.wait_ge(m_ov, n)
                for h in range(2):
                    for k in range(4):
                        m = pe.matmul(ps[:, 5 + h, :], HT[:, k, :], w2v(3 * par + 2)[:, k, h * 512:h * 512 + 512],
                                      start=(k == 0), stop=(k == 3))
                m.then_inc(m_dn, 1)

            def cols_a(act, n):
                act.wait_ge(m_gx, n * 2 + 1)
                act.activation(XT[:, 0:4, :], ps[:, 0, :].rearrange("p (k s) -> p k s", k=4),
                               ACT.Copy).then_inc(m_gxa, 1)

            def cols_v(dve, n):
                dve.wait_ge(m_gx, n * 2 + 2)
                dve.tensor_copy(XT[:, 4:8, :], ps[:, 1, :].rearrange("p (k s) -> p k s", k=4)).then_inc(m_gxv, 1)

            def silu_a(act, n):
                act.wait_ge(m_up, n * 2 + 1)
                if after(n):
                    act.wait_ge(m_hb, n)
                act.activation(HS, ps[:, 2, :], ACT.Silu).then_inc(m_si, 1)

            def gated_v(dve, n):
                dve.wait_ge(m_up, n * 2 + 2)
                dve.wait_ge(m_si, n + 1)
                if after(n):
                    dve.wait_ge(m_tr, n)
                dve.tensor_tensor(HB, HS, ps[:, 3, :], ALU.mult).then_inc(m_hb, 1)

            def out_a(act, n, row):
                act.wait_ge(m_tr, n + 1)
                act.activation(HT, ps[:, 4, :].rearrange("p (k s) -> p k s", k=4), ACT.Copy).then_inc(m_hT, 1)
                act.wait_ge(m_dn, n + 1)
                if after(n):
                    act.wait_ge(m_st, n * 16)
                act.activation(OB[:, 0:512], ps[:, 5, :], ACT.Copy).then_inc(m_oa, 1)
                act.wait_ge(m_oa, n + 1)
                act.wait_ge(m_ov, n + 1)
                act.dma_start(obuf[bass.ds(row, P), :], OB).then_inc(m_st, 16)

            def out_v(dve, n):
                dve.wait_ge(m_dn, n + 1)
                if after(n):
                    dve.wait_ge(m_st, n * 16)
                dve.tensor_copy(OB[:, 512:1024], ps[:, 6, :]).then_inc(m_ov, 1)

            m_rk = sem("m_rk")

            def over(eng, body):
                n_over = eng.value_load(ft[0:1, 0:1], min_val=0, max_val=NOVER)
                for q in range(NOVER):
                    with eng.If(n_over > q):
                        body(q, NE + q)

            def expert_of(eng, q):
                return eng.value_load(ft[0:1, 1 + q:2 + q], min_val=0, max_val=NE - 1)

            def ex_pe(pe, ch):
                gather(pe, 0)
                for n in range(2):
                    up(pe, n, n, 1)
                    gather(pe, n + 1)
                    down(pe, n, n, 1)
                with pe.Fori(1, NE // 2 - 1) as i:
                    for par in range(2):
                        n = i * 2 + par
                        up(pe, n, par, i + 1)
                        gather(pe, n + 1)
                        down(pe, n, par, i + 1)
                up(pe, NE - 2, 0, NE // 2)
                gather(pe, NE - 1)
                down(pe, NE - 2, 0, NE // 2)
                up(pe, NE - 1, 1, NE // 2)
                down(pe, NE - 1, 1, NE // 2)

                def body(q, n):
                    gather(pe, n)
                    up(pe, n, 0, NE // 2 + 1 + q)
                    down(pe, n, 0, NE // 2 + 1 + q)
                over(pe, body)

            def ex_act(act, ch):
                cols_a(act, 0)
                silu_a(act, 0)
                cols_a(act, 1)
                out_a(act, 0, 0)
                with act.Fori(1, NE - 1) as n:
                    silu_a(act, n)
                    cols_a(act, n + 1)
                    out_a(act, n, n * P)
                silu_a(act, NE - 1)
                out_a(act, NE - 1, (NE - 1) * P)

                def body(q, n):
                    cols_a(act, n)
                    silu_a(act, n)
                    out_a(act, n, n * P)
                    act.wait_ge(m_st, 16 * (n + 1))
                act.wait_ge(m_st, 16 * NE)
                act.wait_ge(z_in, 16 * NOVER)
                over(act, body)

            def ex_dve(dve, ch):
                onehot(dve, 0, 0)
                cols_v(dve, 0)
                onehot(dve, 1, 1)
                gated_v(dve, 0)
                cols_v(dve, 1)
                onehot(dve, 2, 2)
                out_v(dve, 0)
                with dve.Fori(1, NE - 2) as n:
                    gated_v(dve, n)
                    cols_v(dve, n + 1)
                    onehot(dve, n + 2, n + 2)
                    out_v(dve, n)
                gated_v(dve, NE - 2)
                cols_v(dve, NE - 1)
                out_v(dve, NE - 2)
                gated_v(dve, NE - 1)
                out_v(dve, NE - 1)

                def body(q, n):
                    e = expert_of(dve, q)
                    dve.tensor_scalar(rkq, RK[:, :, bass.ds(e, 1)], vsh[:, q:q + 1], None,
                                      ALU.subtract).then_inc(m_rk, 1)
                    dve.wait_ge(m_rk, q + 1)
                    dve.tensor_tensor(OH, rank1[:, :].rearrange("p (o c) -> p o c", o=1).to_broadcast([P, NT, P]),
                                      rkq.to_broadcast([P, NT, P]), ALU.is_equal).then_inc(m_oh, 1)
                    cols_v(dve, n)
                    gated_v(dve, n)
                    out_v(dve, n)
                over(dve, body)
            stage(ex_pe, ex_act, ex_dve)

            gbuf = area(0, 0, 4, D)
            fsq = area(0, 4 * D, D)
            ss5, rs5, u5 = use(ssd, NT), use(rsd, NT), use(xsd, NT)

            def fin_po(po, ch):
                for t in range(NT):
                    for k in range(2):
                        if t >= 2:
                            po.wait_ge(g_use, 2 * (t - 2) + k + 1)
                        j = 2 * (t % 2) + k
                        po.indirect_dma_start(
                            out=gbuf[:, j, :], out_offset=None, in_=obuf,
                            in_offset=bass.IndirectOffsetOnAxis(ap=rowu[:, k * NT + t:k * NT + t + 1], axis=0),
                        ).then_inc(g_in[j], 16)
                for t in range(NT):
                    po.wait_ge(ssd, ss5 + t + 1)
                    v = ss[:, t:t + 1]
                    ch(po.tensor_scalar(v, v, 1.0 / D, EPS, ALU.mult, ALU.add))
                    po.tensor_tensor(v, v, nhalf[:, :], ALU.pow).then_inc(rsd, 1)

            def fin_dve(dve, ch):
                for t in range(NT):
                    for k in range(2):
                        j = 2 * (t % 2) + k
                        dve.wait_ge(g_in[j], 16 * (t // 2 + 1))
                        if k:
                            dve.wait_ge(g_use, 2 * t + 1)
                        dve.scalar_tensor_tensor(out=x[:, t, :], in0=gbuf[:, j, :], scalar=gate[:, k, t:t + 1],
                                                 in1=x[:, t, :], op0=ALU.mult, op1=ALU.add).then_inc(g_use, 1)
                dve.wait_ge(*gfin_in)
                for t in range(NT):
                    dve.wait_ge(rsd, rs5 + t + 1)
                    dve.scalar_tensor_tensor(out=x[:, t, :], in0=x[:, t, :], scalar=ss[:, t:t + 1], in1=gfin,
                                             op0=ALU.mult, op1=ALU.mult).then_inc(xsd, 1)

            def fin_act(act, ch):
                for t in range(NT):
                    act.wait_ge(g_use, 2 * t + 2)
                    if t:
                        act.wait_ge(ssd, ss5 + t)
                    act.activation(fsq, x[:, t, :], ACT.Square, accum_out=ss[:, t:t + 1]).then_inc(ssd, 1)
            last_x = (xsd, u5)
            last_stage = len(stages)
            stage(None, fin_act, fin_dve, fin_po)

        block = ctx.enter_context(nc.Block())

        def run(eng, which, chain):
            ch = Chain(eng, chain)
            for n, st_ in enumerate(stages):
                if which == 3:
                    for at, dst, src, s in late:
                        if at == n:
                            eng.dma_start(dst, src).then_inc(s, 16)
                if st_[which]:
                    st_[which](eng, ch)
                eng.drain().then_inc(phase, 1)
                eng.wait_ge(phase, 4 * (n + 1))

        @block.tensor
        def _(pe):
            run(pe, 0, phase)

        @block.scalar
        def _(act):
            run(act, 1, ach)

        @block.vector
        def _(dve):
            run(dve, 2, vch)

        @block.gpsimd
        def _(po):
            run(po, 3, pch)

        @block.sync
        def _(sp):
            for dst, src in crows:
                sp.dma_start(dst, src).then_inc(cst, 16)
            with nc.allow_non_contiguous_dma(reason="512 positions, once"):
                sp.dma_start(posi[:, :].rearrange("p (t a) -> p t a", a=1),
                             I["positions"][0].rearrange("(t p a) -> p t a", p=P, a=1)).then_inc(cst, 16)
            sp.dma_start(x[:, :, :], I["x"][0].rearrange("(t p) d -> p t d", p=P)).then_inc(xin, 16)
            for c, (loads, kt, n, _) in enumerate(chunks):
                if c >= NS:
                    sp.wait_ge(mm, chunks[c - NS][3])
                v = ring[c % NS][:, :kt * n].rearrange("p (k c) -> p k c", c=n)
                for src, c0 in loads:
                    with nc.allow_non_contiguous_dma(reason="narrow weights: gates and router"):
                        sp.dma_start(v[:, :, c0:c0 + src.shape[2]], src).then_inc(w_full[c % NS], 16)
            if on(7):
                def load(e, par):
                    for j, name in enumerate(("w1_2", "w3_2", "w2_2")):
                        v = (w2v if j == 2 else w1v)(3 * par + j)
                        src = I[name][0, bass.ds(e, 1)].rearrange("o (k p) c -> p (o k) c", p=P)
                        sp.dma_start(v, src).then_inc(w_moe[3 * par + j], 16)
                sp.wait_ge(mm, chunks[-1][3])
                sp.wait_ge(phase, 4 * moe_bar)
                load(0, 0)
                load(1, 1)
                with sp.Fori(1, NE // 2) as i:
                    for par in range(2):
                        sp.wait_ge(m_dn, i * 2 + (par - 1))
                        load(i * 2 + par, par)
                sp.wait_ge(phase, 4 * (moe_bar + 1))
                n_over = sp.value_load(ft[0:1, 0:1], min_val=0, max_val=NOVER)
                for q in range(NOVER):
                    with sp.If(n_over > q):
                        sp.wait_ge(m_dn, NE + q)
                        load(expert_of(sp, q), 0)
                for t in range(NT):
                    sp.wait_ge(xsd, last_x[1] + t + 1)
                    sp.dma_start(out[0, t * P:(t + 1) * P, :], x[:, t, :]).then_inc(out_s, 16)
            else:
                sp.wait_ge(phase, 4 * len(stages))
                for t in range(NT):
                    sp.dma_start(out[0, t * P:(t + 1) * P, :], x[:, t, :]).then_inc(out_s, 16)
            sp.wait_ge(out_s, 16 * NT)


_INS = [
    "x", "positions", "l0_attn_norm", "l0_w_in", "l0_mla_q_a_norm", "l0_mla_w_q_up", "l0_mla_kv_a_norm",
    "l0_mla_w_kv_up", "l0_mla_q_norm", "l0_mla_k_norm", "l0_w_o", "l0_ffn_norm", "l0_w_gate", "l0_w_up",
    "l0_w_down", "l1_attn_norm", "l1_w_in", "l1_fox_f_bias", "l1_fox_q_norm", "l1_fox_k_norm", "l1_w_o",
    "l1_ffn_norm", "l1_w_gate", "l1_w_up", "l1_w_down", "mem_2", "norm_mix_g_2", "w_in_2", "b_gate_2", "b_if_2",
    "conv_w_2", "conv_b_2", "mh_norm_g_2", "sgu_norm_g_2", "w_s_2", "b_s_2", "w_out_2", "norm_x_g_2",
    "norm_mem_g_2", "w_xq_2", "w_xkv_2", "w_xo_2", "norm_moe_g_2", "w_rg_2", "b_rg_2", "w_re_2", "b_re_2", "w1_2",
    "w3_2", "w2_2", "norm_f_g_2",
]


def kernel(**inputs):
    import numpy as _np
    import concourse.bacc as _bacc
    from concourse import mybir as _mybir
    from concourse.bass_utils import run_bass_kernel_spmd as _run

    nc = _bacc.Bacc("TRN2", target_bir_lowering=False, num_devices=1)
    arrays, aps = {}, {}
    for name in _INS:
        a = _np.ascontiguousarray(inputs[name])
        arrays[f"in_{name}"] = a
        aps[name] = nc.dram_tensor(f"in_{name}", a.shape, _mybir.dt.from_np(a.dtype), kind="ExternalInput").ap()
    out = nc.dram_tensor("out", (1, S, D), _mybir.dt.float32, kind="ExternalOutput").ap()
    bass_two_blocks_kernel(nc, aps, out)
    r = _run(nc, [arrays], core_ids=[0])
    return r.results[0]["out"]
```

```python
from contextlib import ExitStack

import numpy as np

import concourse.bass as bass
from concourse import mybir

F32 = mybir.dt.float32
I32 = mybir.dt.int32
F32R = mybir.dt.float32r
U32 = mybir.dt.uint32
ALU = mybir.AluOpType
ACT = mybir.ActivationFunctionType
AX = mybir.AxisListType.X

P = 128
S = 512
NT = S // P
D = 1024
KD = D // P
EPS = 1e-6
NEG = -1e30
BANK = 512
NBANK = 8
SLOT = 4096
NS = 3
PIECE = 2048
NSM = 6
QR, KVR, RO, NOPE, MV = 256, 128, 32, 64, 64
QK = NOPE + RO
MH = 8
HALF = RO // 2
C0 = QR + KVR + RO
SBW = 512
FF = 2816
FT = FF // P
FC = FF // 256
FH = 16
LH = 4
DH = 256
NM = 256
MT = NM // P
G8 = 8
NE = 32
NGR = 4
EPG = NE // NGR
EF = 512
NOVER = 7

START, END = 1, 7


class Pair:

    def __init__(self, high, low):
        self.h, self.l, self.high_f = high, low, high.bitcast(F32)

    def __getitem__(self, at):
        return Pair(self.h[at], self.l[at])


class Chain:

    def __init__(self, eng, sem):
        self.eng, self.sem, self.n = eng, sem, 0

    def mark(self, ins):
        self.n += 1
        ins.then_inc(self.sem, 1)

    def wait(self):
        self.eng.wait_ge(self.sem, self.n)

    def __call__(self, ins):
        self.mark(ins)
        self.wait()


def two_pi():
    c1 = 201.0 / 32.0
    c2 = float(np.round((2.0 * np.pi - c1) * 2.0**20) / 2.0**20)
    return c1, c2, float(np.float32(2.0 * np.pi - c1 - c2))


def bass_two_blocks_kernel(nc, I, out):
    def on(n):
        return START <= n <= END

    ctx = ExitStack()

    def sb(name, shape, dt=F32):
        return ctx.enter_context(nc.sbuf_tensor(name, shape, dt))

    def sem(name):
        return ctx.enter_context(nc.semaphore(name))

    with ctx:
        x = sb("x", [P, NT, D])
        def sb_twice(name, shape):
            plain = sb(name, shape)
            at = nc.sbuf_base - 4 * int(np.prod(shape[1:]))
            return plain, nc.alloc_sbuf_tensor_at(name + "_parts", shape, F32R, offset=at)

        actT, actR = sb_twice("actT", [P, KD, S])
        orow = actT[:, :, :].rearrange("p (t a) s -> p t (a s)", t=NT)
        ident = sb("ident", [P, P])
        tri = sb("tri", [P, P])
        ones = sb("ones", [P, P])
        maskz = sb("maskz", [P, S])
        rank1 = sb("rank1", [P, P])
        gains = sb("gains", [P, 64])
        cols2 = sb("cols2", [P, 96])
        nhalf = sb("nhalf", [P, 1])
        desc = sb("desc", [P, NE])
        eidx = sb("eidx", [P, NE])
        ss = sb("ss", [P, 8])
        rs = sb("rs", [P, 8])
        mx = sb("mx", [P, 8])
        bi = sb("bi", [P, 8])
        rinv = sb("rinv", [P, 8])
        em = sb("em", [P, 8])
        ffb = sb("ffb", [P, FH])
        bif = sb("bif", [P, 8])
        rbias = sb("rbias", [P, NGR + NE])
        qg = sb("qg", [P, 2, QK])
        ropec = sb("ropec", [P, NT, HALF])
        ropes = sb("ropes", [P, NT, HALF])
        posi = sb("posi", [P, NT], I32)
        CS = sb("CS", [P, NT, FH])
        FG = sb("FG", [P, 2, NT, FH])
        st = sb("st", [P, 128])
        ft = sb("ft", [1, 16], I32)
        free = (nc.sbuf_bytes_remaining // 4 - 64) // 64 * 64
        sb("arena", [P, free])
        arena = nc.sbuf_base - 4 * free
        placed = {}

        def area(base, off, *shape, dt=F32):
            n = int(np.prod(shape))
            assert base + off + n <= free, (off, n, free - base)
            at = (base + off, n, dt == F32R)
            if at not in placed:
                placed[at] = nc.alloc_sbuf_tensor_at(f"area{len(placed)}", [P, n], dt, offset=arena + 4 * (base + off))
            v = placed[at][:, :]
            if len(shape) == 2:
                v = v.rearrange("p (a b) -> p a b", b=shape[1])
            if len(shape) == 3:
                v = v.rearrange("p (a b c) -> p a b c", b=shape[1], c=shape[2])
            return v

        ring = [area(0, i * SLOT, SLOT) for i in range(NSM)]

        def work(off, *shape):
            return area(NS * SLOT, off, *shape)

        def parts(high, low, *shape):
            return Pair(*(area(NS * SLOT, off, *shape, dt=F32R) for off in (high, low)))

        def act_parts(low):
            return Pair(actR[:, :, :], area(NS * SLOT, low, KD, S, dt=F32R))

        def moe(off, *shape):
            return area(NSM * SLOT, off, *shape)

        ps = ctx.enter_context(nc.psum_tensor("ps", [P, NBANK, BANK], F32))
        G_A0, G_F0, G_A1, G_F1, G_MIX, G_X, G_MEM, G_MOE = range(8)
        norm_names = ["l0_attn_norm", "l0_ffn_norm", "l1_attn_norm", "l1_ffn_norm",
                      "norm_mix_g_2", "norm_x_g_2", "norm_mem_g_2", "norm_moe_g_2"]
        CW, CB, QA, BS, FQ, FK = 0, 64, 80, 83, 91, 92

        w_full = [sem(f"w_full{i}") for i in range(NS)]
        w_moe = [sem(f"w_moe{i}") for i in range(NSM)]
        mm = sem("mm")
        tr = sem("tr")
        ea = sem("ea")
        ev = sem("ev")
        mida = sem("mida")
        midv = sem("midv")
        ssd = sem("ssd")
        rsd = sem("rsd")
        xsd = sem("xsd")
        phase = sem("phase")
        vch, ach, pch = sem("vch"), sem("ach"), sem("pch")
        cst = sem("cst")
        xin = sem("xin")
        w_hi, w_lo = sem("w_hi"), sem("w_lo")
        pu = sem("pu")
        s_sc, s_mx, s_ex = sem("s_sc"), sem("s_mx"), sem("s_ex")
        s_pt, s_pe = sem("s_pt"), sem("s_pe")
        s_o, s_on = sem("s_o"), sem("s_on")
        s_pr, s_pre = sem("s_pr"), sem("s_pre")
        s_t1, s_sp, s_m1, s_w, s_m2 = sem("s_t1"), sem("s_sp"), sem("s_m1"), sem("s_w"), sem("s_m2")
        out_s = sem("out_s")
        m_oh, m_gx, m_gxa, m_gxv = sem("m_oh"), sem("m_gx"), sem("m_gxa"), sem("m_gxv")
        m_up, m_si, m_hb, m_tr, m_hT = sem("m_up"), sem("m_si"), sem("m_hb"), sem("m_tr"), sem("m_hT")
        m_dn, m_oa, m_ov, m_st = sem("m_dn"), sem("m_oa"), sem("m_ov"), sem("m_st")
        g_in = [sem(f"g_in{j}") for j in range(4)]
        g_use = sem("g_use")

        if on(7):
            obuf = nc.dram_tensor("expert_rows", [(NE + NOVER) * P, D], F32, kind="Internal").ap()

        counts = {}

        def use(s, n):
            b = counts.get(s.name, 0)
            counts[s.name] = b + n
            return b

        stages = []

        def stage(pe=None, act=None, dve=None, po=None):
            stages.append((pe, act, dve, po))

        chunks = []
        loads_at = [0] * NS
        pieces = []

        def kpc(w):
            return w.rearrange("(k p) c -> p k c", p=P)

        class Weights:

            def __init__(self, loads, kt, n, runs, last=True):
                slot = len(chunks) % NS
                loads_at[slot] += len(loads)
                self.runs, self.last, self.m0 = runs, last, use(mm, runs if last else 0)
                raw = ring[slot][:, :kt * n].rearrange("p (k c) -> p k c", c=n)
                count = -(-kt * n // PIECE)
                step = -(-kt // count)
                self.cuts = [(k, min(kt, k + step)) for k in range(0, kt, step)]
                self.at = len(pieces)
                self.begun = 0
                for i, (k0, k1) in enumerate(self.cuts):
                    b = len(pieces) % 2
                    used = (mm, self.m0 + runs) if last and i == len(self.cuts) - 1 else (pu, use(pu, 1) + 1)
                    pieces.append((raw[:, k0:k1, :], (w_full[slot], 16 * loads_at[slot]),
                                   parts(2 * b * PIECE, (2 * b + 1) * PIECE, k1 - k0, n), used))
                chunks.append((loads, kt, n, len(pieces)))

            def product(self, pe, operands, dst, free):
                for i, (k0, k1) in enumerate(self.cuts):
                    pe.wait_ge(w_lo, self.at + i + 1)
                    for r in range(self.runs):
                        if free and i == 0:
                            free(r)
                        for k in range(k0, k1):
                            a, b = operands(r, pieces[self.at + i][2], k - k0, k)
                            begin = free is not None and k == 0
                            end = self.last and k == self.cuts[-1][1] - 1
                            pe.matmul(dst(r), a.h, b.h, start=begin, stop=False)
                            pe.matmul(dst(r), a.l, b.h, start=False, stop=False)
                            m = pe.matmul(dst(r), a.h, b.l, start=False, stop=end)
                        if self.last and i == len(self.cuts) - 1:
                            m.then_inc(mm, 1)
                        elif r == self.runs - 1:
                            m.then_inc(pu, 1)

        def high(eng, p):
            raw, full, w, _ = pieces[p]
            eng.wait_ge(*full)
            if p >= 2:
                eng.wait_ge(*pieces[p - 2][3])
            if eng is nc.vector:
                eng.tensor_copy(w.h, raw).then_inc(w_hi, 1)
            else:
                eng.activation(w.h, raw, ACT.Copy).then_inc(w_hi, 1)

        def low(dve, p):
            raw, _, w, _ = pieces[p]
            dve.wait_ge(w_hi, p + 1)
            dve.tensor_tensor(w.l, raw, w.high_f, ALU.subtract).then_inc(w_lo, 1)

        class Split:

            def __init__(self, jobs):
                self.w = [job.w for job in jobs]

            def pieces(self, j, lo, hi):
                if j < len(self.w):
                    n = len(self.w[j].cuts)
                    yield from range(self.w[j].at + max(lo, self.w[j].begun), self.w[j].at + min(hi, n))

            def start(self, eng):
                self.do(eng, self.pieces(0, 0, 99))

            def before(self, eng, j):
                self.do(eng, self.pieces(j + 1, 0, 1))

            def after(self, eng, j):
                self.do(eng, self.pieces(j + 1, 1, 99))

            def do(self, eng, which):
                for p in which:
                    if eng is nc.vector:
                        low(eng, p)
                    else:
                        high(eng, p)

        def ahead(early, w):
            early.append(w)
            w.begun = 1

        def begin(dve, early):
            for w in early:
                high(dve, w.at)
                low(dve, w.at)

        class Groups:

            def __init__(self, n, who):
                self.who = [who[g % len(who)] for g in range(n)]
                sems = {"A": ea, "V": ev, "C": midv}
                base = {k: use(s, self.who.count(k)) for k, s in sems.items()}
                base["X"], sems["X"] = 0, None
                self.freed = []
                for k in self.who:
                    base[k] += 1
                    self.freed.append((sems[k], base[k]))

            def bank(self, g):
                return g % NBANK

            def wait_free(self, eng, g):
                if g >= NBANK:
                    eng.wait_ge(*self.freed[g - NBANK])

            def wait_taken(self, eng, g):
                eng.wait_ge(*self.freed[g])

        def norm_stage(src, dst, gain, tiles, buf, early=()):
            xs = buf[:, 0:2 * D].rearrange("p (a b) -> p a b", b=D)
            junk = buf[:, 2 * D:3 * D]
            tmp = buf[:, 3 * D:4 * D].rearrange("p (a k s) -> p a k s", a=2, k=4)
            ss0, rs0, xs0, tr0 = use(ssd, tiles), use(rsd, tiles), use(xsd, tiles), use(tr, 2 * tiles)
            gr = Groups(2 * tiles, "V")
            hi0, lo0 = use(ea, 2 * tiles), use(midv, 2 * tiles)

            def place(g):
                t, h = divmod(g, 2)
                return slice(None), slice(4 * h, 4 * h + 4), slice(t * P, t * P + P)

            def act(act, ch):
                for t in range(tiles):
                    if t:
                        act.wait_ge(ssd, ss0 + t)
                    act.activation(junk, src[:, t, :], ACT.Square, accum_out=ss[:, t:t + 1]).then_inc(ssd, 1)

                def highs(t):
                    for g in (2 * t, 2 * t + 1):
                        act.wait_ge(ev, gr.freed[g][1])
                        act.activation(dst[place(g)].h, tmp[:, g % 2], ACT.Copy).then_inc(ea, 1)
                for t in range(tiles):
                    act.wait_ge(rsd, rs0 + t + 1)
                    if t >= 2:
                        act.wait_ge(tr, tr0 + 2 * (t - 1))
                    act.mul(xs[:, t % 2, :], src[:, t, :], ss[:, t:t + 1]).then_inc(xsd, 1)
                    if t:
                        highs(t - 1)
                highs(tiles - 1)

            def po(po, ch):
                for t in range(tiles):
                    po.wait_ge(ssd, ss0 + t + 1)
                    v = ss[:, t:t + 1]
                    ch(po.tensor_scalar(v, v, 1.0 / D, EPS, ALU.mult, ALU.add))
                    po.tensor_tensor(v, v, nhalf[:, :], ALU.pow).then_inc(rsd, 1)

            def pe(pe, ch):
                for t in range(tiles):
                    pe.wait_ge(xsd, xs0 + t + 1)
                    for h in range(2):
                        g = 2 * t + h
                        gr.wait_free(pe, g)
                        for j in range(4):
                            m = pe.transpose(ps[:, gr.bank(g), j * P:j * P + P],
                                             xs[:, t % 2, (4 * h + j) * P:(4 * h + j + 1) * P], ident[:, :])
                        m.then_inc(tr, 1)

            def dve(dve, ch):
                begin(dve, early)
                for g in range(2 * tiles + 1):
                    if g < 2 * tiles:
                        h = g % 2
                        dve.wait_ge(tr, tr0 + g + 1)
                        if g >= 2:
                            dve.wait_ge(midv, lo0 + g - 1)
                        dve.tensor_tensor(tmp[:, g % 2], ps[:, gr.bank(g), :].rearrange("p (k s) -> p k s", k=4),
                                          gains[:, 8 * gain + 4 * h:8 * gain + 4 * h + 4].rearrange(
                                              "p (k o) -> p k o", o=1).to_broadcast([P, 4, P]),
                                          ALU.mult).then_inc(ev, 1)
                    if g:
                        q = g - 1
                        dve.wait_ge(ea, hi0 + q + 1)
                        dve.wait_ge(ev, gr.freed[q][1])
                        d = dst[place(q)]
                        dve.tensor_tensor(d.l, tmp[:, q % 2], d.high_f, ALU.subtract).then_inc(midv, 1)
            stage(pe, act, dve, po)

        class Rows:

            def __init__(self, gr, g0, lhs, tiles, loads, n, kt=KD, blocks=1, more=False, past=False):
                self.gr, self.g0, self.lhs, self.tiles, self.n, self.blocks, self.past = (
                    gr, g0, lhs, tiles, n, blocks, past)
                self.w = Weights(loads, kt, n * blocks, tiles * blocks, last=not more)

            def operands(self, r, w, i, k):
                t, h = divmod(r, self.blocks)
                return self.lhs[:, k, t * P:t * P + P], w[:, i, h * self.n:(h + 1) * self.n]

            def pe(self, pe):
                self.w.product(pe, self.operands, self.src,
                               None if self.past else lambda r: self.gr.wait_free(pe, self.g0 + r))

            def ready(self, eng, r):
                eng.wait_ge(mm, self.w.m0 + r + 1)

            def src(self, r):
                return ps[:, self.gr.bank(self.g0 + r), 0:self.n]

        class Cols(Rows):

            def __init__(self, gr, g0, rhs, n, loads, cols=(0, 128, 256, 384)):
                self.gr, self.g0, self.rhs, self.n, self.tiles, self.past, self.cols = gr, g0, rhs, n, 4, False, cols
                self.w = Weights(loads, KD, 512, 4)

            def operands(self, r, w, i, k):
                return w[:, i, self.cols[r]:self.cols[r] + P], self.rhs[:, k, :]

        def take_act(act, src, dst, scale=1.0):
            act.activation(dst, src, ACT.Copy, scale=scale).then_inc(ea, 1)

        def take_dve(dve, src, dst):
            dve.tensor_copy(dst, src).then_inc(ev, 1)

        def plain_stage(jobs, gr):
            sp_ = Split([job for job, _, _ in jobs])

            def pe(pe, ch):
                for job, _, _ in jobs:
                    job.pe(pe)

            def moves(eng, who):
                sp_.start(eng)
                for j, (job, dst, scale) in enumerate(jobs):
                    sp_.before(eng, j)
                    for r in range(job.tiles):
                        if gr.who[job.g0 + r] == who:
                            job.ready(eng, r)
                            if who == "A":
                                take_act(eng, job.src(r), dst(r), scale)
                            else:
                                eng.tensor_scalar(dst(r), job.src(r), scale, None, ALU.mult).then_inc(ev, 1)
                    sp_.after(eng, j)
            stage(pe, lambda act, ch: moves(act, "A"), lambda dve, ch: moves(dve, "V"))

        def out_stage(src, wts):
            oT = parts(A0, A0 + 4096, KD, S)
            gt = Groups(8, "V")
            tr0, hi0 = use(tr, 8), use(ea, 8)
            gr = Groups(8, "V")
            jobs = [Rows(gr, 4 * c, oT, NT, [(kpc(wts[:, c * 512:c * 512 + 512]), 0)], 512) for c in range(2)]
            early = []
            ahead(early, jobs[0].w)
            sp_ = Split(jobs)

            def place(g):
                t, h = divmod(g, 2)
                return slice(None), slice(4 * h, 4 * h + 4), slice(t * P, t * P + P)

            def pe(pe, ch):
                for g in range(8):
                    t, h = divmod(g, 2)
                    for j in range(4):
                        m = pe.transpose(ps[:, g, j * P:j * P + P],
                                         src[:, t, (4 * h + j) * P:(4 * h + j + 1) * P], ident[:, :])
                    m.then_inc(tr, 1)

            def act(act, ch):
                for g in range(8):
                    act.wait_ge(tr, tr0 + g + 1)
                    act.activation(oT[place(g)].h, ps[:, g, :].rearrange("p (k s) -> p k s", k=4),
                                   ACT.Copy).then_inc(ea, 1)

            def dve(dve, ch):
                begin(dve, early)
                for g in range(8):
                    dve.wait_ge(ea, hi0 + g + 1)
                    d = oT[place(g)]
                    dve.tensor_tensor(d.l, ps[:, g, :].rearrange("p (k s) -> p k s", k=4), d.high_f,
                                      ALU.subtract).then_inc(ev, 1)
            stage(pe, act, dve)

            def pe2(pe, ch):
                for job in jobs:
                    job.pe(pe)

            def act2(act, ch):
                sp_.start(act)
                for c in range(2):
                    sp_.before(act, c)
                    sp_.after(act, c)

            def dve2(dve, ch):
                sp_.start(dve)
                for c, job in enumerate(jobs):
                    sp_.before(dve, c)
                    for t in range(NT):
                        job.ready(dve, t)
                        xx = x[:, t, c * 512:c * 512 + 512]
                        dve.tensor_tensor(xx, xx, job.src(t), ALU.add).then_inc(ev, 1)
                    sp_.after(dve, c)
            stage(pe2, act2, dve2)

        def ffn(gain, wg, wu, wd):
            runs = ((0, 6), (6, 11))
            low_x = act_parts(A0)
            gu = parts(A0 + 4096, A0 + 4096 + 12 * S, 12, S)
            sil = work(A0 + 4096 + 24 * S, 4, S)
            early = []
            norm_stage(x, low_x, gain, NT, work(A0 + 4096, 4 * D), early)
            gr = Groups(2 * FT + 16, "V")
            jobs, g = [], 0
            for c0, c1 in runs:
                for c in range(c0, c1):
                    jobs.append((Cols(gr, g, low_x, S, [(kpc(wg[:, 256 * c:256 * c + 256]), 0),
                                                        (kpc(wu[:, 256 * c:256 * c + 256]), 256)],
                                      (0, 256, 128, 384)), "up", 2 * c))
                    g += 4
                k0, k1 = 2 * c0, 2 * c1
                mid = (k0 + k1 + 1) // 2
                for h in range(2):
                    for a, b in ((k0, mid), (mid, k1)):
                        jobs.append((Rows(gr, g, gu[:, a - k0:, :], NT,
                                          [(kpc(wd[a * P:b * P, h * 512:h * 512 + 512]), 0)], 512, b - a,
                                          more=b < k1, past=a > k0), "down" if b == k1 else "more", h))
                    g += 4
            ahead(early, jobs[0][0].w)
            sp_ = Split([job for job, _, _ in jobs])
            si0 = use(mida, FT)
            first = [0, runs[1][0] * 2]

            def pe(pe, ch):
                last = None
                for job, kind, _ in jobs:
                    if kind == "more" and last != "down":
                        gr.wait_taken(pe, job.g0 - 1)
                    job.pe(pe)
                    last = kind

            def act(act, ch):
                sp_.start(act)
                for j, (job, kind, f0) in enumerate(jobs):
                    sp_.before(act, j)
                    if kind == "up":
                        for q in range(2):
                            f = f0 + q
                            job.ready(act, 2 * q)
                            if f >= 4:
                                act.wait_ge(*(sil_used[f - 4]))
                            act.activation(sil[:, f % 4, :], job.src(2 * q), ACT.Silu).then_inc(mida, 1)
                    sp_.after(act, j)
            sil_used = {}
            for job, kind, f0 in jobs:
                if kind == "up":
                    for q in range(2):
                        sil_used[f0 + q] = gr.freed[job.g0 + 2 * q + 1]

            def dve(dve, ch):
                sp_.start(dve)
                for j, (job, kind, f0) in enumerate(jobs):
                    sp_.before(dve, j)
                    if kind == "up":
                        for q in range(2):
                            f = f0 + q
                            d = gu[:, f - first[f >= first[1]], :]
                            s_ = sil[:, f % 4, :]
                            job.ready(dve, 2 * q + 1)
                            dve.wait_ge(mida, si0 + f + 1)
                            ch(dve.tensor_tensor(s_, s_, job.src(2 * q + 1), ALU.mult))
                            ch(dve.tensor_copy(d.h, s_))
                            dve.tensor_tensor(d.l, s_, d.high_f, ALU.subtract).then_inc(ev, 2)
                    elif kind == "down":
                        for t in range(NT):
                            job.ready(dve, t)
                            xx = x[:, t, f0 * 512:f0 * 512 + 512]
                            dve.tensor_tensor(xx, xx, job.src(t), ALU.add).then_inc(ev, 1)
                    sp_.after(dve, j)
            stage(pe, act, dve)

        Pb = work(0, 4, 512)
        PT = work(2048, 2, 512)
        A0 = 4 * PIECE

        def causal(v):
            return (v % NT + 1) * P

        def value_bank(u, dv):
            return ps[:, 5 + u % 2, 0:dv]

        def col(v, u):
            return v[:, u % 8:u % 8 + 1]

        def attention(units, length, scores, values, dv, dst, scale, preps=(), fox=False, mlstm=None):
            sc0, mx0, ex0, pt0, pe0, o0, on0 = (use(s, units) for s in (s_sc, s_mx, s_ex, s_pt, s_pe, s_o, s_on))
            npr = units // NT if mlstm else len(preps)
            pr0, pre0 = use(s_pr, npr), use(s_pre, npr)
            t10, t2 = (use(s_t1, units), use(mida, units)) if mlstm else (0, 0)
            exponents, E = mlstm or (None, None)

            def pe(pe, ch):
                for v in range(units + 3):
                    for n, (at, _, blocks, _, _) in enumerate(preps):
                        if at == v:
                            if n:
                                pe.wait_ge(s_pre, pre0 + n)
                            for t, b in enumerate(blocks):
                                m = pe.transpose(ps[0:b.shape[1], 7, t * P:t * P + P], b, ident[:, :])
                            m.then_inc(s_pr, 1)
                    if mlstm and v < units and v % NT == 0:
                        if v:
                            pe.wait_ge(s_mx, mx0 + v)
                        exponents(pe, v // NT).then_inc(s_pr, 1)
                    if v < units:
                        if v >= 3:
                            pe.wait_ge(s_ex, ex0 + v - 2)
                        scores(pe, v, v % 3, pre0).then_inc(s_sc, 1)
                    if 2 <= v < units + 2:
                        u = v - 2
                        pe.wait_ge(s_ex, ex0 + u + 1)
                        if u >= 2:
                            pe.wait_ge(s_pe, pe0 + u - 1)
                        for j in range(length(u) // P):
                            m = pe.transpose(ps[:, 3 + u % 2, j * P:j * P + P],
                                             Pb[:, u % 4, j * P:j * P + P], ident[:, :])
                        m.then_inc(s_pt, 1)
                    if v >= 3:
                        u = v - 3
                        pe.wait_ge(s_pe, pe0 + u + 1)
                        if u >= 2:
                            pe.wait_ge(s_on, on0 + u - 1)
                        nb = length(u) // P
                        for j in range(nb):
                            m = pe.matmul(value_bank(u, dv), PT[:, u % 2, j * P:j * P + P], values(u, j),
                                          start=(j == 0), stop=(j == nb - 1))
                        m.then_inc(s_o, 1)

            def act(act, ch):
                for v in range(units + 2):
                    if v >= 2:
                        u = v - 2
                        act.wait_ge(s_pt, pt0 + u + 1)
                        if u >= 2:
                            act.wait_ge(s_o, o0 + u - 1)
                        L = length(u)
                        act.activation(PT[:, u % 2, 0:L], ps[:, 3 + u % 2, 0:L], ACT.Copy).then_inc(s_pe, 1)
                    for n, (at, done, _, d, gain) in enumerate(preps):
                        if at == v:
                            act.wait_ge(s_pr, pr0 + n + 1)
                            if done:
                                act.wait_ge(s_sc, sc0 + done)
                            act.activation(d, ps[0:d.shape[0], 7, :], ACT.Copy, scale=gain).then_inc(s_pre, 1)
                    if v < units:
                        L = length(v)
                        act.wait_ge(s_mx, mx0 + v + 1)
                        b = col(bi, v)
                        if mlstm:
                            e = E[:, v % 4, 0:L]
                            act.activation(e, e, ACT.Exp, bias=b).then_inc(s_t1, 1)
                            if v >= 8:
                                act.wait_ge(s_on, on0 + v - 7)
                            h, i = divmod(v, NT)
                            act.activation(col(em, v), b, ACT.Exp, bias=CS[:, i, h:h + 1]).then_inc(mida, 1)
                        else:
                            if v >= 4:
                                act.wait_ge(s_pt, pt0 + v - 3)
                            if v >= 8:
                                act.wait_ge(s_on, on0 + v - 7)
                            act.activation(Pb[:, v % 4, 0:L], ps[:, v % 3, 0:L], ACT.Exp, bias=b, scale=scale,
                                           accum_out=col(rs, v)).then_inc(s_ex, 1)

            def dve(dve, ch):
                for v in range(units + 4):
                    if v < units:
                        L = length(v)
                        h, i = divmod(v, NT)
                        m1, b, bank = col(mx, v), col(bi, v), ps[:, v % 3, 0:L]
                        if mlstm:
                            dve.wait_ge(s_pr, pr0 + h + 1)
                            if v >= 4:
                                dve.wait_ge(s_ex, ex0 + v - 3)
                            ch(dve.tensor_tensor_reduce(E[:, v % 4, 0:L], ps[:, 7, 0:L], maskz[:, S - L:S], 1.0, -3e38,
                                                        ALU.add, ALU.max, m1))
                            if v >= 8:
                                dve.wait_ge(mida, t2 + v - 7)
                            dve.tensor_scalar(b, m1, 0.0, -1.0, ALU.max, ALU.mult).then_inc(s_mx, 1)
                        else:
                            dve.wait_ge(s_sc, sc0 + v + 1)
                            if length is causal:
                                ch(dve.tensor_tensor_reduce(bank, bank, maskz[:, S - L:S], 1.0, -3e38,
                                                            ALU.add, ALU.max, m1))
                            else:
                                ch(dve.tensor_reduce(m1, bank, AX, ALU.max))
                            if v >= 8:
                                dve.wait_ge(s_ex, ex0 + v - 7)
                            if fox:
                                ch(dve.tensor_scalar(m1, m1, scale, CS[:, i, h:h + 1], ALU.mult, ALU.subtract))
                                dve.tensor_scalar(b, m1, -1.0, CS[:, i, h:h + 1], ALU.mult,
                                                  ALU.subtract).then_inc(s_mx, 1)
                            else:
                                dve.tensor_scalar(b, m1, -scale, None, ALU.mult).then_inc(s_mx, 1)
                    if mlstm and 1 <= v <= units:
                        u = v - 1
                        L = length(u)
                        dve.wait_ge(s_sc, sc0 + u + 1)
                        dve.wait_ge(s_t1, t10 + u + 1)
                        if u >= 4:
                            dve.wait_ge(s_pt, pt0 + u - 3)
                        dve.tensor_tensor_reduce(Pb[:, u % 4, 0:L], ps[:, u % 3, 0:L], E[:, u % 4, 0:L],
                                                 DH ** -0.5, 0.0, ALU.mult, ALU.add, col(rs, u)).then_inc(s_ex, 1)
                    if v >= 4:
                        u = v - 4
                        h, i = divmod(u, NT)
                        r, q = col(rinv, u), col(rs, u)
                        dve.wait_ge(s_ex, ex0 + u + 1)
                        if mlstm:
                            dve.wait_ge(mida, t2 + u + 1)
                            ch(dve.scalar_tensor_tensor(out=q, in0=q, scalar=-1.0, in1=q, op0=ALU.mult, op1=ALU.max))
                            ch(dve.tensor_scalar(q, q, col(em, u), None, ALU.max))
                        ch(dve.reciprocal(r, q))
                        dve.wait_ge(s_o, o0 + u + 1)
                        dve.tensor_scalar(dst(h, i), value_bank(u, dv), r, None, ALU.mult).then_inc(s_on, 1)
            stage(pe, act, dve)

        crow = work(0, 256)
        freq = work(256, HALF)
        ang = work(320, NT, HALF)
        angk = work(384, NT, HALF)
        posf = work(448, NT)
        crows = []
        for k, name in enumerate(norm_names):
            v = I[name] if len(I[name].shape) == 1 else I[name][0]
            crows.append((crow[8 * k:8 * k + 8, 0:P], v.rearrange("(k p) -> k p", p=P)))
        crows += [(crow[0:64, P:2 * P], I["conv_w_2"][0].rearrange("w (k p) -> (w k) p", p=P)),
                  (crow[CB:CB + 16, P:2 * P], I["conv_b_2"][0].rearrange("(k p) -> k p", p=P)),
                  (crow[QA:QA + 2, P:2 * P], I["l0_mla_q_a_norm"].rearrange("(k p) -> k p", p=P)),
                  (crow[QA + 2:QA + 3, P:2 * P], I["l0_mla_kv_a_norm"].rearrange("(k p) -> k p", p=P)),
                  (crow[BS:BS + 8, P:2 * P], I["b_s_2"][0])]
        for r, name in ((FQ, "l1_fox_q_norm"), (FK, "l1_fox_k_norm")):
            for h in range(2):
                crows.append((crow[r:r + 1, P + 64 * h:P + 64 * h + 64], I[name].rearrange("(k p) -> k p", p=64)))

        def every(v):
            return v.rearrange("(a n) -> a n", a=1).to_broadcast([P, v.shape[0]])

        crows += [(ffb[:, :], every(I["l1_fox_f_bias"])), (qg[:, 0, :], every(I["l0_mla_q_norm"])),
                  (qg[:, 1, :], every(I["l0_mla_k_norm"])), (bif[:, :], every(I["b_if_2"][0])),
                  (rbias[:, 0:NGR], every(I["b_rg_2"][0])), (rbias[:, NGR:], every(I["b_re_2"][0]))]

        def consts_po(po, ch):
            for m, val in ((ident, 0.0), (tri, 1.0), (ones, 1.0), (maskz, 0.0), (nhalf, -0.5)):
                ch.mark(po.memset(m[:, :], val))
            for j in range(HALF):
                ch.mark(po.memset(freq[:, j:j + 1], float(np.float32(10000.0) ** (-np.float32(j) / np.float32(HALF)))))
            ch.wait()
            ch.mark(po.affine_select(out=ident[:, :], in_=ident[:, :], compare_op=ALU.not_equal, fill=1.0,
                                     base=0, pattern=[[-1, P]], channel_multiplier=1))
            ch.mark(po.affine_select(out=tri[:, :], in_=tri[:, :], compare_op=ALU.is_ge, fill=0.0,
                                     base=0, pattern=[[1, P]], channel_multiplier=-1))
            ch.mark(po.affine_select(out=maskz[:, S - P:S], in_=maskz[:, S - P:S], compare_op=ALU.is_ge, fill=NEG,
                                     base=0, pattern=[[-1, P]], channel_multiplier=1))
            for v, step, n, b in ((rank1, 1, P, 1), (desc, -1, NE, NE), (eidx, 1, NE, 0)):
                ch.mark(po.iota(v[:, :], pattern=[[step, n]], base=b, channel_multiplier=0,
                                allow_small_or_imprecise_dtypes=True))
            ch.wait()
        stage(None, None, None, consts_po)

        tr_c, mv_c = use(tr, 1), use(midv, 1)

        def cols_pe(pe, ch):
            pe.wait_ge(cst, 16 * (len(crows) + 1))
            pe.transpose(ps[0:P, 0, 0:64], crow[0:64, 0:P], ident[0:64, 0:64])
            pe.transpose(ps[0:P, 1, 0:93], crow[0:93, P:2 * P], ident[0:93, 0:93]).then_inc(tr, 1)

        def cols_act(act, ch):
            act.wait_ge(midv, mv_c + 1)
            ch.mark(act.activation(ropes[:, :, :], ropes[:, :, :], ACT.Sin))
            ch(act.activation(ropec[:, :, :], ropec[:, :, :], ACT.Sin))

        def cols_dve(dve, ch):
            dve.wait_ge(cst, 16 * (len(crows) + 1))
            ch(dve.tensor_copy(posf, posi[:, :]))
            c1, c2, c3 = two_pi()
            ch(dve.tensor_tensor(ang, posf.rearrange("p (t o) -> p t o", o=1).to_broadcast([P, NT, HALF]),
                                 freq.rearrange("p (o h) -> p o h", o=1).to_broadcast([P, NT, HALF]), ALU.mult))
            magic = 1.5 * 2.0 ** 23
            ch(dve.tensor_scalar(angk, ang, float(np.float32(1 / (2 * np.pi))), magic, ALU.mult, ALU.add))
            ch(dve.tensor_scalar(angk, angk, magic, None, ALU.subtract))
            for c in (c1, c2, c3):
                ch(dve.scalar_tensor_tensor(out=ang, in0=angk, scalar=-c, in1=ang, op0=ALU.mult, op1=ALU.add))
            lim = 3.1415925
            ch(dve.tensor_scalar(ropes[:, :, :], ang, lim, -lim, ALU.min, ALU.max))
            ch(dve.scalar_tensor_tensor(out=ropec[:, :, :], in0=ropes[:, :, :], scalar=-1.0, in1=ropes[:, :, :],
                                        op0=ALU.mult, op1=ALU.max))
            dve.tensor_scalar(ropec[:, :, :], ropec[:, :, :], -1.0, float(np.float32(np.pi / 2)),
                              ALU.mult, ALU.add).then_inc(midv, 1)
            dve.wait_ge(tr, tr_c + 1)
            ch.mark(dve.tensor_copy(gains[:, :], ps[:, 0, 0:64]))
            ch(dve.tensor_copy(cols2[:, 0:93], ps[:, 1, 0:93]))
            ch.mark(dve.memset(cols2[64:65, FQ:FK + 1], 1.0))
            dve.wait_ge(xin, 16)
            ch.wait()
        stage(cols_pe, cols_act, cols_dve)

        def softplus_stages(n, cs_cols, extra=None):
            f, a = FG[:, 0, :, 0:n], FG[:, 1, :, 0:n]
            v0, a0, t0 = use(midv, 2), use(mida, 1), use(tr, 2 if cs_cols else 1)

            def dve(dve, ch):
                dve.scalar_tensor_tensor(out=a, in0=f, scalar=-1.0, in1=f, op0=ALU.mult, op1=ALU.max).then_inc(midv, 1)
                ch(dve.tensor_scalar(f, f, -1.0, 0.0, ALU.mult, ALU.max))
                dve.wait_ge(mida, a0 + 1)
                dve.tensor_tensor(f, f, a, ALU.add).then_inc(midv, 1)
                dve.wait_ge(tr, t0 + 1)
                ch(dve.tensor_copy(CS[:, :, 0:n], ps[:, 0, 0:NT * n].rearrange("p (t a) -> p t a", t=NT)))
                if extra:
                    extra(dve, ch)

            def act(act, ch):
                act.wait_ge(midv, v0 + 1)
                ch(act.activation(a, a, ACT.Exp, scale=-1.0))
                act.activation(a, a, ACT.Ln, bias=1.0).then_inc(mida, 1)

            def pe(pe, ch):
                pe.wait_ge(midv, v0 + 2)
                for t in range(NT):
                    for j in range(t + 1):
                        m = pe.matmul(ps[:, 0, t * n:t * n + n], (tri if j == t else ones)[:, :], FG[:, 0, j, 0:n],
                                      start=(j == 0), stop=(j == t))
                m.then_inc(tr, 1)
            stage(pe, act, dve)
            if not cs_cols:
                return
            src, dst, scale = cs_cols

            def pe2(pe, ch):
                for t in range(NT):
                    m = pe.transpose(ps[0:n, 1, t * P:t * P + P], src[:, t, 0:n], ident[:, :])
                m.then_inc(tr, 1)

            def act2(act, ch):
                act.wait_ge(tr, t0 + 2)
                ch(act.activation(dst, ps[0:n, 1, :], ACT.Copy, scale=scale))
            stage(pe2, act2)

        if on(1):
            cq0 = work(A0, NT, C0)
            sbq = work(A0 + 1664, NT, S)
            sbk = work(A0 + 3712, NT, S)
            sbv = work(A0 + 5760, NT, SBW)
            Qr = work(A0 + 7808, NT, MH * QK)
            Kr = work(A0 + 10880, NT, MH * QK)
            Vr = work(A0 + 13952, NT, MH * MV)
            QT = work(A0 + 16000, 2, 512)
            KT = work(A0 + 17024, 2, 512)
            low_x = act_parts(A0 + 7808)
            cqT = parts(A0 + 7808, A0 + 7808 + 3 * S, 3, S)
            sqq = work(0, NT * MH, QK)
            sqk = work(A0 + 16000 + 3072, NT * MH, HALF)
            early = []
            norm_stage(x, low_x, G_A0, NT, work(A0, 4 * D), early)
            gr = Groups(16, "AV")
            w = I["l0_w_in"]
            jobs = [
                (Rows(gr, 0, low_x, NT, [(kpc(w[:, 0:C0]), 0)], C0), lambda t: cq0[:, t, :], 1.0),
                (Cols(gr, 4, low_x, S, [(kpc(w[:, C0:C0 + SBW]), 0)]), lambda t: sbq[:, t, :], 64 ** -0.5),
                (Cols(gr, 8, low_x, S, [(kpc(w[:, C0 + SBW:C0 + 2 * SBW]), 0)]), lambda t: sbk[:, t, :], 1.0),
                (Rows(gr, 12, low_x, NT, [(kpc(w[:, C0 + 2 * SBW:C0 + 3 * SBW]), 0)], SBW),
                 lambda t: sbv[:, t, :], 1.0)]
            ahead(early, jobs[0][0].w)
            plain_stage(jobs, gr)

            ss0, rs0, xs0, tr0 = use(ssd, 1), use(rsd, 1), use(xsd, 4), use(tr, 4)
            gr1 = Groups(4, "V")
            hi1 = use(ea, 4)
            junk = work(0, D)
            ctmp = work(D, NT, 3 * P)

            def rank_act(act, ch):
                for t in range(NT):
                    ch(act.activation(junk[:, 0:QR], cq0[:, t, 0:QR], ACT.Square, accum_out=ss[:, t:t + 1]))
                    last = act.activation(junk[:, QR:QR + KVR], cq0[:, t, QR:QR + KVR], ACT.Square,
                                          accum_out=ss[:, 4 + t:5 + t])
                    if t < NT - 1:
                        ch(last)
                last.then_inc(ssd, 1)
                for t in range(NT):
                    act.wait_ge(midv, md1 + t + 1)
                    act.activation(cqT[:, :, t * P:t * P + P].h, ctmp[:, t, :].rearrange("p (k s) -> p k s", k=3),
                                   ACT.Copy).then_inc(ea, 1)
            md1 = use(midv, 4)

            def rank_po(po, ch):
                po.wait_ge(ssd, ss0 + 1)
                ch.mark(po.tensor_scalar(ss[:, 0:4], ss[:, 0:4], 1.0 / QR, EPS, ALU.mult, ALU.add))
                ch(po.tensor_scalar(ss[:, 4:8], ss[:, 4:8], 1.0 / KVR, EPS, ALU.mult, ALU.add))
                po.tensor_tensor(ss[:, :], ss[:, :], nhalf[:, :].to_broadcast([P, 8]), ALU.pow).then_inc(rsd, 1)

            def rank_dve(dve, ch):
                dve.wait_ge(rsd, rs0 + 1)
                for t in range(NT):
                    ch(dve.tensor_scalar(cq0[:, t, 0:QR], cq0[:, t, 0:QR], ss[:, t:t + 1], None, ALU.mult))
                    dve.tensor_scalar(cq0[:, t, QR:QR + KVR], cq0[:, t, QR:QR + KVR], ss[:, 4 + t:5 + t], None,
                                      ALU.mult).then_inc(xsd, 1)
                for t in range(NT):
                    dve.wait_ge(tr, tr0 + t + 1)
                    dve.tensor_tensor(ctmp[:, t, :].rearrange("p (k s) -> p k s", k=3),
                                      ps[:, t, 0:3 * P].rearrange("p (k s) -> p k s", k=3),
                                      cols2[:, QA:QA + 3].rearrange("p (k o) -> p k o", o=1).to_broadcast([P, 3, P]),
                                      ALU.mult).then_inc(midv, 1)
                for t in range(NT):
                    dve.wait_ge(ea, hi1 + t + 1)
                    dve.wait_ge(midv, md1 + t + 1)
                    d = cqT[:, :, t * P:t * P + P]
                    dve.tensor_tensor(d.l, ctmp[:, t, :].rearrange("p (k s) -> p k s", k=3), d.high_f,
                                      ALU.subtract).then_inc(ev, 1)

            def rank_pe(pe, ch):
                for t in range(NT):
                    pe.wait_ge(xsd, xs0 + t + 1)
                    for j in range(3):
                        m = pe.transpose(ps[:, t, j * P:j * P + P], cq0[:, t, j * P:j * P + P], ident[:, :])
                    m.then_inc(tr, 1)
            stage(rank_pe, rank_act, rank_dve, rank_po)

            gr2 = Groups(16, "AV")
            up_q = Rows(gr2, 0, cqT, NT, [(kpc(I["l0_mla_w_q_up"]), 0)], 384, 2, 2)
            up_kv = Rows(gr2, 8, cqT[:, 2:3, :], NT, [(kpc(I["l0_mla_w_kv_up"]), 0)], 512, 1, 2)

            def up_pe(pe, ch):
                up_q.pe(pe)
                up_kv.pe(pe)

            def kv_views(r):
                t, h = divmod(r, 2)
                s = up_kv.src(r).rearrange("p (h c) -> p h c", c=P)
                k = Kr[:, t, :].rearrange("p (h c) -> p h c", c=QK)[:, 4 * h:4 * h + 4, 0:NOPE]
                v = Vr[:, t, :].rearrange("p (h c) -> p h c", c=MV)[:, 4 * h:4 * h + 4, :]
                return s, k, v

            QrT = area(NS * SLOT, A0 + 16000, NT, MH * QK)

            sp1 = Split([up_q, up_kv])

            def up_act(act, ch):
                sp1.start(act)
                sp1.before(act, 0)
                for r in range(0, 8, 2):
                    up_q.ready(act, r)
                    take_act(act, up_q.src(r), QrT[:, r // 2, 0:384])
                for r in range(0, 8, 2):
                    up_kv.ready(act, r)
                    s, k, v = kv_views(r)
                    ch(act.activation(k, s[:, :, 0:NOPE], ACT.Copy))
                    take_act(act, s[:, :, NOPE:P], v)

            def up_dve(dve, ch):
                sp1.start(dve)
                sp1.before(dve, 0)
                for r in range(1, 8, 2):
                    up_q.ready(dve, r)
                    take_dve(dve, up_q.src(r), QrT[:, r // 2, 384:768])
                for r in range(1, 8, 2):
                    up_kv.ready(dve, r)
                    s, k, v = kv_views(r)
                    ch(dve.tensor_copy(k, s[:, :, 0:NOPE]))
                    take_dve(dve, s[:, :, NOPE:P], v)
            stage(up_pe, up_act, up_dve)

            ss1, rs1 = use(ssd, 2), use(rsd, 1)

            def heads(v):
                return v.rearrange("p t (h c) -> p (t h) c", c=QK)

            def head_norm(eng, ch, src, dst, which, stat):
                b = [P, NT * MH, QK]
                ch(eng.tensor_tensor(heads(dst), heads(src), stat.rearrange("p (n o) -> p n o", o=1).to_broadcast(b),
                                     ALU.mult))
                ch(eng.tensor_tensor(heads(dst), heads(dst), qg[:, which:which + 1, :].to_broadcast(b), ALU.mult))
                tmp = (sqq, sqk)[which]
                for t in range(NT):
                    d = dst[:, t, :].rearrange("p (h c) -> p h c", c=QK)
                    r1, r2 = d[:, :, NOPE:NOPE + HALF], d[:, :, NOPE + HALF:QK]
                    cs_, sn = (v[:, t:t + 1, :].to_broadcast([P, MH, HALF]) for v in (ropec, ropes))
                    a = [tmp[:, 8 * q:8 * q + 8, 0:HALF] for q in range(4)]
                    ch.mark(eng.tensor_tensor(a[0], r1, cs_, ALU.mult))
                    ch.mark(eng.tensor_tensor(a[1], r2, sn, ALU.mult))
                    ch.mark(eng.tensor_tensor(a[2], r2, cs_, ALU.mult))
                    ch(eng.tensor_tensor(a[3], r1, sn, ALU.mult))
                    ch.mark(eng.tensor_tensor(r1, a[0], a[1], ALU.subtract))
                    ch(eng.tensor_tensor(r2, a[2], a[3], ALU.add))

            def hn_act(act, ch):
                act.activation(sqq, heads(QrT), ACT.Square).then_inc(ssd, 1)

            def hn_dve(dve, ch):
                for t in range(NT):
                    ch.mark(dve.tensor_copy(
                        Kr[:, t, :].rearrange("p (h c) -> p h c", c=QK)[:, :, NOPE:QK],
                        cq0[:, t:t + 1, QR + KVR:C0].to_broadcast([P, MH, RO])))
                ch.wait()
                dve.wait_ge(ssd, ss1 + 1)
                ch(dve.tensor_reduce(st[:, 0:32], sqq, AX, ALU.add))
                ch(dve.tensor_tensor(sqq, heads(Kr), heads(Kr), ALU.mult))
                dve.tensor_reduce(st[:, 32:64], sqq, AX, ALU.add).then_inc(ssd, 1)
                dve.wait_ge(rsd, rs1 + 1)
                head_norm(dve, ch, QrT, Qr, 0, st[:, 0:32])

            def hn_po(po, ch):
                po.wait_ge(ssd, ss1 + 2)
                ch(po.tensor_scalar(st[:, 0:64], st[:, 0:64], 1.0 / QK, EPS, ALU.mult, ALU.add))
                po.tensor_tensor(st[:, 0:64], st[:, 0:64], nhalf[:, :].to_broadcast([P, 64]), ALU.pow).then_inc(rsd, 1)
                po.wait_ge(rsd, rs1 + 1)
                head_norm(po, ch, Kr, Kr, 1, st[:, 32:64])
            stage(None, hn_act, hn_dve, hn_po)

            preps = []
            for h in range(MH):
                for n, (R, to) in enumerate(((Qr, QT), (Kr, KT))):
                    preps.append((max(0, 4 * h - 3 + n), max(0, 4 * (h - 1)),
                                  [R[:, t, h * QK:h * QK + QK] for t in range(NT)], to[0:QK, h % 2, :], 1.0))

            def sc_mla(pe, v, b, pre0):
                h, i = divmod(v, NT)
                pe.wait_ge(s_pre, pre0 + 2 * h + 2)
                L = causal(v)
                return pe.matmul(ps[:, b, 0:L], QT[0:QK, h % 2, i * P:i * P + P], KT[0:QK, h % 2, 0:L],
                                 start=True, stop=True)
            attention(MH * NT, causal, sc_mla,
                      lambda u, j: Vr[:, j, (u // NT) * MV:(u // NT) * MV + MV], MV,
                      lambda h, i: orow[:, i, h * MV:h * MV + MV], QK ** -0.5, preps)

            T1 = work(A0 + 7808, 4, 512)
            U0 = MH * NT
            sc0, t10, sp0, m10, w0, m20, ex0, pt0, pe0, o0, on0 = (
                use(s, U0) for s in (s_sc, s_t1, s_sp, s_m1, s_w, s_m2, s_ex, s_pt, s_pe, s_o, s_on))
            
            def sb_pe(pe, ch):
                for v in range(U0 + 4):
                    if v < U0:
                        h, i = divmod(v, NT)
                        L = causal(v)
                        if v >= 3:
                            pe.wait_ge(s_w, w0 + v - 2)
                        r = slice(64 * (h % 2), 64 * (h % 2) + 64)
                        pe.matmul(ps[:, v % 3, 0:L], sbq[r, h // 2, i * P:i * P + P], sbk[r, h // 2, 0:L],
                                  start=True, stop=True).then_inc(s_sc, 1)
                    if 3 <= v < U0 + 3:
                        u = v - 3
                        pe.wait_ge(s_ex, ex0 + u + 1)
                        if u >= 2:
                            pe.wait_ge(s_pe, pe0 + u - 1)
                        for j in range(causal(u) // P):
                            m = pe.transpose(ps[:, 3 + u % 2, j * P:j * P + P], Pb[:, u % 4, j * P:j * P + P],
                                             ident[:, :])
                        m.then_inc(s_pt, 1)
                    if v >= 4:
                        u = v - 4
                        h = u // NT
                        pe.wait_ge(s_pe, pe0 + u + 1)
                        if u >= 2:
                            pe.wait_ge(s_on, on0 + u - 1)
                        nb = causal(u) // P
                        for j in range(nb):
                            m = pe.matmul(value_bank(u, 64), PT[:, u % 2, j * P:j * P + P],
                                          sbv[:, j, h * 64:h * 64 + 64], start=(j == 0), stop=(j == nb - 1))
                        m.then_inc(s_o, 1)

            def sb_act(act, ch):
                act.preload_act_table_set("natural_log_exp_and_others")
                for v in range(U0 + 3):
                    if v < U0:
                        act.wait_ge(s_sc, sc0 + v + 1)
                        if v >= 4:
                            act.wait_ge(s_w, w0 + v - 3)
                        t1 = T1[:, v % 4, 0:causal(v)]
                        ch(act.activation(t1, ps[:, v % 3, 0:causal(v)], ACT.Abs))
                        ch(act.activation(t1, t1, ACT.Exp, scale=-1.0))
                        act.activation(t1, t1, ACT.Ln, bias=1.0).then_inc(s_t1, 1)
                    if 2 <= v < U0 + 2:
                        u = v - 2
                        act.wait_ge(s_m2, m20 + u + 1)
                        p = Pb[:, u % 4, 0:causal(u)]
                        act.activation(p, p, ACT.Exp).then_inc(s_ex, 1)
                    if v >= 3:
                        u = v - 3
                        L = causal(u)
                        act.wait_ge(s_pt, pt0 + u + 1)
                        if u >= 2:
                            act.wait_ge(s_o, o0 + u - 1)
                        act.activation(PT[:, u % 2, 0:L], ps[:, 3 + u % 2, 0:L], ACT.Copy).then_inc(s_pe, 1)

            def sb_dve(dve, ch):
                for v in range(U0 + 4):
                    if v < U0:
                        dve.wait_ge(s_t1, t10 + v + 1)
                        t1 = T1[:, v % 4, 0:causal(v)]
                        dve.scalar_tensor_tensor(out=t1, in0=ps[:, v % 3, 0:causal(v)], scalar=0.0, in1=t1,
                                                 op0=ALU.max, op1=ALU.add).then_inc(s_sp, 1)
                    if 1 <= v <= U0:
                        u = v - 1
                        L = causal(u)
                        t1 = T1[:, u % 4, 0:L]
                        p = Pb[:, u % 4, 0:L]
                        dve.wait_ge(s_m1, m10 + u + 1)
                        if u >= 4:
                            dve.wait_ge(s_pt, pt0 + u - 3)
                        ch(dve.tensor_tensor_scan(p[:, ::-1], ones[:, 0:1].to_broadcast([P, L]), t1[:, ::-1], 0.0,
                                                  ALU.mult, ALU.add))
                        dve.tensor_tensor(p, ps[:, u % 3, 0:L], p, ALU.subtract).then_inc(s_w, 1)
                    if v >= 4:
                        u = v - 4
                        h, i = divmod(u, NT)
                        dve.wait_ge(s_o, o0 + u + 1)
                        dve.tensor_copy(orow[:, i, 512 + h * 64:512 + h * 64 + 64],
                                        value_bank(u, 64)).then_inc(s_on, 1)

            def sb_po(po, ch):
                for v in range(U0 + 1):
                    if v < U0:
                        dg = T1[:, v % 4, causal(v) - P:causal(v)]
                        po.wait_ge(s_sp, sp0 + v + 1)
                        po.affine_select(out=dg, in_=dg, compare_op=ALU.is_gt, fill=0.0,
                                         base=0, pattern=[[-1, P]], channel_multiplier=1).then_inc(s_m1, 1)
                    if v >= 1:
                        u = v - 1
                        dg = Pb[:, u % 4, causal(u) - P:causal(u)]
                        po.wait_ge(s_w, w0 + u + 1)
                        po.affine_select(out=dg, in_=dg, compare_op=ALU.is_gt, fill=NEG,
                                         base=0, pattern=[[-1, P]], channel_multiplier=1).then_inc(s_m2, 1)
            stage(sb_pe, sb_act, sb_dve, sb_po)
            out_stage(orow, I["l0_w_o"])
        if on(2):
            ffn(G_F0, I["l0_w_gate"], I["l0_w_up"], I["l0_w_down"])

        if on(3):
            FW = 65
            FQr = work(A0, NT * FH, FW)
            FKr = work(A0 + 4160, NT * FH, FW)
            FVr = work(A0 + 8320, NT, D)
            FQT = work(A0 + 12416, 2, 512)
            FKT = work(A0 + 13440, 2, 512)
            sqf = work(A0 + 14464, 2, 512)
            low_x = act_parts(A0 + 15488)
            w = I["l1_w_in"]
            early = []
            norm_stage(x, low_x, G_A1, NT, work(A0, 4 * D), early)
            gr = Groups(28, "VVVV" + "A" * 16 + "AV" * 4)
            fj = Rows(gr, 0, low_x, NT, [(kpc(w[:, 3 * D:3 * D + FH]), 0)], FH)
            qk_jobs = [(Rows(gr, 4 + 4 * j, low_x, NT, [(kpc(w[:, j * 512:j * 512 + 512]), 0)], 512),
                        (FQr, FKr)[j // 2], j) for j in range(4)]
            v_jobs = [(Rows(gr, 20 + 4 * j, low_x, NT, [(kpc(w[:, (4 + j) * 512:(5 + j) * 512]), 0)], 512), j)
                      for j in range(2)]
            ahead(early, fj.w)
            rows_in = gr
            fsp = Split([fj] + [job for job, _, _ in qk_jobs] + [job for job, _ in v_jobs])
            nn = NT * FH
            sq0, mv2, rs2 = use(ssd, 16), use(midv, 16), use(rsd, 2)
            st4 = st[:, :].rearrange("p (c t a) -> p c t a", c=4, t=NT)

            def head_rows(R, t, j):
                h0 = t * FH + 8 * (j % 2)
                return R[:, h0:h0 + 8, 0:64]

            def fp_pe(pe, ch):
                fj.pe(pe)
                for job, _, _ in qk_jobs:
                    job.pe(pe)
                for job, _ in v_jobs:
                    job.pe(pe)

            def fp_act(act, ch):
                n = 0
                fsp.start(act)
                fsp.before(act, 0)
                fsp.after(act, 0)
                for job, R, j in qk_jobs:
                    fsp.before(act, 1 + j)
                    for t in range(NT):
                        job.ready(act, t)
                        if n >= 2:
                            act.wait_ge(midv, mv2 + n - 1)
                        act.activation(sqf[:, n % 2, :], job.src(t), ACT.Square).then_inc(ssd, 1)
                        act.activation(head_rows(R, t, j), job.src(t).rearrange("p (h c) -> p h c", c=64),
                                       ACT.Copy).then_inc(ea, 1)
                        n += 1
                    fsp.after(act, 1 + j)
                for job, c in v_jobs:
                    fsp.before(act, 5 + c)
                    for t in range(0, NT, 2):
                        job.ready(act, t)
                        take_act(act, job.src(t), FVr[:, t, c * 512:c * 512 + 512])
                    fsp.after(act, 5 + c)

            def fp_norm(eng, ch, which, R):
                eng.wait_ge(rsd, rs2 + which + 1)
                rows_in.wait_taken(eng, 11 + 8 * which)
                for c in range(2):
                    for t in range(NT):
                        r = head_rows(R, t, c)
                        ch.mark(eng.tensor_tensor(r, r, st4[:, 2 * which + c, t, :].rearrange("p (a o) -> p a o", o=1
                                                                                              ).to_broadcast([P, 8, 64]),
                                                  ALU.mult))
                ch.wait()

            def fp_dve(dve, ch):
                fsp.start(dve)
                fsp.before(dve, 0)
                for t in range(NT):
                    fj.ready(dve, t)
                    dve.tensor_tensor(FG[:, 0, t, :], fj.src(t), ffb[:, :], ALU.add).then_inc(ev, 1)
                fsp.after(dve, 0)
                for n in range(16):
                    if n % 4 == 0:
                        fsp.before(dve, 1 + n // 4)
                    dve.wait_ge(ssd, sq0 + n + 1)
                    c, t = divmod(n, NT)
                    dve.tensor_reduce(st4[:, c, t, :], sqf[:, n % 2, :].rearrange("p (h c) -> p h c", c=64), AX,
                                      ALU.add).then_inc(midv, 1)
                    if n % 4 == 3:
                        fsp.after(dve, 1 + n // 4)
                for job, c in v_jobs:
                    fsp.before(dve, 5 + c)
                    for t in range(1, NT, 2):
                        job.ready(dve, t)
                        take_dve(dve, job.src(t), FVr[:, t, c * 512:c * 512 + 512])
                    fsp.after(dve, 5 + c)

            def fp_po(po, ch):
                ch.mark(po.memset(FQr[:, :, 64:65], 1.0))
                for which, R in enumerate((FQr, FKr)):
                    s_ = st[:, which * nn:(which + 1) * nn]
                    po.wait_ge(midv, mv2 + 8 * (which + 1))
                    ch(po.tensor_scalar(s_, s_, 1.0 / 64, EPS, ALU.mult, ALU.add))
                    po.tensor_tensor(s_, s_, nhalf[:, :].to_broadcast([P, nn]), ALU.pow).then_inc(rsd, 1)
                    fp_norm(po, ch, which, R)
            stage(fp_pe, fp_act, fp_dve, fp_po)

            def decay_rows(dve, ch):
                ch(dve.tensor_scalar(FKr[:, :, 64:65].rearrange("p n o -> p (n o)"),
                                     CS[:, :, :].rearrange("p t h -> p (t h)"), 8.0, None, ALU.mult))
            softplus_stages(FH, None, decay_rows)

            preps = []
            for h in range(FH):
                for n, (R, to, g) in enumerate(((FQr, FQT, FQ), (FKr, FKT, FK))):
                    preps.append((max(0, 4 * h - 3 + n), max(0, 4 * (h - 1)),
                                  [R[:, t * FH + h, :] for t in range(NT)], to[0:FW, h % 2, :], cols2[0:FW, g:g + 1]))

            def sc_fox(pe, v, b, pre0):
                h, i = divmod(v, NT)
                pe.wait_ge(s_pre, pre0 + 2 * h + 2)
                return pe.matmul(ps[:, b, 0:causal(v)], FQT[0:FW, h % 2, i * P:i * P + P],
                                 FKT[0:FW, h % 2, 0:causal(v)], start=True, stop=True)
            attention(FH * NT, causal, sc_fox,
                      lambda u, j: FVr[:, j, (u // NT) * 64:(u // NT) * 64 + 64], 64,
                      lambda h, i: orow[:, i, h * 64:h * 64 + 64], 0.125, preps, fox=True)
            out_stage(orow, I["l1_w_o"])
        if on(4):
            ffn(G_F1, I["l1_w_gate"], I["l1_w_up"], I["l1_w_down"])

        late = []

        def load_now(name, dst, src):
            s = sem(name)
            late.append((len(stages), dst, src, s))
            return s, 16

        if on(5):
            mqk = work(A0, 16, S)
            mv = work(A0 + 8192, NT, D)
            H = work(A0 + 12288, NT, D)
            low_x = act_parts(A0 + 16384)
            acc = work(A0 + 20480, 2, 512)
            CTm = work(A0 + 21504, S)
            E = work(3072, 4, 512)
            w = I["w_in_2"][0]
            early = []
            norm_stage(x, low_x, G_MIX, NT, work(A0, 4 * D), early)
            gr = Groups(28, "V" * 4 + "C" * 16 + "AV" * 4)
            ij = Rows(gr, 0, low_x, NT, [(kpc(w[:, 4096:4104]), 0)], 8)
            qkj = [Cols(gr, 4 + 4 * c, low_x, S, [(kpc(w[:, c * 512:c * 512 + 512]), 0)]) for c in range(4)]
            vj = [Rows(gr, 20 + 4 * c, low_x, NT, [(kpc(w[:, 2048 + c * 512:2560 + c * 512]), 0)], 512)
                  for c in range(2)]
            ahead(early, ij.w)
            msp = Split([ij] + qkj + vj)
            cv0, sl0 = gr.freed[4][1] - 1, use(mida, 16)

            def mp_pe(pe, ch):
                for job in [ij] + qkj + vj:
                    job.pe(pe)

            def mp_act(act, ch):
                msp.start(act)
                msp.before(act, 0)
                msp.after(act, 0)
                for c in range(16):
                    if c % 4 == 0:
                        msp.before(act, 1 + c // 4)
                    act.wait_ge(midv, cv0 + c + 1)
                    act.activation(mqk[:, c, :], acc[:, c % 2, :], ACT.Silu,
                                   bias=cols2[:, CB + c:CB + c + 1]).then_inc(mida, 1)
                    if c % 4 == 3:
                        msp.after(act, 1 + c // 4)
                for c, job in enumerate(vj):
                    msp.before(act, 5 + c)
                    for t in range(0, NT, 2):
                        job.ready(act, t)
                        take_act(act, job.src(t), mv[:, t, c * 512:c * 512 + 512])
                    msp.after(act, 5 + c)

            def mp_dve(dve, ch):
                msp.start(dve)
                msp.before(dve, 0)
                for t in range(NT):
                    ij.ready(dve, t)
                    b = ps[:, gr.bank(t), :]
                    ch(dve.tensor_tensor(FG[:, 1, t, 4:8], b[:, 0:4], bif[:, 0:4], ALU.add))
                    dve.tensor_tensor(FG[:, 0, t, 0:4], b[:, 4:8], bif[:, 4:8], ALU.add).then_inc(ev, 1)
                msp.after(dve, 0)
                for c in range(16):
                    job = qkj[c // 4]
                    if c % 4 == 0:
                        msp.before(dve, 1 + c // 4)
                    job.ready(dve, c % 4)
                    if c >= 2:
                        dve.wait_ge(mida, sl0 + c - 1)
                    p, a = job.src(c % 4), acc[:, c % 2, :]
                    tap = lambda i: cols2[:, CW + 16 * i + c:CW + 16 * i + c + 1]
                    ch(dve.tensor_scalar(a, p, tap(3), None, ALU.mult))
                    for s in (1, 2, 3):
                        ins = dve.scalar_tensor_tensor(out=a[:, s:S], in0=p[:, 0:S - s], scalar=tap(3 - s),
                                                       in1=a[:, s:S], op0=ALU.mult, op1=ALU.add)
                        if s < 3:
                            ch(ins)
                    ins.then_inc(midv, 1)
                    if c % 4 == 3:
                        msp.after(dve, 1 + c // 4)
                for c, job in enumerate(vj):
                    msp.before(dve, 5 + c)
                    for t in range(1, NT, 2):
                        job.ready(dve, t)
                        take_dve(dve, job.src(t), mv[:, t, c * 512:c * 512 + 512])
                    msp.after(dve, 5 + c)
            stage(mp_pe, mp_act, mp_dve)

            def input_gates(dve, ch):
                ch(dve.tensor_tensor(FG[:, 1, :, 8:12], FG[:, 1, :, 4:8], CS[:, :, 0:4], ALU.add))
            softplus_stages(LH, (FG[:, 1, :, 8:12], CTm[0:LH, :], 1.0), input_gates)

            def exponents(pe, h):
                return pe.matmul(ps[:, 7, :], ident[0:LH, h:h + 1].to_broadcast([LH, P]), CTm[0:LH, :],
                                 start=True, stop=True)

            def sc_ml(pe, v, b, pre0):
                h, i = divmod(v, NT)
                for k in range(2):
                    m = pe.matmul(ps[:, b, 0:causal(v)], mqk[:, 2 * h + k, i * P:i * P + P],
                                  mqk[:, 8 + 2 * h + k, 0:causal(v)], start=(k == 0), stop=(k == 1))
                return m
            attention(LH * NT, causal, sc_ml, lambda u, j: mv[:, j, (u // NT) * DH:(u // NT) * DH + DH], DH,
                      lambda h, i: H[:, i, h * DH:h * DH + DH], 1.0, mlstm=(exponents, E))

            sqm = work(A0, NT, D)
            mhb = work(A0 + 4096, D)
            mhb_in = load_now("mhb_in", mhb, every(I["mh_norm_g_2"][0]))
            sgb = work(A0 + 5120, D)
            sgb_in = load_now("sgb_in", sgb, every(I["sgu_norm_g_2"][0]))
            gb = work(A0 + 6144, 2 * D)
            gb_in = load_now("gb_in", gb, every(I["b_gate_2"][0]))
            ss3, rs3 = use(ssd, 1), use(rsd, 1)

            def d256(v):
                return v[:, :, :].rearrange("p t (h c) -> p (t h) c", c=DH)

            def hm_act(act, ch):
                act.activation(sqm, H, ACT.Square).then_inc(ssd, 1)
            mv3 = use(midv, 1)

            def hm_dve(dve, ch):
                dve.wait_ge(ssd, ss3 + 1)
                dve.tensor_reduce(st[:, 0:16], d256(sqm), AX, ALU.add).then_inc(midv, 1)
                dve.wait_ge(rsd, rs3 + 1)
                ch(dve.tensor_tensor(d256(H), d256(H),
                                     st[:, 0:16].rearrange("p (n o) -> p n o", o=1).to_broadcast([P, 16, DH]),
                                     ALU.mult))
                dve.wait_ge(*mhb_in)
                ch(dve.tensor_tensor(H, H, mhb.rearrange("p (o c) -> p o c", o=1).to_broadcast([P, NT, D]), ALU.mult))

            def hm_po(po, ch):
                po.wait_ge(midv, mv3 + 1)
                ch(po.tensor_scalar(st[:, 0:16], st[:, 0:16], 1.0 / DH, EPS, ALU.mult, ALU.add))
                po.tensor_tensor(st[:, 0:16], st[:, 0:16], nhalf[:, :].to_broadcast([P, 16]), ALU.pow).then_inc(rsd, 1)
            stage(None, hm_act, hm_dve, hm_po)

            tmp = work(A0 + 20480, 3, 512)
            Vs = work(A0 + 8192, NT, D)
            Mx = work(A0, NT, D)
            wsr = work(A0 + 4096, G8, P)
            wsr_in = load_now("wsr_in", wsr, I["w_s_2"][0].rearrange("g t s -> t g s"))
            wsT = wsr

            def gated_stage(spec, dst_of):
                kinds = [kind for _, kind, _, _ in spec for t in range(NT)]
                gr = Groups(len(kinds), ["A" if k == "gelu" else "C" if k == "bias" else "X" for k in kinds])
                jobs = [(Rows(gr, NT * n, low_x, NT, [(kpc(w[:, c0:c0 + 512]), 0)], 512), kind, half, bcol)
                        for n, (c0, kind, half, bcol) in enumerate(spec)]
                order = [k for k in range(len(kinds)) if kinds[k] != "gelu"]
                a0, u0 = use(mida, len(order)), use(xsd, len(order))
                for n, g in enumerate(order):
                    if gr.who[g] == "X":
                        gr.freed[g] = (mida, a0 + n + 1)

                def steps():
                    n = 0
                    for j, (job, kind, half, bcol) in enumerate(jobs):
                        for t in range(NT):
                            yield n, job, kind, half, bcol, t, NT * j + t
                            n += kind != "gelu"

                def pe(pe, ch):
                    for job, _, _, _ in jobs:
                        job.pe(pe)

                gsp = Split([job for job, _, _, _ in jobs])

                def act(act, ch):
                    gsp.start(act)
                    for n, job, kind, half, _, t, g in steps():
                        if t == 0:
                            gsp.before(act, g // NT)
                        b = tmp[:, n % 3, :]
                        if kind == "gelu":
                            job.ready(act, t)
                            act.activation(Vs[:, t, half * 512:half * 512 + 512], job.src(t),
                                           ACT.Gelu_apprx_tanh).then_inc(ea, 1)
                        elif kind == "bias":
                            act.wait_ge(*gr.freed[g])
                            act.activation(b, b, ACT.Sigmoid).then_inc(mida, 1)
                        else:
                            job.ready(act, t)
                            if n >= 3:
                                act.wait_ge(xsd, u0 + n - 2)
                            act.activation(b, job.src(t), kind).then_inc(mida, 1)
                        if t == NT - 1:
                            gsp.after(act, g // NT)

                def dve(dve, ch):
                    gsp.start(dve)
                    dve.wait_ge(*gb_in)
                    todo = []

                    def finish(n, half, bcol, t):
                        dve.wait_ge(mida, a0 + n + 1)
                        dst, add = dst_of(bcol)
                        d = dst[:, t, half * 512:half * 512 + 512]
                        ins = dve.tensor_tensor(d, d, tmp[:, n % 3, :], ALU.mult)
                        if add:
                            ch(ins)
                            y = H[:, t, half * 512:half * 512 + 512]
                            ins = dve.tensor_tensor(y, y, d, ALU.add)
                        ins.then_inc(xsd, 1)
                    for n, job, kind, half, bcol, t, g in steps():
                        if t == 0:
                            gsp.before(dve, g // NT)
                        if kind == "gelu":
                            if t == NT - 1:
                                gsp.after(dve, g // NT)
                            continue
                        if kind == "bias":
                            job.ready(dve, t)
                            if n >= 3:
                                dve.wait_ge(xsd, u0 + n - 2)
                            dve.tensor_tensor(tmp[:, n % 3, :], job.src(t), gb[:, bcol:bcol + 512],
                                              ALU.add).then_inc(midv, 1)
                        todo.append((n, half, bcol, t))
                        if len(todo) > 1:
                            finish(*todo.pop(0))
                        if t == NT - 1:
                            gsp.after(dve, g // NT)
                    for q in todo:
                        finish(*q)
                stage(pe, act, dve)

            gated_stage([(3072, ACT.Sigmoid, 0, None), (3584, ACT.Sigmoid, 1, None),
                         (6152, "bias", 0, 0), (6664, "bias", 1, 512),
                         (5128, "gelu", 0, None), (5640, "gelu", 1, None)],
                        lambda bcol: (H, False))

            ss4, rs4 = use(ssd, 1), use(rsd, 1)

            def sv_act(act, ch):
                for t in range(NT):
                    ins = act.activation(tmp[:, 0:2, :].rearrange("p a b -> p (a b)"), Vs[:, t, :], ACT.Square,
                                         accum_out=ss[:, t:t + 1])
                    if t < NT - 1:
                        ch(ins)
                ins.then_inc(ssd, 1)

            def sv_po(po, ch):
                po.wait_ge(ssd, ss4 + 1)
                ch(po.tensor_scalar(ss[:, 0:4], ss[:, 0:4], 1.0 / D, EPS, ALU.mult, ALU.add))
                po.tensor_tensor(ss[:, 0:4], ss[:, 0:4], nhalf[:, :].to_broadcast([P, 4]), ALU.pow).then_inc(rsd, 1)
            tr4 = use(tr, 2)

            def sv_pe(pe, ch):
                pe.wait_ge(*wsr_in)
                for g in range(G8):
                    m = pe.transpose(ps[:, g // 4, (g % 4) * P:(g % 4) * P + P], wsr[:, g, :], ident[:, :])
                    if g % 4 == 3:
                        m.then_inc(tr, 1)

            def sv_dve(dve, ch):
                dve.wait_ge(*sgb_in)
                for q in range(2):
                    dve.wait_ge(tr, tr4 + q + 1)
                    ch.mark(dve.tensor_tensor(wsT[:, 4 * q:4 * q + 4, :],
                                              ps[:, q, :].rearrange("p (g s) -> p g s", g=4),
                                              tri[:, :].rearrange("p (o s) -> p o s", o=1).to_broadcast([P, 4, P]),
                                              ALU.mult))
                dve.wait_ge(rsd, rs4 + 1)
                for t in range(NT):
                    ch(dve.scalar_tensor_tensor(out=Vs[:, t, :], in0=Vs[:, t, :], scalar=ss[:, t:t + 1],
                                                in1=sgb, op0=ALU.mult, op1=ALU.mult))
            stage(sv_pe, sv_act, sv_dve, sv_po)

            gm = Groups(8, "A")
            tr5 = use(tr, 8)

            def mix_pe(pe, ch):
                for g in range(G8):
                    for c in range(NT):
                        m = pe.matmul(ps[:, g, c * P:c * P + P], wsT[:, g, :], Vs[:, c, g * P:g * P + P],
                                      start=True, stop=True)
                    m.then_inc(tr, 1)

            def mix_act(act, ch):
                for g in range(G8):
                    act.wait_ge(tr, tr5 + g + 1)
                    act.activation(Mx[:, :, g * P:g * P + P], ps[:, g, :].rearrange("p (c s) -> p c s", c=NT),
                                   ACT.Identity, bias=cols2[:, BS + g:BS + g + 1]).then_inc(ea, 1)
            stage(mix_pe, mix_act)
            gated_stage([(4104, ACT.Gelu_apprx_tanh, 0, None), (4616, ACT.Gelu_apprx_tanh, 1, None),
                         (7176, "bias", 0, 1024), (7688, "bias", 1, 1536)],
                        lambda bcol: (Mx, bcol is not None))
            out_stage(H, I["w_out_2"][0])

        if on(6):
            memr = work(A0, MT, D)
            mem_in = load_now("mem_in", memr, I["mem_2"][0].rearrange("(t p) d -> p t d", p=P))
            memT = parts(A0 + 2048, A0 + 4096, KD, NM)
            xk = work(A0 + 6144, KD, NM)
            xv = work(A0 + 8192, MT, D)
            xq = work(A0 + 10240, KD, S)
            low_x = act_parts(A0 + 14336)

            def mem_dve(dve, ch):
                dve.wait_ge(*mem_in)
            stage(None, None, mem_dve)
            norm_stage(memr, memT, G_MEM, MT, work(A0 + 6144, 4 * D))
            early = []
            norm_stage(x, low_x, G_X, NT, work(A0 + 6144, 4 * D), early)
            gr = Groups(20, "AV")
            jobs = []
            wkv, wq = I["w_xkv_2"][0], I["w_xq_2"][0]

            def cols_to(v, c):
                return lambda r: v[:, 4 * c + r, :]

            def rows_to(v, c):
                return lambda r: v[:, r, c * 512:c * 512 + 512]
            for c in range(2):
                jobs.append((Cols(gr, 4 * c, memT, NM, [(kpc(wkv[:, c * 512:c * 512 + 512]), 0)]), cols_to(xk, c), 1.0))
            for c in range(2):
                jobs.append((Rows(gr, 8 + 2 * c, memT, MT, [(kpc(wkv[:, D + c * 512:D + c * 512 + 512]), 0)], 512),
                             rows_to(xv, c), 1.0))
            for c in range(2):
                jobs.append((Cols(gr, 12 + 4 * c, low_x, S, [(kpc(wq[:, c * 512:c * 512 + 512]), 0)]),
                             cols_to(xq, c), 1.0))
            ahead(early, jobs[0][0].w)
            plain_stage(jobs, gr)

            def sc_x(pe, v, b, pre0):
                h, i = divmod(v, NT)
                for k in range(2):
                    m = pe.matmul(ps[:, b, 0:NM], xq[:, 2 * h + k, i * P:i * P + P], xk[:, 2 * h + k, :],
                                  start=(k == 0), stop=(k == 1))
                return m
            attention(LH * NT, lambda v: NM, sc_x, lambda u, j: xv[:, j, (u // NT) * DH:(u // NT) * DH + DH], DH,
                      lambda h, i: orow[:, i, h * DH:h * DH + DH], DH ** -0.5)
            out_stage(orow, I["w_xo_2"][0])

        if on(7):
            low_x = act_parts(A0)
            xn = moe(0, NT, D)
            LG = moe(4096, NT, NGR + NE)
            OB = moe(4240, D)
            XT = moe(5264, KD, P)
            OH = moe(6288, NT, P)
            HS = moe(6800, 512)
            HB = moe(7312, 512)
            HT = moe(7824, 4, P)
            gmoe = moe(8336, D)
            gfin = moe(9360, D)
            A2 = moe(10384, 2 * NT, NE)
            As = moe(10640, NT, NE)
            RK = moe(10768, NT, NE)
            T32 = moe(11280, NT, NE)
            T4 = moe(11408, NT, NGR)
            GO = moe(11424, NT, NGR)
            s1 = moe(11440, 16, NT)
            gate = moe(11504, 2, NT)
            rowi = moe(11512, 2, NT)
            rowu = sb("rowu", [P, 2 * NT], U32)
            cnt = moe(11520, NE)
            flg = moe(11552, 3, NE)
            pos = moe(11648, 3, NE)
            t96 = moe(11840, 3, NE)
            codee = moe(11936, 3, NE)
            codeb = moe(12032, 3, NE)
            val = moe(12128, 16)
            vsh = moe(12144, NOVER)
            rkq = moe(12152, NT, 1)
            rbase = moe(12160, 4, NE)
            zrow = moe(12288, D)
            early = []
            norm_stage(x, low_x, G_MOE, NT, moe(4240, 4 * D), early)
            gmoe_in = load_now("gmoe_in", gmoe, every(I["norm_moe_g_2"][0]))
            gfin_in = load_now("gfin_in", gfin, every(I["norm_f_g_2"]))
            gr = Groups(4, "V")
            loads = [(kpc(I["w_rg_2"][0]), 0), (kpc(I["w_re_2"][0]), NGR)]
            rj = Rows(gr, 0, low_x, NT, loads, NGR + NE)
            ahead(early, rj.w)
            moe_bar = len(stages)
            v0, a0, t0 = use(midv, 2), use(mida, 1), use(tr, 1)

            def b3(v, n):
                return v.rearrange("p (a o) -> p a o", o=1).to_broadcast([P, v.shape[1], n])

            def first_of(dve, ch, oh, vals, m, n, tmpv):
                ch(dve.tensor_reduce(m, vals, AX, ALU.max))
                ch(dve.tensor_tensor(oh, vals, b3(m, n), ALU.is_equal))
                ch(dve.tensor_tensor(oh, oh, desc[:, NE - n:NE].rearrange("p (o c) -> p o c", o=1
                                                                          ).to_broadcast([P, NT, n]), ALU.mult))
                ch(dve.tensor_reduce(tmpv, oh, AX, ALU.max))
                ch(dve.tensor_tensor(oh, oh, b3(tmpv, n), ALU.is_equal))

            def rt_pe(pe, ch):
                rj.pe(pe)
                pe.wait_ge(midv, v0 + 2)
                for t in range(NT):
                    for j in range(t + 1):
                        m = pe.matmul(ps[:, 4, t * NE:t * NE + NE], (tri if j == t else ones)[:, :], As[:, j, :],
                                      start=(j == 0), stop=(j == t))
                for j in range(NT):
                    m = pe.matmul(ps[:, 5, 0:NE], ones[:, :], As[:, j, :], start=(j == 0), stop=(j == NT - 1))
                m.then_inc(tr, 1)

            rsp = Split([rj])

            def rt_act(act, ch):
                rsp.start(act)
                for t in range(NT):
                    act.mul(xn[:, t, :], x[:, t, :], ss[:, t:t + 1]).then_inc(xsd, 1)
                act.wait_ge(midv, v0 + 1)
                ch(act.activation(T4, T4, ACT.Exp))
                act.activation(s1[:, 5, :], s1[:, 5, :], ACT.Exp).then_inc(mida, 1)
            xn0 = use(xsd, NT)

            z_in = sem("z_in")

            def rt_po(po, ch):
                ch(po.memset(zrow, 0.0))
                for q in range(NOVER):
                    po.dma_start(obuf[(NE + q) * P:(NE + q + 1) * P, :], zrow).then_inc(z_in, 16)
                po.wait_ge(xsd, xn0 + NT)
                po.wait_ge(*gmoe_in)
                ch(po.tensor_tensor(xn, xn, gmoe.rearrange("p (o c) -> p o c", o=1).to_broadcast([P, NT, D]),
                                    ALU.mult))

            def rt_dve(dve, ch):
                rsp.start(dve)
                for t in range(NT):
                    rj.ready(dve, t)
                    dve.tensor_tensor(LG[:, t, :], rj.src(t), rbias[:, :], ALU.add).then_inc(ev, 1)
                gr.wait_taken(dve, NT - 1)
                G, Ee = LG[:, :, 0:NGR], LG[:, :, NGR:NGR + NE]
                m1, m2, gm_, w_ = s1[:, 0, :], s1[:, 1, :], s1[:, 2, :], s1[:, 3, :]
                first_of(dve, ch, GO, G, gm_, NGR, w_)
                ch(dve.tensor_tensor(T4, G, b3(gm_, NGR), ALU.subtract))
                ch(dve.tensor_scalar(GO, GO, 1.0, 1e30, ALU.subtract, ALU.mult))
                Eg = Ee.rearrange("p t (g e) -> p t g e", e=EPG)
                for g in range(NGR):
                    ch(dve.tensor_tensor(Eg[:, :, g, :], Eg[:, :, g, :],
                                         GO[:, :, g:g + 1].to_broadcast([P, NT, EPG]), ALU.add))
                first_of(dve, ch, A2[:, 0:NT, :], Ee, m1, NE, w_)
                ch(dve.scalar_tensor_tensor(out=T32, in0=A2[:, 0:NT, :], scalar=-2e30, in1=Ee,
                                            op0=ALU.mult, op1=ALU.add))
                first_of(dve, ch, A2[:, NT:2 * NT, :], T32, m2, NE, w_)
                dve.tensor_tensor(s1[:, 5, :], m2, m1, ALU.subtract).then_inc(midv, 1)
                dve.tensor_tensor(As, A2[:, 0:NT, :], A2[:, NT:2 * NT, :], ALU.add).then_inc(midv, 1)
                dve.wait_ge(midv, v0 + 2)
                dve.wait_ge(mida, a0 + 1)
                ch(dve.tensor_reduce(s1[:, 6, :], T4, AX, ALU.add))
                ch(dve.tensor_scalar(s1[:, 7, :], s1[:, 5, :], 1.0, None, ALU.add))
                ch(dve.tensor_tensor(s1[:, 6, :], s1[:, 6, :], s1[:, 7, :], ALU.mult))
                ch(dve.reciprocal(gate[:, 0, :], s1[:, 6, :]))
                ch(dve.tensor_tensor(gate[:, 1, :], gate[:, 0, :], s1[:, 5, :], ALU.mult))
                dve.wait_ge(tr, t0 + 1)
                rk = ps[:, 4, 0:NT * NE].rearrange("p (t e) -> p t e", t=NT)
                ch(dve.tensor_tensor(RK, As, rk, ALU.mult))
                ch(dve.tensor_copy(cnt, ps[:, 5, 0:NE]))
                for b in range(3):
                    ch.mark(dve.tensor_scalar(flg[:, b, :], cnt, 128.0 * (b + 1) + 0.5, None, ALU.is_gt))
                    ch.mark(dve.tensor_copy(codee[:, b, :], eidx[:, :]))
                    ch.mark(dve.memset(codeb[:, b, :], 128.0 * (b + 1)))
                ch.mark(dve.memset(val, 0.0))
                ch.wait()
                f1, p1, q1, ce, cb = (v.rearrange("p b e -> p (b e)") for v in (flg, pos, t96, codee, codeb))
                ch(dve.tensor_tensor_scan(p1, ones[:, 0:96], f1, 0.0, ALU.mult, ALU.add))
                ch(dve.tensor_copy(val[:, 0:1], p1[:, 95:96]))
                ch(dve.tensor_tensor(p1, p1, f1, ALU.mult))
                for q in range(NOVER):
                    for c1, to in ((ce, val[:, 1 + q:2 + q]), (cb, vsh[:, q:q + 1])):
                        ch(dve.scalar_tensor_tensor(out=q1, in0=p1, scalar=float(q + 1), in1=c1,
                                                    op0=ALU.is_equal, op1=ALU.mult))
                        ch(dve.tensor_reduce(to, q1, AX, ALU.add))
                ch(dve.tensor_copy(ft[0:1, :], val[0:1, :]))
                ch.mark(dve.tensor_scalar(rbase[:, 0, :], eidx[:, :], float(P), None, ALU.mult))
                for b in range(3):
                    ch.mark(dve.tensor_scalar(rbase[:, 1 + b, :], pos[:, b, :], float(P),
                                              float((NE - 1) * P - P * (b + 1)), ALU.mult, ALU.add))
                ch.wait()
                for b in (3, 2, 1):
                    ch(dve.tensor_tensor(rbase[:, b, :], rbase[:, b, :], rbase[:, b - 1, :], ALU.subtract))
                for k in range(2):
                    A = A2[:, NT * k:NT * k + NT, :]
                    rank, part, row = s1[:, 9, :], s1[:, 8, :], rowi[:, k, :]
                    ch(dve.tensor_tensor(T32, A, RK, ALU.mult))
                    ch(dve.tensor_reduce(rank, T32, AX, ALU.add))
                    ch(dve.tensor_scalar(row, rank, 1.0, None, ALU.subtract))
                    for b in range(4):
                        ch(dve.tensor_tensor(T32, A, rbase[:, b:b + 1, :].to_broadcast([P, NT, NE]), ALU.mult))
                        ch(dve.tensor_reduce(part, T32, AX, ALU.add))
                        if b:
                            ch(dve.scalar_tensor_tensor(out=part, in0=rank, scalar=P * b + 0.5, in1=part,
                                                        op0=ALU.is_gt, op1=ALU.mult))
                        ch(dve.tensor_tensor(row, row, part, ALU.add))
                ch(dve.tensor_copy(rowu[:, :].rearrange("p (k t) -> p k t", k=2), rowi))
            stage(rt_pe, rt_act, rt_dve, rt_po)

            def w1v(s):
                return ring[s].rearrange("p (k c) -> p k c", c=EF)

            def w2v(s):
                return ring[s].rearrange("p (k c) -> p k c", c=D)

            def after(n):
                return not (isinstance(n, int) and n == 0)

            def onehot(dve, n, col):
                rk = RK[:, :, bass.ds(col, 1)]
                dve.tensor_tensor(OH, rank1[:, :].rearrange("p (o c) -> p o c", o=1).to_broadcast([P, NT, P]),
                                  rk.to_broadcast([P, NT, P]), ALU.is_equal).then_inc(m_oh, 1)
            def gather(pe, n):
                pe.wait_ge(m_oh, n + 1)
                for k in range(KD):
                    for t in range(NT):
                        m = pe.matmul(ps[:, k // 4, (k % 4) * P:(k % 4) * P + P], xn[:, t, k * P:k * P + P],
                                      OH[:, t, :], start=(t == 0), stop=(t == NT - 1))
                    if k % 4 == 3:
                        m.then_inc(m_gx, 1)

            def up(pe, n, par, load):
                pe.wait_ge(m_gxa, n + 1)
                pe.wait_ge(m_gxv, n + 1)
                if after(n):
                    pe.wait_ge(m_hb, n)
                for j in range(2):
                    pe.wait_ge(w_moe[3 * par + j], 16 * load)
                    for k in range(KD):
                        m = pe.matmul(ps[:, 2 + j, :], XT[:, k, :], w1v(3 * par + j)[:, k, :],
                                      start=(k == 0), stop=(k == KD - 1))
                    m.then_inc(m_up, 1)

            def down(pe, n, par, load):
                pe.wait_ge(m_hb, n + 1)
                for j in range(4):
                    m = pe.transpose(ps[:, 4, j * P:j * P + P], HB[:, j * P:j * P + P], ident[:, :])
                m.then_inc(m_tr, 1)
                pe.wait_ge(m_hT, n + 1)
                pe.wait_ge(w_moe[3 * par + 2], 16 * load)
                if after(n):
                    pe.wait_ge(m_oa, n)
                    pe.wait_ge(m_ov, n)
                for h in range(2):
                    for k in range(4):
                        m = pe.matmul(ps[:, 5 + h, :], HT[:, k, :], w2v(3 * par + 2)[:, k, h * 512:h * 512 + 512],
                                      start=(k == 0), stop=(k == 3))
                m.then_inc(m_dn, 1)

            def cols_a(act, n):
                act.wait_ge(m_gx, n * 2 + 1)
                act.activation(XT[:, 0:4, :], ps[:, 0, :].rearrange("p (k s) -> p k s", k=4),
                               ACT.Copy).then_inc(m_gxa, 1)

            def cols_v(dve, n):
                dve.wait_ge(m_gx, n * 2 + 2)
                dve.tensor_copy(XT[:, 4:8, :], ps[:, 1, :].rearrange("p (k s) -> p k s", k=4)).then_inc(m_gxv, 1)

            def silu_a(act, n):
                act.wait_ge(m_up, n * 2 + 1)
                if after(n):
                    act.wait_ge(m_hb, n)
                act.activation(HS, ps[:, 2, :], ACT.Silu).then_inc(m_si, 1)

            def gated_v(dve, n):
                dve.wait_ge(m_up, n * 2 + 2)
                dve.wait_ge(m_si, n + 1)
                if after(n):
                    dve.wait_ge(m_tr, n)
                dve.tensor_tensor(HB, HS, ps[:, 3, :], ALU.mult).then_inc(m_hb, 1)

            def out_a(act, n, row):
                act.wait_ge(m_tr, n + 1)
                act.activation(HT, ps[:, 4, :].rearrange("p (k s) -> p k s", k=4), ACT.Copy).then_inc(m_hT, 1)
                act.wait_ge(m_dn, n + 1)
                if after(n):
                    act.wait_ge(m_st, n * 16)
                act.activation(OB[:, 0:512], ps[:, 5, :], ACT.Copy).then_inc(m_oa, 1)
                act.wait_ge(m_oa, n + 1)
                act.wait_ge(m_ov, n + 1)
                act.dma_start(obuf[bass.ds(row, P), :], OB).then_inc(m_st, 16)

            def out_v(dve, n):
                dve.wait_ge(m_dn, n + 1)
                if after(n):
                    dve.wait_ge(m_st, n * 16)
                dve.tensor_copy(OB[:, 512:1024], ps[:, 6, :]).then_inc(m_ov, 1)

            m_rk = sem("m_rk")

            def over(eng, body):
                n_over = eng.value_load(ft[0:1, 0:1], min_val=0, max_val=NOVER)
                for q in range(NOVER):
                    with eng.If(n_over > q):
                        body(q, NE + q)

            def expert_of(eng, q):
                return eng.value_load(ft[0:1, 1 + q:2 + q], min_val=0, max_val=NE - 1)

            def ex_pe(pe, ch):
                gather(pe, 0)
                for n in range(2):
                    up(pe, n, n, 1)
                    gather(pe, n + 1)
                    down(pe, n, n, 1)
                with pe.Fori(1, NE // 2 - 1) as i:
                    for par in range(2):
                        n = i * 2 + par
                        up(pe, n, par, i + 1)
                        gather(pe, n + 1)
                        down(pe, n, par, i + 1)
                up(pe, NE - 2, 0, NE // 2)
                gather(pe, NE - 1)
                down(pe, NE - 2, 0, NE // 2)
                up(pe, NE - 1, 1, NE // 2)
                down(pe, NE - 1, 1, NE // 2)

                def body(q, n):
                    gather(pe, n)
                    up(pe, n, 0, NE // 2 + 1 + q)
                    down(pe, n, 0, NE // 2 + 1 + q)
                over(pe, body)

            def ex_act(act, ch):
                cols_a(act, 0)
                silu_a(act, 0)
                cols_a(act, 1)
                out_a(act, 0, 0)
                with act.Fori(1, NE - 1) as n:
                    silu_a(act, n)
                    cols_a(act, n + 1)
                    out_a(act, n, n * P)
                silu_a(act, NE - 1)
                out_a(act, NE - 1, (NE - 1) * P)

                def body(q, n):
                    cols_a(act, n)
                    silu_a(act, n)
                    out_a(act, n, n * P)
                    act.wait_ge(m_st, 16 * (n + 1))
                act.wait_ge(m_st, 16 * NE)
                act.wait_ge(z_in, 16 * NOVER)
                over(act, body)

            def ex_dve(dve, ch):
                onehot(dve, 0, 0)
                cols_v(dve, 0)
                onehot(dve, 1, 1)
                gated_v(dve, 0)
                cols_v(dve, 1)
                onehot(dve, 2, 2)
                out_v(dve, 0)
                with dve.Fori(1, NE - 2) as n:
                    gated_v(dve, n)
                    cols_v(dve, n + 1)
                    onehot(dve, n + 2, n + 2)
                    out_v(dve, n)
                gated_v(dve, NE - 2)
                cols_v(dve, NE - 1)
                out_v(dve, NE - 2)
                gated_v(dve, NE - 1)
                out_v(dve, NE - 1)

                def body(q, n):
                    e = expert_of(dve, q)
                    dve.tensor_scalar(rkq, RK[:, :, bass.ds(e, 1)], vsh[:, q:q + 1], None,
                                      ALU.subtract).then_inc(m_rk, 1)
                    dve.wait_ge(m_rk, q + 1)
                    dve.tensor_tensor(OH, rank1[:, :].rearrange("p (o c) -> p o c", o=1).to_broadcast([P, NT, P]),
                                      rkq.to_broadcast([P, NT, P]), ALU.is_equal).then_inc(m_oh, 1)
                    cols_v(dve, n)
                    gated_v(dve, n)
                    out_v(dve, n)
                over(dve, body)
            stage(ex_pe, ex_act, ex_dve)

            gbuf = area(0, 0, 4, D)
            fsq = area(0, 4 * D, D)
            ss5, rs5, u5 = use(ssd, NT), use(rsd, NT), use(xsd, NT)

            def fin_po(po, ch):
                for t in range(NT):
                    for k in range(2):
                        if t >= 2:
                            po.wait_ge(g_use, 2 * (t - 2) + k + 1)
                        j = 2 * (t % 2) + k
                        po.indirect_dma_start(
                            out=gbuf[:, j, :], out_offset=None, in_=obuf,
                            in_offset=bass.IndirectOffsetOnAxis(ap=rowu[:, k * NT + t:k * NT + t + 1], axis=0),
                        ).then_inc(g_in[j], 16)
                for t in range(NT):
                    po.wait_ge(ssd, ss5 + t + 1)
                    v = ss[:, t:t + 1]
                    ch(po.tensor_scalar(v, v, 1.0 / D, EPS, ALU.mult, ALU.add))
                    po.tensor_tensor(v, v, nhalf[:, :], ALU.pow).then_inc(rsd, 1)

            def fin_dve(dve, ch):
                for t in range(NT):
                    for k in range(2):
                        j = 2 * (t % 2) + k
                        dve.wait_ge(g_in[j], 16 * (t // 2 + 1))
                        if k:
                            dve.wait_ge(g_use, 2 * t + 1)
                        dve.scalar_tensor_tensor(out=x[:, t, :], in0=gbuf[:, j, :], scalar=gate[:, k, t:t + 1],
                                                 in1=x[:, t, :], op0=ALU.mult, op1=ALU.add).then_inc(g_use, 1)
                dve.wait_ge(*gfin_in)
                for t in range(NT):
                    dve.wait_ge(rsd, rs5 + t + 1)
                    dve.scalar_tensor_tensor(out=x[:, t, :], in0=x[:, t, :], scalar=ss[:, t:t + 1], in1=gfin,
                                             op0=ALU.mult, op1=ALU.mult).then_inc(xsd, 1)

            def fin_act(act, ch):
                for t in range(NT):
                    act.wait_ge(g_use, 2 * t + 2)
                    if t:
                        act.wait_ge(ssd, ss5 + t)
                    act.activation(fsq, x[:, t, :], ACT.Square, accum_out=ss[:, t:t + 1]).then_inc(ssd, 1)
            last_x = (xsd, u5)
            last_stage = len(stages)
            stage(None, fin_act, fin_dve, fin_po)

        block = ctx.enter_context(nc.Block())

        def run(eng, which, chain):
            ch = Chain(eng, chain)
            for n, st_ in enumerate(stages):
                if which == 3:
                    for at, dst, src, s in late:
                        if at == n:
                            eng.dma_start(dst, src).then_inc(s, 16)
                if st_[which]:
                    st_[which](eng, ch)
                eng.drain().then_inc(phase, 1)
                eng.wait_ge(phase, 4 * (n + 1))

        @block.tensor
        def _(pe):
            run(pe, 0, phase)

        @block.scalar
        def _(act):
            run(act, 1, ach)

        @block.vector
        def _(dve):
            run(dve, 2, vch)

        @block.gpsimd
        def _(po):
            run(po, 3, pch)

        @block.sync
        def _(sp):
            for dst, src in crows:
                sp.dma_start(dst, src).then_inc(cst, 16)
            with nc.allow_non_contiguous_dma(reason="512 positions, once"):
                sp.dma_start(posi[:, :].rearrange("p (t a) -> p t a", a=1),
                             I["positions"][0].rearrange("(t p a) -> p t a", p=P, a=1)).then_inc(cst, 16)
            sp.dma_start(x[:, :, :], I["x"][0].rearrange("(t p) d -> p t d", p=P)).then_inc(xin, 16)
            for c, (loads, kt, n, _) in enumerate(chunks):
                if c >= NS:
                    sp.wait_ge(w_lo, chunks[c - NS][3])
                v = ring[c % NS][:, :kt * n].rearrange("p (k c) -> p k c", c=n)
                for src, c0 in loads:
                    with nc.allow_non_contiguous_dma(reason="narrow weights: gates and router"):
                        sp.dma_start(v[:, :, c0:c0 + src.shape[2]], src).then_inc(w_full[c % NS], 16)
            if on(7):
                def load(e, par):
                    for j, name in enumerate(("w1_2", "w3_2", "w2_2")):
                        v = (w2v if j == 2 else w1v)(3 * par + j)
                        src = I[name][0, bass.ds(e, 1)].rearrange("o (k p) c -> p (o k) c", p=P)
                        sp.dma_start(v, src).then_inc(w_moe[3 * par + j], 16)
                sp.wait_ge(w_lo, chunks[-1][3])
                load(0, 0)
                sp.wait_ge(phase, 4 * (moe_bar + 1))
                load(1, 1)
                with sp.Fori(1, NE // 2) as i:
                    for par in range(2):
                        sp.wait_ge(m_dn, i * 2 + (par - 1))
                        load(i * 2 + par, par)
                n_over = sp.value_load(ft[0:1, 0:1], min_val=0, max_val=NOVER)
                for q in range(NOVER):
                    with sp.If(n_over > q):
                        sp.wait_ge(m_dn, NE + q)
                        load(expert_of(sp, q), 0)
                for t in range(NT):
                    sp.wait_ge(xsd, last_x[1] + t + 1)
                    sp.dma_start(out[0, t * P:(t + 1) * P, :], x[:, t, :]).then_inc(out_s, 16)
            else:
                sp.wait_ge(phase, 4 * len(stages))
                for t in range(NT):
                    sp.dma_start(out[0, t * P:(t + 1) * P, :], x[:, t, :]).then_inc(out_s, 16)
            sp.wait_ge(out_s, 16 * NT)


_INS = [
    "x", "positions", "l0_attn_norm", "l0_w_in", "l0_mla_q_a_norm", "l0_mla_w_q_up", "l0_mla_kv_a_norm",
    "l0_mla_w_kv_up", "l0_mla_q_norm", "l0_mla_k_norm", "l0_w_o", "l0_ffn_norm", "l0_w_gate", "l0_w_up",
    "l0_w_down", "l1_attn_norm", "l1_w_in", "l1_fox_f_bias", "l1_fox_q_norm", "l1_fox_k_norm", "l1_w_o",
    "l1_ffn_norm", "l1_w_gate", "l1_w_up", "l1_w_down", "mem_2", "norm_mix_g_2", "w_in_2", "b_gate_2", "b_if_2",
    "conv_w_2", "conv_b_2", "mh_norm_g_2", "sgu_norm_g_2", "w_s_2", "b_s_2", "w_out_2", "norm_x_g_2",
    "norm_mem_g_2", "w_xq_2", "w_xkv_2", "w_xo_2", "norm_moe_g_2", "w_rg_2", "b_rg_2", "w_re_2", "b_re_2", "w1_2",
    "w3_2", "w2_2", "norm_f_g_2",
]


def kernel(**inputs):
    import numpy as _np
    import concourse.bacc as _bacc
    from concourse import mybir as _mybir
    from concourse.bass_utils import run_bass_kernel_spmd as _run

    nc = _bacc.Bacc("TRN2", target_bir_lowering=False, num_devices=1)
    arrays, aps = {}, {}
    for name in _INS:
        a = _np.ascontiguousarray(inputs[name])
        arrays[f"in_{name}"] = a
        aps[name] = nc.dram_tensor(f"in_{name}", a.shape, _mybir.dt.from_np(a.dtype), kind="ExternalInput").ap()
    out = nc.dram_tensor("out", (1, S, D), _mybir.dt.float32, kind="ExternalOutput").ap()
    bass_two_blocks_kernel(nc, aps, out)
    r = _run(nc, [arrays], core_ids=[0])
    return r.results[0]["out"]
```

```python
from contextlib import ExitStack

import numpy as np

import concourse.bass as bass
from concourse import mybir

F32 = mybir.dt.float32
I32 = mybir.dt.int32
F32R = mybir.dt.float32r
U32 = mybir.dt.uint32
ALU = mybir.AluOpType
ACT = mybir.ActivationFunctionType
AX = mybir.AxisListType.X

P = 128
S = 512
NT = S // P
D = 1024
KD = D // P
EPS = 1e-6
NEG = -1e30
BANK = 512
NBANK = 8
SLOT = 4096
NS = 3
PIECE = 2048
MP = 1024
NMB = 6
NPC = 3 * SLOT // MP
PM = NPC // 3
QR, KVR, RO, NOPE, MV = 256, 128, 32, 64, 64
QK = NOPE + RO
MH = 8
HALF = RO // 2
C0 = QR + KVR + RO
SBW = 512
FF = 2816
FT = FF // P
FC = FF // 256
FH = 16
LH = 4
DH = 256
NM = 256
MT = NM // P
G8 = 8
NE = 32
NGR = 4
EPG = NE // NGR
EF = 512
NOVER = 7

START, END = 1, 7


class Pair:

    def __init__(self, high, low):
        self.h, self.l, self.high_f = high, low, high.bitcast(F32)

    def __getitem__(self, at):
        return Pair(self.h[at], self.l[at])


class Chain:

    def __init__(self, eng, sem):
        self.eng, self.sem, self.n = eng, sem, 0

    def mark(self, ins):
        self.n += 1
        ins.then_inc(self.sem, 1)

    def wait(self, n=None):
        self.eng.wait_ge(self.sem, self.n if n is None else n)

    def __call__(self, ins):
        self.mark(ins)
        self.wait()


def two_pi():
    c1 = 201.0 / 32.0
    c2 = float(np.round((2.0 * np.pi - c1) * 2.0**20) / 2.0**20)
    return c1, c2, float(np.float32(2.0 * np.pi - c1 - c2))


def bass_two_blocks_kernel(nc, I, out):
    def on(n):
        return START <= n <= END

    ctx = ExitStack()

    def sb(name, shape, dt=F32):
        return ctx.enter_context(nc.sbuf_tensor(name, shape, dt))

    def sem(name):
        return ctx.enter_context(nc.semaphore(name))

    with ctx:
        x = sb("x", [P, NT, D])
        def sb_twice(name, shape):
            plain = sb(name, shape)
            at = nc.sbuf_base - 4 * int(np.prod(shape[1:]))
            return plain, nc.alloc_sbuf_tensor_at(name + "_parts", shape, F32R, offset=at)

        actT, actR = sb_twice("actT", [P, KD, S])
        orow = actT[:, :, :].rearrange("p (t a) s -> p t (a s)", t=NT)
        ident = sb("ident", [P, P])
        tri = sb("tri", [P, P])
        ones = sb("ones", [P, P])
        maskz = sb("maskz", [P, S])
        rank1 = sb("rank1", [P, P])
        gains = sb("gains", [P, 64])
        cols2 = sb("cols2", [P, 96])
        nhalf = sb("nhalf", [P, 1])
        desc = sb("desc", [P, NE])
        eidx = sb("eidx", [P, NE])
        ss = sb("ss", [P, 8])
        rx = sb("rx", [P, NT])
        rs = sb("rs", [P, 8])
        mx = sb("mx", [P, 8])
        bi = sb("bi", [P, 8])
        rinv = sb("rinv", [P, 8])
        em = sb("em", [P, 8])
        ffb = sb("ffb", [P, FH])
        bif = sb("bif", [P, 8])
        rbias = sb("rbias", [P, NGR + NE])
        qg = sb("qg", [P, 2, QK])
        ropec = sb("ropec", [P, NT, HALF])
        ropes = sb("ropes", [P, NT, HALF])
        posi = sb("posi", [P, NT], I32)
        CS = sb("CS", [P, NT, FH])
        FG = sb("FG", [P, 2, NT, FH])
        st = sb("st", [P, 128])
        ft = sb("ft", [1, 16], I32)
        free = (nc.sbuf_bytes_remaining // 4 - 64) // 64 * 64
        sb("arena", [P, free])
        arena = nc.sbuf_base - 4 * free
        placed = {}

        def area(base, off, *shape, dt=F32):
            n = int(np.prod(shape))
            assert base + off + n <= free, (off, n, free - base)
            at = (base + off, n, dt == F32R)
            if at not in placed:
                placed[at] = nc.alloc_sbuf_tensor_at(f"area{len(placed)}", [P, n], dt, offset=arena + 4 * (base + off))
            v = placed[at][:, :]
            if len(shape) == 2:
                v = v.rearrange("p (a b) -> p a b", b=shape[1])
            if len(shape) == 3:
                v = v.rearrange("p (a b c) -> p a b c", b=shape[1], c=shape[2])
            return v

        ring = [area(0, i * SLOT, SLOT) for i in range(NS)]

        def work(off, *shape):
            return area(NS * SLOT, off, *shape)

        def parts(high, low, *shape):
            return Pair(*(area(NS * SLOT, off, *shape, dt=F32R) for off in (high, low)))

        def act_parts(low):
            return Pair(actR[:, :, :], area(NS * SLOT, low, KD, S, dt=F32R))

        def moe(off, *shape):
            return area(NS * SLOT + NMB * 2 * MP, off, *shape)

        ps = ctx.enter_context(nc.psum_tensor("ps", [P, NBANK, BANK], F32))
        G_A0, G_F0, G_A1, G_F1, G_MIX, G_X, G_MEM, G_MOE = range(8)
        norm_names = ["l0_attn_norm", "l0_ffn_norm", "l1_attn_norm", "l1_ffn_norm",
                      "norm_mix_g_2", "norm_x_g_2", "norm_mem_g_2", "norm_moe_g_2"]
        CW, CB, QA, BS, FQ, FK = 0, 64, 80, 83, 91, 92

        w_full = [sem(f"w_full{i}") for i in range(NS)]
        w_moe = [sem(f"w_moe{i}") for i in range(3)]
        mm = sem("mm")
        tr = sem("tr")
        ea = sem("ea")
        ev = sem("ev")
        mida = sem("mida")
        midv = sem("midv")
        midp = sem("midp")
        ssd = sem("ssd")
        rsd = sem("rsd")
        xsd = sem("xsd")
        phase = sem("phase")
        vch, ach, pch = sem("vch"), sem("ach"), sem("pch")
        cst = sem("cst")
        xin = sem("xin")
        w_hi, w_lo = sem("w_hi"), sem("w_lo")
        pu = sem("pu")
        s_sc, s_mx, s_ex = sem("s_sc"), sem("s_mx"), sem("s_ex")
        s_pt, s_pe = sem("s_pt"), sem("s_pe")
        s_o, s_on = sem("s_o"), sem("s_on")
        s_pr, s_pre = sem("s_pr"), sem("s_pre")
        s_t1, s_sp, s_m1, s_w, s_m2 = sem("s_t1"), sem("s_sp"), sem("s_m1"), sem("s_w"), sem("s_m2")
        out_s = sem("out_s")
        m_oh, m_gx, m_gxh, m_gxl = sem("m_oh"), sem("m_gx"), sem("m_gxh"), sem("m_gxl")
        m_ra, m_rv, m_gt = sem("m_ra"), sem("m_rv"), sem("m_gt")
        m_si, m_hb, m_tr, m_hh, m_hl = sem("m_si"), sem("m_hb"), sem("m_tr"), sem("m_hh"), sem("m_hl")
        m_o, m_st = sem("m_o"), sem("m_st")
        x_hi, x_lo, x_use = sem("x_hi"), sem("x_lo"), sem("x_use")
        g_in = [sem(f"g_in{j}") for j in range(4)]
        g_use = sem("g_use")

        if on(7):
            obuf = nc.dram_tensor("expert_rows", [(NE + NOVER) * P, D], F32, kind="Internal").ap()

        counts = {}

        def use(s, n):
            b = counts.get(s.name, 0)
            counts[s.name] = b + n
            return b

        stages = []

        def stage(pe=None, act=None, dve=None, po=None):
            stages.append((pe, act, dve, po))

        chunks = []
        loads_at = [0] * NS
        pieces = []

        def kpc(w):
            return w.rearrange("(k p) c -> p k c", p=P)

        class Weights:

            def __init__(self, loads, kt, n, runs, last=True):
                slot = len(chunks) % NS
                loads_at[slot] += len(loads)
                self.runs, self.last, self.m0 = runs, last, use(mm, runs if last else 0)
                raw = ring[slot][:, :kt * n].rearrange("p (k c) -> p k c", c=n)
                count = -(-kt * n // PIECE)
                step = -(-kt // count)
                self.cuts = [(k, min(kt, k + step)) for k in range(0, kt, step)]
                self.at = len(pieces)
                self.begun = 0
                for i, (k0, k1) in enumerate(self.cuts):
                    b = len(pieces) % 2
                    used = (mm, self.m0 + runs) if last and i == len(self.cuts) - 1 else (pu, use(pu, 1) + 1)
                    pieces.append((raw[:, k0:k1, :], (w_full[slot], 16 * loads_at[slot]),
                                   parts(2 * b * PIECE, (2 * b + 1) * PIECE, k1 - k0, n), used))
                chunks.append((loads, kt, n, len(pieces)))

            def product(self, pe, operands, dst, free):
                for i, (k0, k1) in enumerate(self.cuts):
                    pe.wait_ge(w_lo, self.at + i + 1)
                    for r in range(self.runs):
                        if free and i == 0:
                            free(r)
                        for k in range(k0, k1):
                            a, b = operands(r, pieces[self.at + i][2], k - k0, k)
                            begin = free is not None and k == 0
                            end = self.last and k == self.cuts[-1][1] - 1
                            pe.matmul(dst(r), a.h, b.h, start=begin, stop=False)
                            pe.matmul(dst(r), a.l, b.h, start=False, stop=False)
                            m = pe.matmul(dst(r), a.h, b.l, start=False, stop=end)
                        if self.last and i == len(self.cuts) - 1:
                            m.then_inc(mm, 1)
                        elif r == self.runs - 1:
                            m.then_inc(pu, 1)

        def high(eng, p):
            raw, full, w, _ = pieces[p]
            eng.wait_ge(*full)
            if p >= 2:
                eng.wait_ge(*pieces[p - 2][3])
            if eng is nc.vector:
                eng.tensor_copy(w.h, raw).then_inc(w_hi, 1)
            else:
                eng.activation(w.h, raw, ACT.Copy).then_inc(w_hi, 1)

        def low(dve, p):
            raw, _, w, _ = pieces[p]
            dve.wait_ge(w_hi, p + 1)
            dve.tensor_tensor(w.l, raw, w.high_f, ALU.subtract).then_inc(w_lo, 1)

        class Split:

            def __init__(self, jobs):
                self.w = [job.w for job in jobs]

            def pieces(self, j, lo, hi):
                if j < len(self.w):
                    n = len(self.w[j].cuts)
                    yield from range(self.w[j].at + max(lo, self.w[j].begun), self.w[j].at + min(hi, n))

            def start(self, eng):
                self.do(eng, self.pieces(0, 0, 99))

            def before(self, eng, j):
                self.do(eng, self.pieces(j + 1, 0, 1))

            def after(self, eng, j):
                self.do(eng, self.pieces(j + 1, 1, 99))

            def do(self, eng, which):
                for p in which:
                    if eng is nc.vector:
                        low(eng, p)
                    else:
                        high(eng, p)

        def ahead(early, w):
            early.append(w)
            w.begun = 1

        def begin(dve, early):
            for w in early:
                high(dve, w.at)
                low(dve, w.at)

        class Groups:

            def __init__(self, n, who):
                self.who = [who[g % len(who)] for g in range(n)]
                sems = {"A": ea, "V": ev, "C": midv}
                base = {k: use(s, self.who.count(k)) for k, s in sems.items()}
                base["X"], sems["X"] = 0, None
                self.freed = []
                for k in self.who:
                    base[k] += 1
                    self.freed.append((sems[k], base[k]))

            def bank(self, g):
                return g % NBANK

            def wait_free(self, eng, g):
                if g >= NBANK:
                    eng.wait_ge(*self.freed[g - NBANK])

            def wait_taken(self, eng, g):
                eng.wait_ge(*self.freed[g])

        class Tail:

            def __init__(self, added):
                self.added, self.early = added, []
                self.ss0, self.rs0 = use(ssd, NT), use(rsd, NT)

            def act(self, act):
                for t in range(NT):
                    act.wait_ge(*self.added[t])
                    if t:
                        act.wait_ge(ssd, self.ss0 + t)
                    act.activation(work(A0 + 18432, D), x[:, t, :], ACT.Square,
                                   accum_out=rx[:, t:t + 1]).then_inc(ssd, 1)

            def po(self, po, ch):
                for t in range(NT):
                    po.wait_ge(ssd, self.ss0 + t + 1)
                    v = rx[:, t:t + 1]
                    ch(po.tensor_scalar(v, v, 1.0 / D, EPS, ALU.mult, ALU.add))
                    po.tensor_tensor(v, v, nhalf[:, :], ALU.pow).then_inc(rsd, 1)

        tails = []

        def norm_stage(src, dst, gain, tiles, buf, early=None):
            tail = tails.pop() if tails and src is x else None
            if tail:
                early_here, tail.early = (), early
            else:
                early_here = early if early is not None else ()
            diag = buf[:, 0:NT * P].rearrange("p (a b) -> p a b", b=P)
            junk = buf[:, D:2 * D]
            tmp = buf[:, 2 * D:4 * D].rearrange("p (a k s) -> p a k s", a=4, k=4)
            r = rx if src is x else ss
            ss0, rs0, tr0 = (0, 0, use(tr, 2 * tiles)) if tail else (use(ssd, tiles), use(rsd, tiles), use(tr, 2 * tiles))
            xs0 = use(xsd, tiles)
            gr = Groups(2 * tiles, "V")
            hi0, lo_v, lo_p = use(ea, 2 * tiles), use(midv, tiles), use(midp, tiles)

            def place(g):
                t, h = divmod(g, 2)
                return slice(None), slice(4 * h, 4 * h + 4), slice(t * P, t * P + P)

            def act(act, ch):
                if not tail:
                    for t in range(tiles):
                        if t:
                            act.wait_ge(ssd, ss0 + t)
                        act.activation(junk, src[:, t, :], ACT.Square, accum_out=r[:, t:t + 1]).then_inc(ssd, 1)
                for t in range(tiles):
                    if not tail:
                        act.wait_ge(rsd, rs0 + t + 1)
                    act.activation(diag[:, t, :], ident[:, :], ACT.Copy, scale=r[:, t:t + 1]).then_inc(xsd, 1)
                for g in range(2 * tiles):
                    act.wait_ge(ev, gr.freed[g][1])
                    act.activation(dst[place(g)].h, tmp[:, g % 4], ACT.Copy).then_inc(ea, 1)

            def low_part(eng, g, s):
                eng.wait_ge(ea, hi0 + g + 1)
                eng.wait_ge(ev, gr.freed[g][1])
                d = dst[place(g)]
                eng.tensor_tensor(d.l, tmp[:, g % 4], d.high_f, ALU.subtract).then_inc(s, 1)

            def po(po, ch):
                if not tail:
                    for t in range(tiles):
                        po.wait_ge(ssd, ss0 + t + 1)
                        v = r[:, t:t + 1]
                        ch(po.tensor_scalar(v, v, 1.0 / D, EPS, ALU.mult, ALU.add))
                        po.tensor_tensor(v, v, nhalf[:, :], ALU.pow).then_inc(rsd, 1)
                for g in range(1, 2 * tiles, 2):
                    low_part(po, g, midp)

            def pe(pe, ch):
                for t in range(tiles):
                    pe.wait_ge(xsd, xs0 + t + 1)
                    for h in range(2):
                        g = 2 * t + h
                        gr.wait_free(pe, g)
                        for j in range(4):
                            m = pe.matmul(ps[:, gr.bank(g), j * P:j * P + P],
                                          src[:, t, (4 * h + j) * P:(4 * h + j + 1) * P], diag[:, t, :],
                                          start=True, stop=True)
                        m.then_inc(tr, 1)

            def dve(dve, ch):
                begin(dve, early_here)
                for g in range(2 * tiles + 1):
                    if g < 2 * tiles:
                        h = g % 2
                        dve.wait_ge(tr, tr0 + g + 1)
                        if g >= 4:
                            dve.wait_ge(*((midp, lo_p + g // 2 - 1) if h else (midv, lo_v + g // 2 - 1)))
                        dve.tensor_tensor(tmp[:, g % 4], ps[:, gr.bank(g), :].rearrange("p (k s) -> p k s", k=4),
                                          gains[:, 8 * gain + 4 * h:8 * gain + 4 * h + 4].rearrange(
                                              "p (k o) -> p k o", o=1).to_broadcast([P, 4, P]),
                                          ALU.mult).then_inc(ev, 1)
                    if g % 2:
                        low_part(dve, g - 1, midv)
            stage(pe, act, dve, po)

        class Rows:

            def __init__(self, gr, g0, lhs, tiles, loads, n, kt=KD, blocks=1, more=False, past=False):
                self.gr, self.g0, self.lhs, self.tiles, self.n, self.blocks, self.past = (
                    gr, g0, lhs, tiles, n, blocks, past)
                self.w = Weights(loads, kt, n * blocks, tiles * blocks, last=not more)

            def operands(self, r, w, i, k):
                t, h = divmod(r, self.blocks)
                return self.lhs[:, k, t * P:t * P + P], w[:, i, h * self.n:(h + 1) * self.n]

            def pe(self, pe):
                self.w.product(pe, self.operands, self.src,
                               None if self.past else lambda r: self.gr.wait_free(pe, self.g0 + r))

            def ready(self, eng, r):
                eng.wait_ge(mm, self.w.m0 + r + 1)

            def src(self, r):
                return ps[:, self.gr.bank(self.g0 + r), 0:self.n]

        class Cols(Rows):

            def __init__(self, gr, g0, rhs, n, loads, cols=(0, 128, 256, 384)):
                self.gr, self.g0, self.rhs, self.n, self.tiles, self.past, self.cols = gr, g0, rhs, n, 4, False, cols
                self.w = Weights(loads, KD, 512, 4)

            def operands(self, r, w, i, k):
                return w[:, i, self.cols[r]:self.cols[r] + P], self.rhs[:, k, :]

        def take_act(act, src, dst, scale=1.0):
            act.activation(dst, src, ACT.Copy, scale=scale).then_inc(ea, 1)

        def take_dve(dve, src, dst):
            dve.tensor_copy(dst, src).then_inc(ev, 1)

        def plain_stage(jobs, gr):
            sp_ = Split([job for job, _, _ in jobs])

            def pe(pe, ch):
                for job, _, _ in jobs:
                    job.pe(pe)

            def moves(eng, who):
                sp_.start(eng)
                for j, (job, dst, scale) in enumerate(jobs):
                    sp_.before(eng, j)
                    for r in range(job.tiles):
                        if gr.who[job.g0 + r] == who:
                            job.ready(eng, r)
                            if who == "A":
                                take_act(eng, job.src(r), dst(r), scale)
                            else:
                                eng.tensor_scalar(dst(r), job.src(r), scale, None, ALU.mult).then_inc(ev, 1)
                    sp_.after(eng, j)
            stage(pe, lambda act, ch: moves(act, "A"), lambda dve, ch: moves(dve, "V"))

        def out_stage(src, wts):
            oT = parts(A0, A0 + 4096, KD, S)
            gt = Groups(8, "V")
            tr0, hi0 = use(tr, 8), use(ea, 8)
            gr = Groups(8, "V")
            jobs = [Rows(gr, 4 * c, oT, NT, [(kpc(wts[:, c * 512:c * 512 + 512]), 0)], 512) for c in range(2)]
            early = []
            ahead(early, jobs[0].w)
            sp_ = Split(jobs)

            def place(g):
                t, h = divmod(g, 2)
                return slice(None), slice(4 * h, 4 * h + 4), slice(t * P, t * P + P)

            def pe(pe, ch):
                for g in range(8):
                    t, h = divmod(g, 2)
                    for j in range(4):
                        m = pe.transpose(ps[:, g, j * P:j * P + P],
                                         src[:, t, (4 * h + j) * P:(4 * h + j + 1) * P], ident[:, :])
                    m.then_inc(tr, 1)

            def act(act, ch):
                for g in range(8):
                    act.wait_ge(tr, tr0 + g + 1)
                    act.activation(oT[place(g)].h, ps[:, g, :].rearrange("p (k s) -> p k s", k=4),
                                   ACT.Copy).then_inc(ea, 1)

            def dve(dve, ch):
                begin(dve, early)
                for g in range(8):
                    dve.wait_ge(ea, hi0 + g + 1)
                    d = oT[place(g)]
                    dve.tensor_tensor(d.l, ps[:, g, :].rearrange("p (k s) -> p k s", k=4), d.high_f,
                                      ALU.subtract).then_inc(ev, 1)
            stage(pe, act, dve)
            tail = Tail([gr.freed[4 + t] for t in range(NT)])
            tails.append(tail)

            def pe2(pe, ch):
                for job in jobs:
                    job.pe(pe)

            def act2(act, ch):
                sp_.start(act)
                for c in range(2):
                    sp_.before(act, c)
                    sp_.after(act, c)
                tail.act(act)

            def dve2(dve, ch):
                sp_.start(dve)
                for c, job in enumerate(jobs):
                    sp_.before(dve, c)
                    if c == 1:
                        begin(dve, tail.early)
                    for t in range(NT):
                        job.ready(dve, t)
                        xx = x[:, t, c * 512:c * 512 + 512]
                        dve.tensor_tensor(xx, xx, job.src(t), ALU.add).then_inc(ev, 1)
                    sp_.after(dve, c)
            stage(pe2, act2, dve2, tail.po)

        def ffn(gain, wg, wu, wd):
            runs = ((0, 6), (6, 11))
            low_x = act_parts(A0)
            gu = parts(A0 + 4096, A0 + 4096 + 12 * S, 12, S)
            sil = work(A0 + 4096 + 24 * S, 4, S)
            early = []
            norm_stage(x, low_x, gain, NT, work(A0 + 4096, 4 * D), early)
            gr = Groups(2 * FT + 16, "V")
            jobs, g = [], 0
            for c0, c1 in runs:
                for c in range(c0, c1):
                    jobs.append((Cols(gr, g, low_x, S, [(kpc(wg[:, 256 * c:256 * c + 256]), 0),
                                                        (kpc(wu[:, 256 * c:256 * c + 256]), 256)],
                                      (0, 256, 128, 384)), "up", 2 * c))
                    g += 4
                k0, k1 = 2 * c0, 2 * c1
                mid = (k0 + k1 + 1) // 2
                for h in range(2):
                    for a, b in ((k0, mid), (mid, k1)):
                        jobs.append((Rows(gr, g, gu[:, a - k0:, :], NT,
                                          [(kpc(wd[a * P:b * P, h * 512:h * 512 + 512]), 0)], 512, b - a,
                                          more=b < k1, past=a > k0), "down" if b == k1 else "more", h))
                    g += 4
            ahead(early, jobs[0][0].w)
            sp_ = Split([job for job, _, _ in jobs])
            si0 = use(mida, FT)
            tail = Tail([gr.freed[jobs[-1][0].g0 + t] for t in range(NT)])
            tails.append(tail)
            first = [0, runs[1][0] * 2]

            def pe(pe, ch):
                last = None
                for job, kind, _ in jobs:
                    if kind == "more" and last != "down":
                        gr.wait_taken(pe, job.g0 - 1)
                    job.pe(pe)
                    last = kind

            def act(act, ch):
                sp_.start(act)
                for j, (job, kind, f0) in enumerate(jobs):
                    sp_.before(act, j)
                    if kind == "up":
                        for q in range(2):
                            f = f0 + q
                            job.ready(act, 2 * q)
                            if f >= 4:
                                act.wait_ge(*(sil_used[f - 4]))
                            act.activation(sil[:, f % 4, :], job.src(2 * q), ACT.Silu).then_inc(mida, 1)
                    sp_.after(act, j)
                tail.act(act)
            sil_used = {}
            for job, kind, f0 in jobs:
                if kind == "up":
                    for q in range(2):
                        sil_used[f0 + q] = gr.freed[job.g0 + 2 * q + 1]

            def dve(dve, ch):
                sp_.start(dve)
                for j, (job, kind, f0) in enumerate(jobs):
                    sp_.before(dve, j)
                    if kind == "up":
                        for q in range(2):
                            f = f0 + q
                            d = gu[:, f - first[f >= first[1]], :]
                            s_ = sil[:, f % 4, :]
                            job.ready(dve, 2 * q + 1)
                            dve.wait_ge(mida, si0 + f + 1)
                            ch(dve.tensor_tensor(s_, s_, job.src(2 * q + 1), ALU.mult))
                            ch(dve.tensor_copy(d.h, s_))
                            dve.tensor_tensor(d.l, s_, d.high_f, ALU.subtract).then_inc(ev, 2)
                    elif kind == "down":
                        if j == len(jobs) - 1:
                            begin(dve, tail.early)
                        for t in range(NT):
                            job.ready(dve, t)
                            xx = x[:, t, f0 * 512:f0 * 512 + 512]
                            dve.tensor_tensor(xx, xx, job.src(t), ALU.add).then_inc(ev, 1)
                    sp_.after(dve, j)
            stage(pe, act, dve, tail.po)

        Pb = work(0, 4, 512)
        PT = work(2048, 2, 512)
        A0 = 4 * PIECE

        def causal(v):
            return (v % NT + 1) * P

        def value_bank(u, dv):
            return ps[:, 5 + u % 2, 0:dv]

        def col(v, u):
            return v[:, u % 8:u % 8 + 1]

        def attention(units, length, scores, values, dv, dst, scale, preps=(), fox=False, mlstm=None):
            sc0, mx0, ex0, pt0, pe0, o0, on0 = (use(s, units) for s in (s_sc, s_mx, s_ex, s_pt, s_pe, s_o, s_on))
            npr = units // NT if mlstm else len(preps)
            pr0, pre0 = use(s_pr, npr), use(s_pre, npr)
            t10, t2 = (use(s_t1, units), use(mida, units)) if mlstm else (0, 0)
            exponents, E = mlstm or (None, None)

            def pe(pe, ch):
                for v in range(units + 3):
                    for n, (at, _, blocks, _, _) in enumerate(preps):
                        if at == v:
                            if n:
                                pe.wait_ge(s_pre, pre0 + n)
                            for t, b in enumerate(blocks):
                                m = pe.transpose(ps[0:b.shape[1], 7, t * P:t * P + P], b, ident[:, :])
                            m.then_inc(s_pr, 1)
                    if mlstm and v < units and v % NT == 0:
                        if v:
                            pe.wait_ge(s_mx, mx0 + v)
                        exponents(pe, v // NT).then_inc(s_pr, 1)
                    if v < units:
                        if v >= 3:
                            pe.wait_ge(s_ex, ex0 + v - 2)
                        scores(pe, v, v % 3, pre0).then_inc(s_sc, 1)
                    if 2 <= v < units + 2:
                        u = v - 2
                        pe.wait_ge(s_ex, ex0 + u + 1)
                        if u >= 2:
                            pe.wait_ge(s_pe, pe0 + u - 1)
                        for j in range(length(u) // P):
                            m = pe.transpose(ps[:, 3 + u % 2, j * P:j * P + P],
                                             Pb[:, u % 4, j * P:j * P + P], ident[:, :])
                        m.then_inc(s_pt, 1)
                    if v >= 3:
                        u = v - 3
                        pe.wait_ge(s_pe, pe0 + u + 1)
                        if u >= 2:
                            pe.wait_ge(s_on, on0 + u - 1)
                        nb = length(u) // P
                        for j in range(nb):
                            m = pe.matmul(value_bank(u, dv), PT[:, u % 2, j * P:j * P + P], values(u, j),
                                          start=(j == 0), stop=(j == nb - 1))
                        m.then_inc(s_o, 1)

            def act(act, ch):
                for v in range(units + 2):
                    if v >= 2:
                        u = v - 2
                        act.wait_ge(s_pt, pt0 + u + 1)
                        if u >= 2:
                            act.wait_ge(s_o, o0 + u - 1)
                        L = length(u)
                        act.activation(PT[:, u % 2, 0:L], ps[:, 3 + u % 2, 0:L], ACT.Copy).then_inc(s_pe, 1)
                    for n, (at, done, _, d, gain) in enumerate(preps):
                        if at == v:
                            act.wait_ge(s_pr, pr0 + n + 1)
                            if done:
                                act.wait_ge(s_sc, sc0 + done)
                            act.activation(d, ps[0:d.shape[0], 7, :], ACT.Copy, scale=gain).then_inc(s_pre, 1)
                    if v < units:
                        L = length(v)
                        act.wait_ge(s_mx, mx0 + v + 1)
                        b = col(bi, v)
                        if mlstm:
                            e = E[:, v % 4, 0:L]
                            act.activation(e, e, ACT.Exp, bias=b).then_inc(s_t1, 1)
                            if v >= 8:
                                act.wait_ge(s_on, on0 + v - 7)
                            h, i = divmod(v, NT)
                            act.activation(col(em, v), b, ACT.Exp, bias=CS[:, i, h:h + 1]).then_inc(mida, 1)
                        else:
                            if v >= 4:
                                act.wait_ge(s_pt, pt0 + v - 3)
                            if v >= 8:
                                act.wait_ge(s_on, on0 + v - 7)
                            act.activation(Pb[:, v % 4, 0:L], ps[:, v % 3, 0:L], ACT.Exp, bias=b, scale=scale,
                                           accum_out=col(rs, v)).then_inc(s_ex, 1)

            def dve(dve, ch):
                for v in range(units + 4):
                    if v < units:
                        L = length(v)
                        h, i = divmod(v, NT)
                        m1, b, bank = col(mx, v), col(bi, v), ps[:, v % 3, 0:L]
                        if mlstm:
                            dve.wait_ge(s_pr, pr0 + h + 1)
                            if v >= 4:
                                dve.wait_ge(s_ex, ex0 + v - 3)
                            ch(dve.tensor_tensor_reduce(E[:, v % 4, 0:L], ps[:, 7, 0:L], maskz[:, S - L:S], 1.0, -3e38,
                                                        ALU.add, ALU.max, m1))
                            if v >= 8:
                                dve.wait_ge(mida, t2 + v - 7)
                            dve.tensor_scalar(b, m1, 0.0, -1.0, ALU.max, ALU.mult).then_inc(s_mx, 1)
                        else:
                            dve.wait_ge(s_sc, sc0 + v + 1)
                            if length is causal:
                                ch.mark(dve.tensor_tensor_reduce(bank, bank, maskz[:, S - L:S], 1.0, -3e38,
                                                                 ALU.add, ALU.max, m1))
                            else:
                                ch.mark(dve.tensor_reduce(m1, bank, AX, ALU.max))
                    at_max = ch.n
                    if mlstm and 1 <= v <= units:
                        u = v - 1
                        L = length(u)
                        dve.wait_ge(s_sc, sc0 + u + 1)
                        dve.wait_ge(s_t1, t10 + u + 1)
                        if u >= 4:
                            dve.wait_ge(s_pt, pt0 + u - 3)
                        dve.tensor_tensor_reduce(Pb[:, u % 4, 0:L], ps[:, u % 3, 0:L], E[:, u % 4, 0:L],
                                                 DH ** -0.5, 0.0, ALU.mult, ALU.add, col(rs, u)).then_inc(s_ex, 1)
                    if v >= 4:
                        u = v - 4
                        r, q = col(rinv, u), col(rs, u)
                        dve.wait_ge(s_ex, ex0 + u + 1)
                        if mlstm:
                            dve.wait_ge(mida, t2 + u + 1)
                            ch(dve.scalar_tensor_tensor(out=q, in0=q, scalar=-1.0, in1=q, op0=ALU.mult, op1=ALU.max))
                            ch(dve.tensor_scalar(q, q, col(em, u), None, ALU.max))
                        ch.mark(dve.reciprocal(r, q))
                    at_sum = ch.n
                    if v < units and not mlstm:
                        h, i = divmod(v, NT)
                        m1, b = col(mx, v), col(bi, v)
                        ch.wait(at_max)
                        if fox:
                            ch.mark(dve.tensor_scalar(m1, m1, scale, CS[:, i, h:h + 1], ALU.mult, ALU.subtract))
                            at_max = ch.n
                    if v >= 4:
                        u = v - 4
                        h, i = divmod(u, NT)
                        ch.wait(at_sum)
                        dve.wait_ge(s_o, o0 + u + 1)
                        dve.tensor_scalar(dst(h, i), value_bank(u, dv), col(rinv, u), None, ALU.mult).then_inc(s_on, 1)
                    if v < units and not mlstm:
                        h, i = divmod(v, NT)
                        if v >= 8:
                            dve.wait_ge(s_ex, ex0 + v - 7)
                        if fox:
                            ch.wait(at_max)
                            dve.tensor_scalar(b, m1, -1.0, CS[:, i, h:h + 1], ALU.mult,
                                              ALU.subtract).then_inc(s_mx, 1)
                        else:
                            dve.tensor_scalar(b, m1, -scale, None, ALU.mult).then_inc(s_mx, 1)
            stage(pe, act, dve)

        crow = work(0, 256)
        freq = work(256, HALF)
        ang = work(320, NT, HALF)
        angk = work(384, NT, HALF)
        posf = work(448, NT)
        crows = []
        for k, name in enumerate(norm_names):
            v = I[name] if len(I[name].shape) == 1 else I[name][0]
            crows.append((crow[8 * k:8 * k + 8, 0:P], v.rearrange("(k p) -> k p", p=P)))
        crows += [(crow[0:64, P:2 * P], I["conv_w_2"][0].rearrange("w (k p) -> (w k) p", p=P)),
                  (crow[CB:CB + 16, P:2 * P], I["conv_b_2"][0].rearrange("(k p) -> k p", p=P)),
                  (crow[QA:QA + 2, P:2 * P], I["l0_mla_q_a_norm"].rearrange("(k p) -> k p", p=P)),
                  (crow[QA + 2:QA + 3, P:2 * P], I["l0_mla_kv_a_norm"].rearrange("(k p) -> k p", p=P)),
                  (crow[BS:BS + 8, P:2 * P], I["b_s_2"][0])]
        for r, name in ((FQ, "l1_fox_q_norm"), (FK, "l1_fox_k_norm")):
            for h in range(2):
                crows.append((crow[r:r + 1, P + 64 * h:P + 64 * h + 64], I[name].rearrange("(k p) -> k p", p=64)))

        def every(v):
            return v.rearrange("(a n) -> a n", a=1).to_broadcast([P, v.shape[0]])

        crows += [(ffb[:, :], every(I["l1_fox_f_bias"])), (qg[:, 0, :], every(I["l0_mla_q_norm"])),
                  (qg[:, 1, :], every(I["l0_mla_k_norm"])), (bif[:, :], every(I["b_if_2"][0])),
                  (rbias[:, 0:NGR], every(I["b_rg_2"][0])), (rbias[:, NGR:], every(I["b_re_2"][0]))]

        def consts_po(po, ch):
            for m, val in ((ident, 0.0), (tri, 1.0), (ones, 1.0), (maskz, 0.0), (nhalf, -0.5)):
                ch.mark(po.memset(m[:, :], val))
            for j in range(HALF):
                ch.mark(po.memset(freq[:, j:j + 1], float(np.float32(10000.0) ** (-np.float32(j) / np.float32(HALF)))))
            ch.wait()
            ch.mark(po.affine_select(out=ident[:, :], in_=ident[:, :], compare_op=ALU.not_equal, fill=1.0,
                                     base=0, pattern=[[-1, P]], channel_multiplier=1))
            ch.mark(po.affine_select(out=tri[:, :], in_=tri[:, :], compare_op=ALU.is_ge, fill=0.0,
                                     base=0, pattern=[[1, P]], channel_multiplier=-1))
            ch.mark(po.affine_select(out=maskz[:, S - P:S], in_=maskz[:, S - P:S], compare_op=ALU.is_ge, fill=NEG,
                                     base=0, pattern=[[-1, P]], channel_multiplier=1))
            for v, step, n, b in ((rank1, 1, P, 1), (desc, -1, NE, NE), (eidx, 1, NE, 0)):
                ch.mark(po.iota(v[:, :], pattern=[[step, n]], base=b, channel_multiplier=0,
                                allow_small_or_imprecise_dtypes=True))
            ch.wait()
        stage(None, None, None, consts_po)

        tr_c, mv_c = use(tr, 1), use(midv, 1)

        def cols_pe(pe, ch):
            pe.wait_ge(cst, 16 * (len(crows) + 1))
            pe.transpose(ps[0:P, 0, 0:64], crow[0:64, 0:P], ident[0:64, 0:64])
            pe.transpose(ps[0:P, 1, 0:93], crow[0:93, P:2 * P], ident[0:93, 0:93]).then_inc(tr, 1)

        def cols_act(act, ch):
            act.wait_ge(midv, mv_c + 1)
            ch.mark(act.activation(ropes[:, :, :], ropes[:, :, :], ACT.Sin))
            ch(act.activation(ropec[:, :, :], ropec[:, :, :], ACT.Sin))

        def cols_dve(dve, ch):
            dve.wait_ge(cst, 16 * (len(crows) + 1))
            ch(dve.tensor_copy(posf, posi[:, :]))
            c1, c2, c3 = two_pi()
            ch(dve.tensor_tensor(ang, posf.rearrange("p (t o) -> p t o", o=1).to_broadcast([P, NT, HALF]),
                                 freq.rearrange("p (o h) -> p o h", o=1).to_broadcast([P, NT, HALF]), ALU.mult))
            magic = 1.5 * 2.0 ** 23
            ch(dve.tensor_scalar(angk, ang, float(np.float32(1 / (2 * np.pi))), magic, ALU.mult, ALU.add))
            ch(dve.tensor_scalar(angk, angk, magic, None, ALU.subtract))
            for c in (c1, c2, c3):
                ch(dve.scalar_tensor_tensor(out=ang, in0=angk, scalar=-c, in1=ang, op0=ALU.mult, op1=ALU.add))
            lim = 3.1415925
            ch(dve.tensor_scalar(ropes[:, :, :], ang, lim, -lim, ALU.min, ALU.max))
            ch(dve.scalar_tensor_tensor(out=ropec[:, :, :], in0=ropes[:, :, :], scalar=-1.0, in1=ropes[:, :, :],
                                        op0=ALU.mult, op1=ALU.max))
            dve.tensor_scalar(ropec[:, :, :], ropec[:, :, :], -1.0, float(np.float32(np.pi / 2)),
                              ALU.mult, ALU.add).then_inc(midv, 1)
            dve.wait_ge(tr, tr_c + 1)
            ch.mark(dve.tensor_copy(gains[:, :], ps[:, 0, 0:64]))
            ch(dve.tensor_copy(cols2[:, 0:93], ps[:, 1, 0:93]))
            ch.mark(dve.memset(cols2[64:65, FQ:FK + 1], 1.0))
            dve.wait_ge(xin, 16)
            ch.wait()
        stage(cols_pe, cols_act, cols_dve)

        def softplus_stages(n, cs_cols, extra=None):
            f, a = FG[:, 0, :, 0:n], FG[:, 1, :, 0:n]
            v0, a0, t0 = use(midv, 2), use(mida, 1), use(tr, 2 if cs_cols else 1)

            def dve(dve, ch):
                dve.scalar_tensor_tensor(out=a, in0=f, scalar=-1.0, in1=f, op0=ALU.mult, op1=ALU.max).then_inc(midv, 1)
                ch(dve.tensor_scalar(f, f, -1.0, 0.0, ALU.mult, ALU.max))
                dve.wait_ge(mida, a0 + 1)
                dve.tensor_tensor(f, f, a, ALU.add).then_inc(midv, 1)
                dve.wait_ge(tr, t0 + 1)
                ch(dve.tensor_copy(CS[:, :, 0:n], ps[:, 0, 0:NT * n].rearrange("p (t a) -> p t a", t=NT)))
                if extra:
                    extra(dve, ch)

            def act(act, ch):
                act.wait_ge(midv, v0 + 1)
                ch(act.activation(a, a, ACT.Exp, scale=-1.0))
                act.activation(a, a, ACT.Ln, bias=1.0).then_inc(mida, 1)

            def pe(pe, ch):
                pe.wait_ge(midv, v0 + 2)
                for t in range(NT):
                    for j in range(t + 1):
                        m = pe.matmul(ps[:, 0, t * n:t * n + n], (tri if j == t else ones)[:, :], FG[:, 0, j, 0:n],
                                      start=(j == 0), stop=(j == t))
                m.then_inc(tr, 1)
            stage(pe, act, dve)
            if not cs_cols:
                return
            src, dst, scale = cs_cols

            def pe2(pe, ch):
                for t in range(NT):
                    m = pe.transpose(ps[0:n, 1, t * P:t * P + P], src[:, t, 0:n], ident[:, :])
                m.then_inc(tr, 1)

            def act2(act, ch):
                act.wait_ge(tr, t0 + 2)
                ch(act.activation(dst, ps[0:n, 1, :], ACT.Copy, scale=scale))
            stage(pe2, act2)

        if on(1):
            cq0 = work(A0, NT, C0)
            sbq = work(A0 + 1664, NT, S)
            sbk = work(A0 + 3712, NT, S)
            sbv = work(A0 + 5760, NT, SBW)
            Qr = work(A0 + 7808, NT, MH * QK)
            Kr = work(A0 + 10880, NT, MH * QK)
            Vr = work(A0 + 13952, NT, MH * MV)
            QT = work(A0 + 16000, 2, 512)
            KT = work(A0 + 17024, 2, 512)
            low_x = act_parts(A0 + 7808)
            cqT = parts(A0 + 7808, A0 + 7808 + 3 * S, 3, S)
            sqq = work(0, NT * MH, QK)
            sqk = work(A0 + 16000 + 3072, NT * MH, HALF)
            early = []
            norm_stage(x, low_x, G_A0, NT, work(A0, 4 * D), early)
            gr = Groups(16, "AV")
            w = I["l0_w_in"]
            jobs = [
                (Rows(gr, 0, low_x, NT, [(kpc(w[:, 0:C0]), 0)], C0), lambda t: cq0[:, t, :], 1.0),
                (Cols(gr, 4, low_x, S, [(kpc(w[:, C0:C0 + SBW]), 0)]), lambda t: sbq[:, t, :], 64 ** -0.5),
                (Cols(gr, 8, low_x, S, [(kpc(w[:, C0 + SBW:C0 + 2 * SBW]), 0)]), lambda t: sbk[:, t, :], 1.0),
                (Rows(gr, 12, low_x, NT, [(kpc(w[:, C0 + 2 * SBW:C0 + 3 * SBW]), 0)], SBW),
                 lambda t: sbv[:, t, :], 1.0)]
            ahead(early, jobs[0][0].w)
            plain_stage(jobs, gr)

            ss0, rs0, xs0, tr0 = use(ssd, 1), use(rsd, 1), use(xsd, 4), use(tr, 4)
            gr1 = Groups(4, "V")
            hi1 = use(ea, 4)
            junk = work(0, D)
            ctmp = work(D, NT, 3 * P)

            def rank_act(act, ch):
                for t in range(NT):
                    ch(act.activation(junk[:, 0:QR], cq0[:, t, 0:QR], ACT.Square, accum_out=ss[:, t:t + 1]))
                    last = act.activation(junk[:, QR:QR + KVR], cq0[:, t, QR:QR + KVR], ACT.Square,
                                          accum_out=ss[:, 4 + t:5 + t])
                    if t < NT - 1:
                        ch(last)
                last.then_inc(ssd, 1)
                for t in range(NT):
                    act.wait_ge(midv, md1 + t + 1)
                    act.activation(cqT[:, :, t * P:t * P + P].h, ctmp[:, t, :].rearrange("p (k s) -> p k s", k=3),
                                   ACT.Copy).then_inc(ea, 1)
            md1 = use(midv, 4)

            def rank_po(po, ch):
                po.wait_ge(ssd, ss0 + 1)
                ch.mark(po.tensor_scalar(ss[:, 0:4], ss[:, 0:4], 1.0 / QR, EPS, ALU.mult, ALU.add))
                ch(po.tensor_scalar(ss[:, 4:8], ss[:, 4:8], 1.0 / KVR, EPS, ALU.mult, ALU.add))
                po.tensor_tensor(ss[:, :], ss[:, :], nhalf[:, :].to_broadcast([P, 8]), ALU.pow).then_inc(rsd, 1)

            def rank_dve(dve, ch):
                dve.wait_ge(rsd, rs0 + 1)
                for t in range(NT):
                    ch(dve.tensor_scalar(cq0[:, t, 0:QR], cq0[:, t, 0:QR], ss[:, t:t + 1], None, ALU.mult))
                    dve.tensor_scalar(cq0[:, t, QR:QR + KVR], cq0[:, t, QR:QR + KVR], ss[:, 4 + t:5 + t], None,
                                      ALU.mult).then_inc(xsd, 1)
                for t in range(NT):
                    dve.wait_ge(tr, tr0 + t + 1)
                    dve.tensor_tensor(ctmp[:, t, :].rearrange("p (k s) -> p k s", k=3),
                                      ps[:, t, 0:3 * P].rearrange("p (k s) -> p k s", k=3),
                                      cols2[:, QA:QA + 3].rearrange("p (k o) -> p k o", o=1).to_broadcast([P, 3, P]),
                                      ALU.mult).then_inc(midv, 1)
                for t in range(NT):
                    dve.wait_ge(ea, hi1 + t + 1)
                    dve.wait_ge(midv, md1 + t + 1)
                    d = cqT[:, :, t * P:t * P + P]
                    dve.tensor_tensor(d.l, ctmp[:, t, :].rearrange("p (k s) -> p k s", k=3), d.high_f,
                                      ALU.subtract).then_inc(ev, 1)

            def rank_pe(pe, ch):
                for t in range(NT):
                    pe.wait_ge(xsd, xs0 + t + 1)
                    for j in range(3):
                        m = pe.transpose(ps[:, t, j * P:j * P + P], cq0[:, t, j * P:j * P + P], ident[:, :])
                    m.then_inc(tr, 1)
            stage(rank_pe, rank_act, rank_dve, rank_po)

            gr2 = Groups(16, "AV")
            up_q = Rows(gr2, 0, cqT, NT, [(kpc(I["l0_mla_w_q_up"]), 0)], 384, 2, 2)
            up_kv = Rows(gr2, 8, cqT[:, 2:3, :], NT, [(kpc(I["l0_mla_w_kv_up"]), 0)], 512, 1, 2)

            def up_pe(pe, ch):
                up_q.pe(pe)
                up_kv.pe(pe)

            def kv_views(r):
                t, h = divmod(r, 2)
                s = up_kv.src(r).rearrange("p (h c) -> p h c", c=P)
                k = Kr[:, t, :].rearrange("p (h c) -> p h c", c=QK)[:, 4 * h:4 * h + 4, 0:NOPE]
                v = Vr[:, t, :].rearrange("p (h c) -> p h c", c=MV)[:, 4 * h:4 * h + 4, :]
                return s, k, v

            QrT = area(NS * SLOT, A0 + 16000, NT, MH * QK)

            sp1 = Split([up_q, up_kv])

            def up_act(act, ch):
                sp1.start(act)
                sp1.before(act, 0)
                for r in range(0, 8, 2):
                    up_q.ready(act, r)
                    take_act(act, up_q.src(r), QrT[:, r // 2, 0:384])
                for r in range(0, 8, 2):
                    up_kv.ready(act, r)
                    s, k, v = kv_views(r)
                    ch(act.activation(k, s[:, :, 0:NOPE], ACT.Copy))
                    take_act(act, s[:, :, NOPE:P], v)

            def up_dve(dve, ch):
                sp1.start(dve)
                sp1.before(dve, 0)
                for r in range(1, 8, 2):
                    up_q.ready(dve, r)
                    take_dve(dve, up_q.src(r), QrT[:, r // 2, 384:768])
                for r in range(1, 8, 2):
                    up_kv.ready(dve, r)
                    s, k, v = kv_views(r)
                    ch(dve.tensor_copy(k, s[:, :, 0:NOPE]))
                    take_dve(dve, s[:, :, NOPE:P], v)
            stage(up_pe, up_act, up_dve)

            ss1, rs1 = use(ssd, 2), use(rsd, 1)

            def heads(v):
                return v.rearrange("p t (h c) -> p (t h) c", c=QK)

            def head_norm(eng, ch, src, dst, which, stat):
                b = [P, NT * MH, QK]
                ch(eng.tensor_tensor(heads(dst), heads(src), stat.rearrange("p (n o) -> p n o", o=1).to_broadcast(b),
                                     ALU.mult))
                ch(eng.tensor_tensor(heads(dst), heads(dst), qg[:, which:which + 1, :].to_broadcast(b), ALU.mult))
                tmp = (sqq, sqk)[which]
                for t in range(NT):
                    d = dst[:, t, :].rearrange("p (h c) -> p h c", c=QK)
                    r1, r2 = d[:, :, NOPE:NOPE + HALF], d[:, :, NOPE + HALF:QK]
                    cs_, sn = (v[:, t:t + 1, :].to_broadcast([P, MH, HALF]) for v in (ropec, ropes))
                    a = [tmp[:, 8 * q:8 * q + 8, 0:HALF] for q in range(4)]
                    ch.mark(eng.tensor_tensor(a[0], r1, cs_, ALU.mult))
                    ch.mark(eng.tensor_tensor(a[1], r2, sn, ALU.mult))
                    ch.mark(eng.tensor_tensor(a[2], r2, cs_, ALU.mult))
                    ch(eng.tensor_tensor(a[3], r1, sn, ALU.mult))
                    ch.mark(eng.tensor_tensor(r1, a[0], a[1], ALU.subtract))
                    ch(eng.tensor_tensor(r2, a[2], a[3], ALU.add))

            def hn_act(act, ch):
                act.activation(sqq, heads(QrT), ACT.Square).then_inc(ssd, 1)

            def hn_dve(dve, ch):
                for t in range(NT):
                    ch.mark(dve.tensor_copy(
                        Kr[:, t, :].rearrange("p (h c) -> p h c", c=QK)[:, :, NOPE:QK],
                        cq0[:, t:t + 1, QR + KVR:C0].to_broadcast([P, MH, RO])))
                ch.wait()
                dve.wait_ge(ssd, ss1 + 1)
                ch(dve.tensor_reduce(st[:, 0:32], sqq, AX, ALU.add))
                ch(dve.tensor_tensor(sqq, heads(Kr), heads(Kr), ALU.mult))
                dve.tensor_reduce(st[:, 32:64], sqq, AX, ALU.add).then_inc(ssd, 1)
                dve.wait_ge(rsd, rs1 + 1)
                head_norm(dve, ch, QrT, Qr, 0, st[:, 0:32])

            def hn_po(po, ch):
                po.wait_ge(ssd, ss1 + 2)
                ch(po.tensor_scalar(st[:, 0:64], st[:, 0:64], 1.0 / QK, EPS, ALU.mult, ALU.add))
                po.tensor_tensor(st[:, 0:64], st[:, 0:64], nhalf[:, :].to_broadcast([P, 64]), ALU.pow).then_inc(rsd, 1)
                po.wait_ge(rsd, rs1 + 1)
                head_norm(po, ch, Kr, Kr, 1, st[:, 32:64])
            stage(None, hn_act, hn_dve, hn_po)

            preps = []
            for h in range(MH):
                for n, (R, to) in enumerate(((Qr, QT), (Kr, KT))):
                    preps.append((max(0, 4 * h - 3 + n), max(0, 4 * (h - 1)),
                                  [R[:, t, h * QK:h * QK + QK] for t in range(NT)], to[0:QK, h % 2, :], 1.0))

            def sc_mla(pe, v, b, pre0):
                h, i = divmod(v, NT)
                pe.wait_ge(s_pre, pre0 + 2 * h + 2)
                L = causal(v)
                return pe.matmul(ps[:, b, 0:L], QT[0:QK, h % 2, i * P:i * P + P], KT[0:QK, h % 2, 0:L],
                                 start=True, stop=True)
            attention(MH * NT, causal, sc_mla,
                      lambda u, j: Vr[:, j, (u // NT) * MV:(u // NT) * MV + MV], MV,
                      lambda h, i: orow[:, i, h * MV:h * MV + MV], QK ** -0.5, preps)

            T1 = work(A0 + 7808, 4, 512)
            U0 = MH * NT
            sc0, t10, sp0, m10, w0, m20, ex0, pt0, pe0, o0, on0 = (
                use(s, U0) for s in (s_sc, s_t1, s_sp, s_m1, s_w, s_m2, s_ex, s_pt, s_pe, s_o, s_on))
            
            def sb_pe(pe, ch):
                for v in range(U0 + 4):
                    if v < U0:
                        h, i = divmod(v, NT)
                        L = causal(v)
                        if v >= 3:
                            pe.wait_ge(s_w, w0 + v - 2)
                        r = slice(64 * (h % 2), 64 * (h % 2) + 64)
                        pe.matmul(ps[:, v % 3, 0:L], sbq[r, h // 2, i * P:i * P + P], sbk[r, h // 2, 0:L],
                                  start=True, stop=True).then_inc(s_sc, 1)
                    if 3 <= v < U0 + 3:
                        u = v - 3
                        pe.wait_ge(s_ex, ex0 + u + 1)
                        if u >= 2:
                            pe.wait_ge(s_pe, pe0 + u - 1)
                        for j in range(causal(u) // P):
                            m = pe.transpose(ps[:, 3 + u % 2, j * P:j * P + P], Pb[:, u % 4, j * P:j * P + P],
                                             ident[:, :])
                        m.then_inc(s_pt, 1)
                    if v >= 4:
                        u = v - 4
                        h = u // NT
                        pe.wait_ge(s_pe, pe0 + u + 1)
                        if u >= 2:
                            pe.wait_ge(s_on, on0 + u - 1)
                        nb = causal(u) // P
                        for j in range(nb):
                            m = pe.matmul(value_bank(u, 64), PT[:, u % 2, j * P:j * P + P],
                                          sbv[:, j, h * 64:h * 64 + 64], start=(j == 0), stop=(j == nb - 1))
                        m.then_inc(s_o, 1)

            def sb_act(act, ch):
                act.preload_act_table_set("natural_log_exp_and_others")
                for v in range(U0 + 3):
                    if v < U0:
                        act.wait_ge(s_sc, sc0 + v + 1)
                        if v >= 4:
                            act.wait_ge(s_w, w0 + v - 3)
                        t1 = T1[:, v % 4, 0:causal(v)]
                        ch(act.activation(t1, ps[:, v % 3, 0:causal(v)], ACT.Abs))
                        ch(act.activation(t1, t1, ACT.Exp, scale=-1.0))
                        act.activation(t1, t1, ACT.Ln, bias=1.0).then_inc(s_t1, 1)
                    if 2 <= v < U0 + 2:
                        u = v - 2
                        act.wait_ge(s_m2, m20 + u + 1)
                        p = Pb[:, u % 4, 0:causal(u)]
                        act.activation(p, p, ACT.Exp).then_inc(s_ex, 1)
                    if v >= 3:
                        u = v - 3
                        L = causal(u)
                        act.wait_ge(s_pt, pt0 + u + 1)
                        if u >= 2:
                            act.wait_ge(s_o, o0 + u - 1)
                        act.activation(PT[:, u % 2, 0:L], ps[:, 3 + u % 2, 0:L], ACT.Copy).then_inc(s_pe, 1)

            def sb_dve(dve, ch):
                for v in range(U0 + 4):
                    if v < U0:
                        dve.wait_ge(s_t1, t10 + v + 1)
                        t1 = T1[:, v % 4, 0:causal(v)]
                        dve.scalar_tensor_tensor(out=t1, in0=ps[:, v % 3, 0:causal(v)], scalar=0.0, in1=t1,
                                                 op0=ALU.max, op1=ALU.add).then_inc(s_sp, 1)
                    if 1 <= v <= U0:
                        u = v - 1
                        L = causal(u)
                        t1 = T1[:, u % 4, 0:L]
                        p = Pb[:, u % 4, 0:L]
                        dve.wait_ge(s_m1, m10 + u + 1)
                        if u >= 4:
                            dve.wait_ge(s_pt, pt0 + u - 3)
                        ch(dve.tensor_tensor_scan(p[:, ::-1], ones[:, 0:1].to_broadcast([P, L]), t1[:, ::-1], 0.0,
                                                  ALU.mult, ALU.add))
                        dve.tensor_tensor(p, ps[:, u % 3, 0:L], p, ALU.subtract).then_inc(s_w, 1)
                    if v >= 4:
                        u = v - 4
                        h, i = divmod(u, NT)
                        dve.wait_ge(s_o, o0 + u + 1)
                        dve.tensor_copy(orow[:, i, 512 + h * 64:512 + h * 64 + 64],
                                        value_bank(u, 64)).then_inc(s_on, 1)

            def sb_po(po, ch):
                for v in range(U0 + 1):
                    if v < U0:
                        dg = T1[:, v % 4, causal(v) - P:causal(v)]
                        po.wait_ge(s_sp, sp0 + v + 1)
                        po.affine_select(out=dg, in_=dg, compare_op=ALU.is_gt, fill=0.0,
                                         base=0, pattern=[[-1, P]], channel_multiplier=1).then_inc(s_m1, 1)
                    if v >= 1:
                        u = v - 1
                        dg = Pb[:, u % 4, causal(u) - P:causal(u)]
                        po.wait_ge(s_w, w0 + u + 1)
                        po.affine_select(out=dg, in_=dg, compare_op=ALU.is_gt, fill=NEG,
                                         base=0, pattern=[[-1, P]], channel_multiplier=1).then_inc(s_m2, 1)
            stage(sb_pe, sb_act, sb_dve, sb_po)
            out_stage(orow, I["l0_w_o"])
        if on(2):
            ffn(G_F0, I["l0_w_gate"], I["l0_w_up"], I["l0_w_down"])

        if on(3):
            FW = 65
            FQr = work(A0, NT * FH, FW)
            FKr = work(A0 + 4160, NT * FH, FW)
            FVr = work(A0 + 8320, NT, D)
            FQT = work(A0 + 12416, 2, 512)
            FKT = work(A0 + 13440, 2, 512)
            sqf = work(A0 + 14464, 2, 512)
            low_x = act_parts(A0 + 15488)
            w = I["l1_w_in"]
            early = []
            norm_stage(x, low_x, G_A1, NT, work(A0, 4 * D), early)
            gr = Groups(28, "VVVV" + "A" * 16 + "AV" * 4)
            fj = Rows(gr, 0, low_x, NT, [(kpc(w[:, 3 * D:3 * D + FH]), 0)], FH)
            qk_jobs = [(Rows(gr, 4 + 4 * j, low_x, NT, [(kpc(w[:, j * 512:j * 512 + 512]), 0)], 512),
                        (FQr, FKr)[j // 2], j) for j in range(4)]
            v_jobs = [(Rows(gr, 20 + 4 * j, low_x, NT, [(kpc(w[:, (4 + j) * 512:(5 + j) * 512]), 0)], 512), j)
                      for j in range(2)]
            ahead(early, fj.w)
            rows_in = gr
            fsp = Split([fj] + [job for job, _, _ in qk_jobs] + [job for job, _ in v_jobs])
            nn = NT * FH
            sq0, mv2, rs2 = use(ssd, 16), use(midv, 16), use(rsd, 2)
            st4 = st[:, :].rearrange("p (c t a) -> p c t a", c=4, t=NT)

            def head_rows(R, t, j):
                h0 = t * FH + 8 * (j % 2)
                return R[:, h0:h0 + 8, 0:64]

            def fp_pe(pe, ch):
                fj.pe(pe)
                for job, _, _ in qk_jobs:
                    job.pe(pe)
                for job, _ in v_jobs:
                    job.pe(pe)

            def fp_act(act, ch):
                n = 0
                fsp.start(act)
                fsp.before(act, 0)
                fsp.after(act, 0)
                for job, R, j in qk_jobs:
                    fsp.before(act, 1 + j)
                    for t in range(NT):
                        job.ready(act, t)
                        if n >= 2:
                            act.wait_ge(midv, mv2 + n - 1)
                        act.activation(sqf[:, n % 2, :], job.src(t), ACT.Square).then_inc(ssd, 1)
                        act.activation(head_rows(R, t, j), job.src(t).rearrange("p (h c) -> p h c", c=64),
                                       ACT.Copy).then_inc(ea, 1)
                        n += 1
                    fsp.after(act, 1 + j)
                for job, c in v_jobs:
                    fsp.before(act, 5 + c)
                    for t in range(0, NT, 2):
                        job.ready(act, t)
                        take_act(act, job.src(t), FVr[:, t, c * 512:c * 512 + 512])
                    fsp.after(act, 5 + c)

            def fp_norm(eng, ch, which, R):
                eng.wait_ge(rsd, rs2 + which + 1)
                rows_in.wait_taken(eng, 11 + 8 * which)
                for c in range(2):
                    for t in range(NT):
                        r = head_rows(R, t, c)
                        ch.mark(eng.tensor_tensor(r, r, st4[:, 2 * which + c, t, :].rearrange("p (a o) -> p a o", o=1
                                                                                              ).to_broadcast([P, 8, 64]),
                                                  ALU.mult))
                ch.wait()

            def fp_dve(dve, ch):
                fsp.start(dve)
                fsp.before(dve, 0)
                for t in range(NT):
                    fj.ready(dve, t)
                    dve.tensor_tensor(FG[:, 0, t, :], fj.src(t), ffb[:, :], ALU.add).then_inc(ev, 1)
                fsp.after(dve, 0)
                for n in range(16):
                    if n % 4 == 0:
                        fsp.before(dve, 1 + n // 4)
                    dve.wait_ge(ssd, sq0 + n + 1)
                    c, t = divmod(n, NT)
                    dve.tensor_reduce(st4[:, c, t, :], sqf[:, n % 2, :].rearrange("p (h c) -> p h c", c=64), AX,
                                      ALU.add).then_inc(midv, 1)
                    if n % 4 == 3:
                        fsp.after(dve, 1 + n // 4)
                for job, c in v_jobs:
                    fsp.before(dve, 5 + c)
                    for t in range(1, NT, 2):
                        job.ready(dve, t)
                        take_dve(dve, job.src(t), FVr[:, t, c * 512:c * 512 + 512])
                    fsp.after(dve, 5 + c)

            def fp_po(po, ch):
                ch.mark(po.memset(FQr[:, :, 64:65], 1.0))
                for which, R in enumerate((FQr, FKr)):
                    s_ = st[:, which * nn:(which + 1) * nn]
                    po.wait_ge(midv, mv2 + 8 * (which + 1))
                    ch(po.tensor_scalar(s_, s_, 1.0 / 64, EPS, ALU.mult, ALU.add))
                    po.tensor_tensor(s_, s_, nhalf[:, :].to_broadcast([P, nn]), ALU.pow).then_inc(rsd, 1)
                    fp_norm(po, ch, which, R)
            stage(fp_pe, fp_act, fp_dve, fp_po)

            def decay_rows(dve, ch):
                ch(dve.tensor_scalar(FKr[:, :, 64:65].rearrange("p n o -> p (n o)"),
                                     CS[:, :, :].rearrange("p t h -> p (t h)"), 8.0, None, ALU.mult))
            softplus_stages(FH, None, decay_rows)

            preps = []
            for h in range(FH):
                for n, (R, to, g) in enumerate(((FQr, FQT, FQ), (FKr, FKT, FK))):
                    preps.append((max(0, 4 * h - 3 + n), max(0, 4 * (h - 1)),
                                  [R[:, t * FH + h, :] for t in range(NT)], to[0:FW, h % 2, :], cols2[0:FW, g:g + 1]))

            def sc_fox(pe, v, b, pre0):
                h, i = divmod(v, NT)
                pe.wait_ge(s_pre, pre0 + 2 * h + 2)
                return pe.matmul(ps[:, b, 0:causal(v)], FQT[0:FW, h % 2, i * P:i * P + P],
                                 FKT[0:FW, h % 2, 0:causal(v)], start=True, stop=True)
            attention(FH * NT, causal, sc_fox,
                      lambda u, j: FVr[:, j, (u // NT) * 64:(u // NT) * 64 + 64], 64,
                      lambda h, i: orow[:, i, h * 64:h * 64 + 64], 0.125, preps, fox=True)
            out_stage(orow, I["l1_w_o"])
        if on(4):
            ffn(G_F1, I["l1_w_gate"], I["l1_w_up"], I["l1_w_down"])

        late = []

        def load_now(name, dst, src):
            s = sem(name)
            late.append((len(stages), dst, src, s))
            return s, 16

        memr = work(A0 + 19456, MT, D)

        def load_memory():
            return load_now("mem_in", memr, I["mem_2"][0].rearrange("(t p) d -> p t d", p=P))

        if on(5):
            mqk = work(A0, 16, S)
            mv = work(A0 + 8192, NT, D)
            H = work(A0 + 12288, NT, D)
            low_x = act_parts(A0 + 16384)
            acc = work(A0 + 20480, 2, 512)
            CTm = work(A0 + 21504, S)
            E = work(3072, 4, 512)
            w = I["w_in_2"][0]
            early = []
            norm_stage(x, low_x, G_MIX, NT, work(A0, 4 * D), early)
            gr = Groups(28, "V" * 4 + "C" * 16 + "AV" * 4)
            ij = Rows(gr, 0, low_x, NT, [(kpc(w[:, 4096:4104]), 0)], 8)
            qkj = [Cols(gr, 4 + 4 * c, low_x, S, [(kpc(w[:, c * 512:c * 512 + 512]), 0)]) for c in range(4)]
            vj = [Rows(gr, 20 + 4 * c, low_x, NT, [(kpc(w[:, 2048 + c * 512:2560 + c * 512]), 0)], 512)
                  for c in range(2)]
            ahead(early, ij.w)
            msp = Split([ij] + qkj + vj)
            cv0, sl0 = gr.freed[4][1] - 1, use(mida, 16)

            def mp_pe(pe, ch):
                for job in [ij] + qkj + vj:
                    job.pe(pe)

            def mp_act(act, ch):
                msp.start(act)
                msp.before(act, 0)
                msp.after(act, 0)
                for c in range(16):
                    if c % 4 == 0:
                        msp.before(act, 1 + c // 4)
                    act.wait_ge(midv, cv0 + c + 1)
                    act.activation(mqk[:, c, :], acc[:, c % 2, :], ACT.Silu,
                                   bias=cols2[:, CB + c:CB + c + 1]).then_inc(mida, 1)
                    if c % 4 == 3:
                        msp.after(act, 1 + c // 4)
                for c, job in enumerate(vj):
                    msp.before(act, 5 + c)
                    for t in range(0, NT, 2):
                        job.ready(act, t)
                        take_act(act, job.src(t), mv[:, t, c * 512:c * 512 + 512])
                    msp.after(act, 5 + c)

            def mp_dve(dve, ch):
                msp.start(dve)
                msp.before(dve, 0)
                for t in range(NT):
                    ij.ready(dve, t)
                    b = ps[:, gr.bank(t), :]
                    ch(dve.tensor_tensor(FG[:, 1, t, 4:8], b[:, 0:4], bif[:, 0:4], ALU.add))
                    dve.tensor_tensor(FG[:, 0, t, 0:4], b[:, 4:8], bif[:, 4:8], ALU.add).then_inc(ev, 1)
                msp.after(dve, 0)
                for c in range(16):
                    job = qkj[c // 4]
                    if c % 4 == 0:
                        msp.before(dve, 1 + c // 4)
                    job.ready(dve, c % 4)
                    if c >= 2:
                        dve.wait_ge(mida, sl0 + c - 1)
                    p, a = job.src(c % 4), acc[:, c % 2, :]
                    tap = lambda i: cols2[:, CW + 16 * i + c:CW + 16 * i + c + 1]
                    ch(dve.tensor_scalar(a, p, tap(3), None, ALU.mult))
                    for s in (1, 2, 3):
                        ins = dve.scalar_tensor_tensor(out=a[:, s:S], in0=p[:, 0:S - s], scalar=tap(3 - s),
                                                       in1=a[:, s:S], op0=ALU.mult, op1=ALU.add)
                        if s < 3:
                            ch(ins)
                    ins.then_inc(midv, 1)
                    if c % 4 == 3:
                        msp.after(dve, 1 + c // 4)
                for c, job in enumerate(vj):
                    msp.before(dve, 5 + c)
                    for t in range(1, NT, 2):
                        job.ready(dve, t)
                        take_dve(dve, job.src(t), mv[:, t, c * 512:c * 512 + 512])
                    msp.after(dve, 5 + c)
            stage(mp_pe, mp_act, mp_dve)

            def input_gates(dve, ch):
                ch(dve.tensor_tensor(FG[:, 1, :, 8:12], FG[:, 1, :, 4:8], CS[:, :, 0:4], ALU.add))
            softplus_stages(LH, (FG[:, 1, :, 8:12], CTm[0:LH, :], 1.0), input_gates)

            def exponents(pe, h):
                return pe.matmul(ps[:, 7, :], ident[0:LH, h:h + 1].to_broadcast([LH, P]), CTm[0:LH, :],
                                 start=True, stop=True)

            def sc_ml(pe, v, b, pre0):
                h, i = divmod(v, NT)
                for k in range(2):
                    m = pe.matmul(ps[:, b, 0:causal(v)], mqk[:, 2 * h + k, i * P:i * P + P],
                                  mqk[:, 8 + 2 * h + k, 0:causal(v)], start=(k == 0), stop=(k == 1))
                return m
            attention(LH * NT, causal, sc_ml, lambda u, j: mv[:, j, (u // NT) * DH:(u // NT) * DH + DH], DH,
                      lambda h, i: H[:, i, h * DH:h * DH + DH], 1.0, mlstm=(exponents, E))

            sqm = work(A0, NT, D)
            mhb = work(A0 + 4096, D)
            mhb_in = load_now("mhb_in", mhb, every(I["mh_norm_g_2"][0]))
            sgb = work(A0 + 5120, D)
            sgb_in = load_now("sgb_in", sgb, every(I["sgu_norm_g_2"][0]))
            gb = work(A0 + 6144, 2 * D)
            gb_in = load_now("gb_in", gb, every(I["b_gate_2"][0]))
            ss3, rs3 = use(ssd, 1), use(rsd, 1)

            def d256(v):
                return v[:, :, :].rearrange("p t (h c) -> p (t h) c", c=DH)

            def hm_act(act, ch):
                act.activation(sqm, H, ACT.Square).then_inc(ssd, 1)
            mv3 = use(midv, 1)

            def hm_dve(dve, ch):
                dve.wait_ge(ssd, ss3 + 1)
                dve.tensor_reduce(st[:, 0:16], d256(sqm), AX, ALU.add).then_inc(midv, 1)
                dve.wait_ge(rsd, rs3 + 1)
                ch(dve.tensor_tensor(d256(H), d256(H),
                                     st[:, 0:16].rearrange("p (n o) -> p n o", o=1).to_broadcast([P, 16, DH]),
                                     ALU.mult))
                dve.wait_ge(*mhb_in)
                ch(dve.tensor_tensor(H, H, mhb.rearrange("p (o c) -> p o c", o=1).to_broadcast([P, NT, D]), ALU.mult))

            def hm_po(po, ch):
                po.wait_ge(midv, mv3 + 1)
                ch(po.tensor_scalar(st[:, 0:16], st[:, 0:16], 1.0 / DH, EPS, ALU.mult, ALU.add))
                po.tensor_tensor(st[:, 0:16], st[:, 0:16], nhalf[:, :].to_broadcast([P, 16]), ALU.pow).then_inc(rsd, 1)
            stage(None, hm_act, hm_dve, hm_po)

            tmp = work(A0 + 20480, 3, 512)
            Vs = work(A0 + 8192, NT, D)
            Mx = work(A0, NT, D)
            wsr = work(A0 + 4096, G8, P)
            wsr_in = load_now("wsr_in", wsr, I["w_s_2"][0].rearrange("g t s -> t g s"))
            wsT = wsr

            def gated_stage(spec, dst_of):
                kinds = [kind for _, kind, _, _ in spec for t in range(NT)]
                gr = Groups(len(kinds), ["A" if k == "gelu" else "C" if k == "bias" else "X" for k in kinds])
                jobs = [(Rows(gr, NT * n, low_x, NT, [(kpc(w[:, c0:c0 + 512]), 0)], 512), kind, half, bcol)
                        for n, (c0, kind, half, bcol) in enumerate(spec)]
                order = [k for k in range(len(kinds)) if kinds[k] != "gelu"]
                a0, u0 = use(mida, len(order)), use(xsd, len(order))
                for n, g in enumerate(order):
                    if gr.who[g] == "X":
                        gr.freed[g] = (mida, a0 + n + 1)

                def steps():
                    n = 0
                    for j, (job, kind, half, bcol) in enumerate(jobs):
                        for t in range(NT):
                            yield n, job, kind, half, bcol, t, NT * j + t
                            n += kind != "gelu"

                def pe(pe, ch):
                    for job, _, _, _ in jobs:
                        job.pe(pe)

                gsp = Split([job for job, _, _, _ in jobs])

                def act(act, ch):
                    gsp.start(act)
                    for n, job, kind, half, _, t, g in steps():
                        if t == 0:
                            gsp.before(act, g // NT)
                        b = tmp[:, n % 3, :]
                        if kind == "gelu":
                            job.ready(act, t)
                            act.activation(Vs[:, t, half * 512:half * 512 + 512], job.src(t),
                                           ACT.Gelu_apprx_tanh).then_inc(ea, 1)
                        elif kind == "bias":
                            act.wait_ge(*gr.freed[g])
                            act.activation(b, b, ACT.Sigmoid).then_inc(mida, 1)
                        else:
                            job.ready(act, t)
                            if n >= 3:
                                act.wait_ge(xsd, u0 + n - 2)
                            act.activation(b, job.src(t), kind).then_inc(mida, 1)
                        if t == NT - 1:
                            gsp.after(act, g // NT)

                def dve(dve, ch):
                    gsp.start(dve)
                    dve.wait_ge(*gb_in)
                    todo = []

                    def finish(n, half, bcol, t):
                        dve.wait_ge(mida, a0 + n + 1)
                        dst, add = dst_of(bcol)
                        d = dst[:, t, half * 512:half * 512 + 512]
                        ins = dve.tensor_tensor(d, d, tmp[:, n % 3, :], ALU.mult)
                        if add:
                            ch(ins)
                            y = H[:, t, half * 512:half * 512 + 512]
                            ins = dve.tensor_tensor(y, y, d, ALU.add)
                        ins.then_inc(xsd, 1)
                    for n, job, kind, half, bcol, t, g in steps():
                        if t == 0:
                            gsp.before(dve, g // NT)
                        if kind == "gelu":
                            if t == NT - 1:
                                gsp.after(dve, g // NT)
                            continue
                        if kind == "bias":
                            job.ready(dve, t)
                            if n >= 3:
                                dve.wait_ge(xsd, u0 + n - 2)
                            dve.tensor_tensor(tmp[:, n % 3, :], job.src(t), gb[:, bcol:bcol + 512],
                                              ALU.add).then_inc(midv, 1)
                        todo.append((n, half, bcol, t))
                        if len(todo) > 1:
                            finish(*todo.pop(0))
                        if t == NT - 1:
                            gsp.after(dve, g // NT)
                    for q in todo:
                        finish(*q)
                stage(pe, act, dve)

            gated_stage([(3072, ACT.Sigmoid, 0, None), (3584, ACT.Sigmoid, 1, None),
                         (6152, "bias", 0, 0), (6664, "bias", 1, 512),
                         (5128, "gelu", 0, None), (5640, "gelu", 1, None)],
                        lambda bcol: (H, False))

            ss4, rs4 = use(ssd, 1), use(rsd, 1)

            def sv_act(act, ch):
                for t in range(NT):
                    ins = act.activation(tmp[:, 0:2, :].rearrange("p a b -> p (a b)"), Vs[:, t, :], ACT.Square,
                                         accum_out=ss[:, t:t + 1])
                    if t < NT - 1:
                        ch(ins)
                ins.then_inc(ssd, 1)

            def sv_po(po, ch):
                po.wait_ge(ssd, ss4 + 1)
                ch(po.tensor_scalar(ss[:, 0:4], ss[:, 0:4], 1.0 / D, EPS, ALU.mult, ALU.add))
                po.tensor_tensor(ss[:, 0:4], ss[:, 0:4], nhalf[:, :].to_broadcast([P, 4]), ALU.pow).then_inc(rsd, 1)
            tr4 = use(tr, 2)

            def sv_pe(pe, ch):
                pe.wait_ge(*wsr_in)
                for g in range(G8):
                    m = pe.transpose(ps[:, g // 4, (g % 4) * P:(g % 4) * P + P], wsr[:, g, :], ident[:, :])
                    if g % 4 == 3:
                        m.then_inc(tr, 1)

            def sv_dve(dve, ch):
                dve.wait_ge(*sgb_in)
                for q in range(2):
                    dve.wait_ge(tr, tr4 + q + 1)
                    ch.mark(dve.tensor_tensor(wsT[:, 4 * q:4 * q + 4, :],
                                              ps[:, q, :].rearrange("p (g s) -> p g s", g=4),
                                              tri[:, :].rearrange("p (o s) -> p o s", o=1).to_broadcast([P, 4, P]),
                                              ALU.mult))
                dve.wait_ge(rsd, rs4 + 1)
                for t in range(NT):
                    ch(dve.scalar_tensor_tensor(out=Vs[:, t, :], in0=Vs[:, t, :], scalar=ss[:, t:t + 1],
                                                in1=sgb, op0=ALU.mult, op1=ALU.mult))
            stage(sv_pe, sv_act, sv_dve, sv_po)

            gm = Groups(8, "A")
            tr5 = use(tr, 8)

            def mix_pe(pe, ch):
                for g in range(G8):
                    for c in range(NT):
                        m = pe.matmul(ps[:, g, c * P:c * P + P], wsT[:, g, :], Vs[:, c, g * P:g * P + P],
                                      start=True, stop=True)
                    m.then_inc(tr, 1)

            def mix_act(act, ch):
                for g in range(G8):
                    act.wait_ge(tr, tr5 + g + 1)
                    act.activation(Mx[:, :, g * P:g * P + P], ps[:, g, :].rearrange("p (c s) -> p c s", c=NT),
                                   ACT.Identity, bias=cols2[:, BS + g:BS + g + 1]).then_inc(ea, 1)
            stage(mix_pe, mix_act)
            gated_stage([(4104, ACT.Gelu_apprx_tanh, 0, None), (4616, ACT.Gelu_apprx_tanh, 1, None),
                         (7176, "bias", 0, 1024), (7688, "bias", 1, 1536)],
                        lambda bcol: (Mx, bcol is not None))
            if on(6):
                mem_in = load_memory()
            out_stage(H, I["w_out_2"][0])

        if on(6):
            if not on(5):
                mem_in = load_memory()
            memT = parts(A0 + 2048, A0 + 4096, KD, NM)
            xk = work(A0 + 6144, KD, NM)
            xv = work(A0 + 8192, MT, D)
            xq = work(A0 + 10240, KD, S)
            low_x = act_parts(A0 + 14336)

            def mem_dve(dve, ch):
                dve.wait_ge(*mem_in)
            stage(None, None, mem_dve)
            norm_stage(memr, memT, G_MEM, MT, work(A0 + 6144, 4 * D))
            early = []
            norm_stage(x, low_x, G_X, NT, work(A0 + 6144, 4 * D), early)
            gr = Groups(20, "AV")
            jobs = []
            wkv, wq = I["w_xkv_2"][0], I["w_xq_2"][0]

            def cols_to(v, c):
                return lambda r: v[:, 4 * c + r, :]

            def rows_to(v, c):
                return lambda r: v[:, r, c * 512:c * 512 + 512]
            for c in range(2):
                jobs.append((Cols(gr, 4 * c, memT, NM, [(kpc(wkv[:, c * 512:c * 512 + 512]), 0)]), cols_to(xk, c), 1.0))
            for c in range(2):
                jobs.append((Rows(gr, 8 + 2 * c, memT, MT, [(kpc(wkv[:, D + c * 512:D + c * 512 + 512]), 0)], 512),
                             rows_to(xv, c), 1.0))
            for c in range(2):
                jobs.append((Cols(gr, 12 + 4 * c, low_x, S, [(kpc(wq[:, c * 512:c * 512 + 512]), 0)]),
                             cols_to(xq, c), 1.0))
            ahead(early, jobs[0][0].w)
            plain_stage(jobs, gr)

            def sc_x(pe, v, b, pre0):
                h, i = divmod(v, NT)
                for k in range(2):
                    m = pe.matmul(ps[:, b, 0:NM], xq[:, 2 * h + k, i * P:i * P + P], xk[:, 2 * h + k, :],
                                  start=(k == 0), stop=(k == 1))
                return m
            attention(LH * NT, lambda v: NM, sc_x, lambda u, j: xv[:, j, (u // NT) * DH:(u // NT) * DH + DH], DH,
                      lambda h, i: orow[:, i, h * DH:h * DH + DH], DH ** -0.5)
            out_stage(orow, I["w_xo_2"][0])

        if on(7):
            low_x = act_parts(A0)
            xn = moe(5264, NT, D)
            xnp = Pair(actR[:, :, :].rearrange("p (t a) s -> p t (a s)", t=NT),
                       area(NS * SLOT + NMB * 2 * MP, 0, NT, D, dt=F32R))
            LG = moe(4096, NT, NGR + NE)
            OB = moe(4240, D)


            def moe_parts(high, low, *shape):
                return Pair(*(area(NS * SLOT + NMB * 2 * MP, off, *shape, dt=F32R) for off in (high, low)))
            XT = moe_parts(5264, 6288, KD, P)
            HS = moe(7312, 512)
            HB = moe(7824, 512)
            HT = moe_parts(8336, 8848, 4, P)
            OH = area(NS * SLOT + NMB * 2 * MP, 13312, NT, P, dt=F32R)
            gmoe = moe(13824, D)
            XR = moe(14848, D)
            gfin = moe(9360, D)
            A2 = moe(10384, 2 * NT, NE)
            As = moe(10640, NT, NE)
            RK = moe(10768, NT, NE)
            T32 = moe(11280, NT, NE)
            T4 = moe(11408, NT, NGR)
            GO = moe(11424, NT, NGR)
            s1 = moe(11440, 16, NT)
            gate = moe(11504, 2, NT)
            rowi = moe(11512, 2, NT)
            rowu = sb("rowu", [P, 2 * NT], U32)
            cnt = moe(11520, NE)
            flg = moe(11552, 3, NE)
            pos = moe(11648, 3, NE)
            t96 = moe(11840, 3, NE)
            codee = moe(11936, 3, NE)
            codeb = moe(12032, 3, NE)
            val = moe(12128, 16)
            vsh = moe(12144, NOVER)
            rkq = moe(12152, NT, 1)
            rbase = moe(12160, 4, NE)
            zrow = moe(12288, D)
            early = []
            norm_stage(x, low_x, G_MOE, NT, moe(4240, 4 * D), early)
            gmoe_in = load_now("gmoe_in", gmoe, every(I["norm_moe_g_2"][0]))
            gfin_in = load_now("gfin_in", gfin, every(I["norm_f_g_2"]))
            gr = Groups(4, "V")
            loads = [(kpc(I["w_rg_2"][0]), 0), (kpc(I["w_re_2"][0]), NGR)]
            rj = Rows(gr, 0, low_x, NT, loads, NGR + NE)
            ahead(early, rj.w)
            moe_bar = len(stages)
            v0, a0, t0 = use(midv, 2), use(mida, 1), use(tr, 1)

            def b3(v, n):
                return v.rearrange("p (a o) -> p a o", o=1).to_broadcast([P, v.shape[1], n])

            def first_of(dve, ch, oh, vals, m, n, tmpv):
                ch(dve.tensor_reduce(m, vals, AX, ALU.max))
                ch(dve.tensor_tensor(oh, vals, b3(m, n), ALU.is_equal))
                ch(dve.tensor_tensor(oh, oh, desc[:, NE - n:NE].rearrange("p (o c) -> p o c", o=1
                                                                          ).to_broadcast([P, NT, n]), ALU.mult))
                ch(dve.tensor_reduce(tmpv, oh, AX, ALU.max))
                ch(dve.tensor_tensor(oh, oh, b3(tmpv, n), ALU.is_equal))

            def rt_pe(pe, ch):
                rj.pe(pe)
                pe.wait_ge(midv, v0 + 2)
                for t in range(NT):
                    for j in range(t + 1):
                        m = pe.matmul(ps[:, 4, t * NE:t * NE + NE], (tri if j == t else ones)[:, :], As[:, j, :],
                                      start=(j == 0), stop=(j == t))
                for j in range(NT):
                    m = pe.matmul(ps[:, 5, 0:NE], ones[:, :], As[:, j, :], start=(j == 0), stop=(j == NT - 1))
                m.then_inc(tr, 1)

            rsp = Split([rj])

            def rt_act(act, ch):
                rsp.start(act)
                for t in range(NT):
                    act.mul(xn[:, t, :], x[:, t, :], rx[:, t:t + 1]).then_inc(xsd, 1)
                act.wait_ge(midv, v0 + 1)
                ch(act.activation(T4, T4, ACT.Exp))
                act.activation(s1[:, 5, :], s1[:, 5, :], ACT.Exp).then_inc(mida, 1)
                rj.ready(act, NT - 1)
                act.wait_ge(xsd, xn0 + NT + 1)
                act.activation(xnp.h, xn, ACT.Copy).then_inc(ea, 1)
            xn0, hi7 = use(xsd, NT + 1), use(ea, 1)

            z_in = sem("z_in")

            def rt_po(po, ch):
                ch(po.memset(zrow, 0.0))
                for q in range(NOVER):
                    po.dma_start(obuf[(NE + q) * P:(NE + q + 1) * P, :], zrow).then_inc(z_in, 16)
                po.wait_ge(xsd, xn0 + NT)
                po.wait_ge(*gmoe_in)
                po.tensor_tensor(xn, xn, gmoe.rearrange("p (o c) -> p o c", o=1).to_broadcast([P, NT, D]),
                                 ALU.mult).then_inc(xsd, 1)
                po.wait_ge(ea, hi7 + 1)
                po.wait_ge(xsd, xn0 + NT + 1)
                ch(po.tensor_tensor(xnp.l, xn, xnp.high_f, ALU.subtract))

            def rt_dve(dve, ch):
                rsp.start(dve)
                for t in range(NT):
                    rj.ready(dve, t)
                    dve.tensor_tensor(LG[:, t, :], rj.src(t), rbias[:, :], ALU.add).then_inc(ev, 1)
                gr.wait_taken(dve, NT - 1)
                G, Ee = LG[:, :, 0:NGR], LG[:, :, NGR:NGR + NE]
                m1, m2, gm_, w_ = s1[:, 0, :], s1[:, 1, :], s1[:, 2, :], s1[:, 3, :]
                first_of(dve, ch, GO, G, gm_, NGR, w_)
                ch(dve.tensor_tensor(T4, G, b3(gm_, NGR), ALU.subtract))
                ch(dve.tensor_scalar(GO, GO, 1.0, 1e30, ALU.subtract, ALU.mult))
                Eg = Ee.rearrange("p t (g e) -> p t g e", e=EPG)
                for g in range(NGR):
                    ch(dve.tensor_tensor(Eg[:, :, g, :], Eg[:, :, g, :],
                                         GO[:, :, g:g + 1].to_broadcast([P, NT, EPG]), ALU.add))
                first_of(dve, ch, A2[:, 0:NT, :], Ee, m1, NE, w_)
                ch(dve.scalar_tensor_tensor(out=T32, in0=A2[:, 0:NT, :], scalar=-2e30, in1=Ee,
                                            op0=ALU.mult, op1=ALU.add))
                first_of(dve, ch, A2[:, NT:2 * NT, :], T32, m2, NE, w_)
                dve.tensor_tensor(s1[:, 5, :], m2, m1, ALU.subtract).then_inc(midv, 1)
                dve.tensor_tensor(As, A2[:, 0:NT, :], A2[:, NT:2 * NT, :], ALU.add).then_inc(midv, 1)
                dve.wait_ge(midv, v0 + 2)
                dve.wait_ge(mida, a0 + 1)
                ch(dve.tensor_reduce(s1[:, 6, :], T4, AX, ALU.add))
                ch(dve.tensor_scalar(s1[:, 7, :], s1[:, 5, :], 1.0, None, ALU.add))
                ch(dve.tensor_tensor(s1[:, 6, :], s1[:, 6, :], s1[:, 7, :], ALU.mult))
                ch(dve.reciprocal(gate[:, 0, :], s1[:, 6, :]))
                ch(dve.tensor_tensor(gate[:, 1, :], gate[:, 0, :], s1[:, 5, :], ALU.mult))
                dve.wait_ge(tr, t0 + 1)
                rk = ps[:, 4, 0:NT * NE].rearrange("p (t e) -> p t e", t=NT)
                ch(dve.tensor_tensor(RK, As, rk, ALU.mult))
                ch(dve.tensor_copy(cnt, ps[:, 5, 0:NE]))
                for b in range(3):
                    ch.mark(dve.tensor_scalar(flg[:, b, :], cnt, 128.0 * (b + 1) + 0.5, None, ALU.is_gt))
                    ch.mark(dve.tensor_copy(codee[:, b, :], eidx[:, :]))
                    ch.mark(dve.memset(codeb[:, b, :], 128.0 * (b + 1)))
                ch.mark(dve.memset(val, 0.0))
                ch.wait()
                f1, p1, q1, ce, cb = (v.rearrange("p b e -> p (b e)") for v in (flg, pos, t96, codee, codeb))
                ch(dve.tensor_tensor_scan(p1, ones[:, 0:96], f1, 0.0, ALU.mult, ALU.add))
                ch(dve.tensor_copy(val[:, 0:1], p1[:, 95:96]))
                ch(dve.tensor_tensor(p1, p1, f1, ALU.mult))
                for q in range(NOVER):
                    for c1, to in ((ce, val[:, 1 + q:2 + q]), (cb, vsh[:, q:q + 1])):
                        ch(dve.scalar_tensor_tensor(out=q1, in0=p1, scalar=float(q + 1), in1=c1,
                                                    op0=ALU.is_equal, op1=ALU.mult))
                        ch(dve.tensor_reduce(to, q1, AX, ALU.add))
                ch(dve.tensor_copy(ft[0:1, :], val[0:1, :]))
                ch.mark(dve.tensor_scalar(rbase[:, 0, :], eidx[:, :], float(P), None, ALU.mult))
                for b in range(3):
                    ch.mark(dve.tensor_scalar(rbase[:, 1 + b, :], pos[:, b, :], float(P),
                                              float((NE - 1) * P - P * (b + 1)), ALU.mult, ALU.add))
                ch.wait()
                for b in (3, 2, 1):
                    ch(dve.tensor_tensor(rbase[:, b, :], rbase[:, b, :], rbase[:, b - 1, :], ALU.subtract))
                for k in range(2):
                    A = A2[:, NT * k:NT * k + NT, :]
                    rank, part, row = s1[:, 9, :], s1[:, 8, :], rowi[:, k, :]
                    ch(dve.tensor_tensor(T32, A, RK, ALU.mult))
                    ch(dve.tensor_reduce(rank, T32, AX, ALU.add))
                    ch(dve.tensor_scalar(row, rank, 1.0, None, ALU.subtract))
                    for b in range(4):
                        ch(dve.tensor_tensor(T32, A, rbase[:, b:b + 1, :].to_broadcast([P, NT, NE]), ALU.mult))
                        ch(dve.tensor_reduce(part, T32, AX, ALU.add))
                        if b:
                            ch(dve.scalar_tensor_tensor(out=part, in0=rank, scalar=P * b + 0.5, in1=part,
                                                        op0=ALU.is_gt, op1=ALU.mult))
                        ch(dve.tensor_tensor(row, row, part, ALU.add))
                ch(dve.tensor_copy(rowu[:, :].rearrange("p (k t) -> p k t", k=2), rowi))
            stage(rt_pe, rt_act, rt_dve, rt_po)

            def matrix(j):
                return ring[j].rearrange("p (k c) -> p k c", c=(EF, EF, D)[j])

            def piece(q):
                j, i = divmod(q, PM)
                w = matrix(j)
                kt = w.shape[1] // PM
                at = 2 * MP * (q % NMB)
                return w[:, kt * i:kt * i + kt, :], parts(at, at + MP, kt, w.shape[2])

            def after(n):
                return not (isinstance(n, int) and n == 0)

            def split_high(act, n, q):
                raw, w = piece(q)
                if q % PM == 0:
                    act.wait_ge(w_moe[q // PM], (n + 1) * 16)
                if after(n) or q >= NMB:
                    act.wait_ge(x_use, n * NPC + (q - NMB + 1))
                act.activation(w.h, raw, ACT.Copy).then_inc(x_hi, 1)

            def split_low(dve, n, q):
                raw, w = piece(q)
                dve.wait_ge(x_hi, n * NPC + (q + 1))
                dve.tensor_tensor(w.l, raw, w.high_f, ALU.subtract).then_inc(x_lo, 1)

            def onehot(dve, n, col, ranks=None):
                rk = RK[:, :, bass.ds(col, 1)] if ranks is None else ranks
                if after(n):
                    dve.wait_ge(m_gx, n * 2)
                dve.tensor_tensor(OH, rank1[:, :].rearrange("p (o c) -> p o c", o=1).to_broadcast([P, NT, P]),
                                  rk.to_broadcast([P, NT, P]), ALU.is_equal).then_inc(m_oh, 1)

            def gather(pe, n, half):
                if half == 0:
                    pe.wait_ge(m_oh, n + 1)
                for t in range(NT):
                    for i, src in enumerate((xnp.h, xnp.l)):
                        m = pe.matmul(ps[:, half, :], OH[:, t, :], src[:, t, 512 * half:512 * half + 512],
                                      start=(t == 0 and i == 0), stop=(t == NT - 1 and i == 1))
                m.then_inc(m_gx, 1)

            def rows_a(act, n):
                act.wait_ge(m_gx, n * 2 + 1)
                act.activation(XR[:, 0:512], ps[:, 0, :], ACT.Copy).then_inc(m_ra, 1)

            def rows_v(dve, n):
                dve.wait_ge(m_gx, n * 2 + 2)
                dve.tensor_copy(XR[:, 512:1024], ps[:, 1, :]).then_inc(m_rv, 1)

            def turn_rows(pe, n, half):
                pe.wait_ge((m_ra, m_rv)[half], n + 1)
                for j in range(4):
                    m = pe.transpose(ps[:, 2 + half, j * P:j * P + P],
                                     XR[:, (4 * half + j) * P:(4 * half + j + 1) * P], ident[:, :])
                m.then_inc(m_gt, 1)

            def cols_high(act, n, half):
                act.wait_ge(m_gt, n * 2 + (half + 1))
                act.activation(XT.h[:, 4 * half:4 * half + 4, :],
                               ps[:, 2 + half, :].rearrange("p (k s) -> p k s", k=4), ACT.Copy).then_inc(m_gxh, 1)

            def cols_low(dve, n, half):
                dve.wait_ge(m_gxh, n * 2 + (half + 1))
                dve.tensor_tensor(XT.l[:, 4 * half:4 * half + 4, :],
                                  ps[:, 2 + half, :].rearrange("p (k s) -> p k s", k=4),
                                  XT.high_f[:, 4 * half:4 * half + 4, :], ALU.subtract).then_inc(m_gxl, 1)

            def three(pe, dst, a, b, first, last):
                pe.matmul(dst, a.h, b.h, start=first, stop=False)
                pe.matmul(dst, a.l, b.h, start=False, stop=False)
                return pe.matmul(dst, a.h, b.l, start=False, stop=last)

            def up(pe, n):
                pe.wait_ge(m_gxh, n * 2 + 2)
                pe.wait_ge(m_gxl, n * 2 + 2)
                for q in range(2 * PM):
                    pe.wait_ge(x_lo, n * NPC + (q + 1))
                    j, i = divmod(q, PM)
                    w = piece(q)[1]
                    kt = KD // PM
                    for k in range(kt):
                        m = three(pe, ps[:, 4 + j, :], XT[:, kt * i + k, :], w[:, k, :],
                                  i == 0 and k == 0, i == PM - 1 and k == kt - 1)
                    m.then_inc(x_use, 1)

            def turn(pe, n):
                pe.wait_ge(m_hb, n + 1)
                for j in range(4):
                    m = pe.transpose(ps[:, 4, j * P:j * P + P], HB[:, j * P:j * P + P], ident[:, :])
                m.then_inc(m_tr, 1)

            def down(pe, n, with_next=False):
                pe.wait_ge(m_hl, n + 1)
                if after(n):
                    pe.wait_ge(m_o, n * 2)
                for i in range(PM):
                    if with_next and i == PM // 2:
                        turn_rows(pe, n + 1, 1)
                    q = 2 * PM + i
                    pe.wait_ge(x_lo, n * NPC + (q + 1))
                    w = piece(q)[1]
                    for h in range(2):
                        m = three(pe, ps[:, 6 + h, :], HT[:, i, :], w[:, 0, h * 512:h * 512 + 512], i == 0, i == PM - 1)
                    m.then_inc(x_use, 1)

            def silu(act, n):
                act.wait_ge(x_use, n * NPC + PM)
                if after(n):
                    act.wait_ge(m_hb, n)
                act.activation(HS, ps[:, 4, :], ACT.Silu).then_inc(m_si, 1)

            def gated(dve, n):
                dve.wait_ge(x_use, n * NPC + 2 * PM)
                dve.wait_ge(m_si, n + 1)
                dve.tensor_tensor(HB, HS, ps[:, 5, :], ALU.mult).then_inc(m_hb, 1)

            def turned_high(act, n):
                act.wait_ge(m_tr, n + 1)
                act.activation(HT.h, ps[:, 4, :].rearrange("p (k s) -> p k s", k=4), ACT.Copy).then_inc(m_hh, 1)

            def turned_low(dve, n):
                dve.wait_ge(m_hh, n + 1)
                dve.tensor_tensor(HT.l, ps[:, 4, :].rearrange("p (k s) -> p k s", k=4), HT.high_f,
                                  ALU.subtract).then_inc(m_hl, 1)

            def store(act, n, row):
                act.wait_ge(x_use, n * NPC + NPC)
                if after(n):
                    act.wait_ge(m_st, n * 16)
                for h in range(2):
                    act.activation(OB[:, h * 512:h * 512 + 512], ps[:, 6 + h, :], ACT.Copy).then_inc(m_o, 1)
                act.wait_ge(m_o, n * 2 + 2)
                act.dma_start(obuf[bass.ds(row, P), :], OB).then_inc(m_st, 16)

            def block_pe(pe, n, with_next):
                up(pe, n)
                if with_next:
                    gather(pe, n + 1, 0)
                turn(pe, n)
                if with_next:
                    gather(pe, n + 1, 1)
                    turn_rows(pe, n + 1, 0)
                down(pe, n, with_next)

            def block_act(act, n, row, with_next):
                for q in (6, 7, 8, 9):
                    split_high(act, n, q)
                silu(act, n)
                for q in (10, 11):
                    split_high(act, n, q)
                if with_next:
                    split_high(act, n + 1, 0)
                    rows_a(act, n + 1)
                turned_high(act, n)
                if with_next:
                    split_high(act, n + 1, 1)
                    cols_high(act, n + 1, 0)
                    split_high(act, n + 1, 2)
                    cols_high(act, n + 1, 1)
                    for q in (3, 4, 5):
                        split_high(act, n + 1, q)
                store(act, n, row)

            def block_dve(dve, n, with_next):
                for q in (6, 7, 8, 9):
                    split_low(dve, n, q)
                if with_next:
                    onehot(dve, n + 1, n + 1)
                for q in (10, 11):
                    split_low(dve, n, q)
                gated(dve, n)
                if with_next:
                    split_low(dve, n + 1, 0)
                turned_low(dve, n)
                if with_next:
                    rows_v(dve, n + 1)
                    split_low(dve, n + 1, 1)
                    cols_low(dve, n + 1, 0)
                    split_low(dve, n + 1, 2)
                    cols_low(dve, n + 1, 1)
                    for q in (3, 4, 5):
                        split_low(dve, n + 1, q)

            def first_pe(pe, n):
                for half in range(2):
                    gather(pe, n, half)
                for half in range(2):
                    turn_rows(pe, n, half)

            def first_act(act, n):
                rows_a(act, n)
                for q in range(NMB):
                    split_high(act, n, q)
                for half in range(2):
                    cols_high(act, n, half)

            def first_dve(dve, n):
                rows_v(dve, n)
                for q in range(NMB):
                    split_low(dve, n, q)
                for half in range(2):
                    cols_low(dve, n, half)

            m_rk = sem("m_rk")

            def over(eng, body):
                n_over = eng.value_load(ft[0:1, 0:1], min_val=0, max_val=NOVER)
                for q in range(NOVER):
                    with eng.If(n_over > q):
                        body(q, NE + q)

            def expert_of(eng, q):
                return eng.value_load(ft[0:1, 1 + q:2 + q], min_val=0, max_val=NE - 1)

            def ex_pe(pe, ch):
                first_pe(pe, 0)
                block_pe(pe, 0, True)
                with pe.Fori(1, NE - 1) as n:
                    block_pe(pe, n, True)
                block_pe(pe, NE - 1, False)

                def body(q, n):
                    first_pe(pe, n)
                    block_pe(pe, n, False)
                over(pe, body)

            def ex_act(act, ch):
                first_act(act, 0)
                block_act(act, 0, 0, True)
                with act.Fori(1, NE - 1) as n:
                    block_act(act, n, n * P, True)
                block_act(act, NE - 1, (NE - 1) * P, False)
                act.wait_ge(m_st, 16 * NE)
                act.wait_ge(z_in, 16 * NOVER)

                def body(q, n):
                    first_act(act, n)
                    block_act(act, n, n * P, False)
                    act.wait_ge(m_st, 16 * (n + 1))
                over(act, body)

            def ex_dve(dve, ch):
                onehot(dve, 0, 0)
                first_dve(dve, 0)
                block_dve(dve, 0, True)
                with dve.Fori(1, NE - 1) as n:
                    block_dve(dve, n, True)
                block_dve(dve, NE - 1, False)

                def body(q, n):
                    e = expert_of(dve, q)
                    dve.tensor_scalar(rkq, RK[:, :, bass.ds(e, 1)], vsh[:, q:q + 1], None,
                                      ALU.subtract).then_inc(m_rk, 1)
                    dve.wait_ge(m_rk, q + 1)
                    onehot(dve, n, None, rkq)
                    first_dve(dve, n)
                    block_dve(dve, n, False)
                over(dve, body)
            stage(ex_pe, ex_act, ex_dve)

            gbuf = area(0, 0, 4, D)
            fsq = area(0, 4 * D, D)
            ss5, rs5, u5 = use(ssd, NT), use(rsd, NT), use(xsd, NT)

            def fin_po(po, ch):
                for t in range(NT):
                    for k in range(2):
                        if t >= 2:
                            po.wait_ge(g_use, 2 * (t - 2) + k + 1)
                        j = 2 * (t % 2) + k
                        po.indirect_dma_start(
                            out=gbuf[:, j, :], out_offset=None, in_=obuf,
                            in_offset=bass.IndirectOffsetOnAxis(ap=rowu[:, k * NT + t:k * NT + t + 1], axis=0),
                        ).then_inc(g_in[j], 16)
                for t in range(NT):
                    po.wait_ge(ssd, ss5 + t + 1)
                    v = ss[:, t:t + 1]
                    ch(po.tensor_scalar(v, v, 1.0 / D, EPS, ALU.mult, ALU.add))
                    po.tensor_tensor(v, v, nhalf[:, :], ALU.pow).then_inc(rsd, 1)

            def fin_dve(dve, ch):
                for t in range(NT):
                    for k in range(2):
                        j = 2 * (t % 2) + k
                        dve.wait_ge(g_in[j], 16 * (t // 2 + 1))
                        if k:
                            dve.wait_ge(g_use, 2 * t + 1)
                        dve.scalar_tensor_tensor(out=x[:, t, :], in0=gbuf[:, j, :], scalar=gate[:, k, t:t + 1],
                                                 in1=x[:, t, :], op0=ALU.mult, op1=ALU.add).then_inc(g_use, 1)
                dve.wait_ge(*gfin_in)
                for t in range(NT):
                    dve.wait_ge(rsd, rs5 + t + 1)
                    dve.scalar_tensor_tensor(out=x[:, t, :], in0=x[:, t, :], scalar=ss[:, t:t + 1], in1=gfin,
                                             op0=ALU.mult, op1=ALU.mult).then_inc(xsd, 1)

            def fin_act(act, ch):
                for t in range(NT):
                    act.wait_ge(g_use, 2 * t + 2)
                    if t:
                        act.wait_ge(ssd, ss5 + t)
                    act.activation(fsq, x[:, t, :], ACT.Square, accum_out=ss[:, t:t + 1]).then_inc(ssd, 1)
            last_x = (xsd, u5)
            last_stage = len(stages)
            stage(None, fin_act, fin_dve, fin_po)

        block = ctx.enter_context(nc.Block())

        def run(eng, which, chain):
            ch = Chain(eng, chain)
            for n, st_ in enumerate(stages):
                if which == 3:
                    for at, dst, src, s in late:
                        if at == n:
                            eng.dma_start(dst, src).then_inc(s, 16)
                if st_[which]:
                    st_[which](eng, ch)
                eng.drain().then_inc(phase, 1)
                eng.wait_ge(phase, 4 * (n + 1))

        @block.tensor
        def _(pe):
            run(pe, 0, phase)

        @block.scalar
        def _(act):
            run(act, 1, ach)

        @block.vector
        def _(dve):
            run(dve, 2, vch)

        @block.gpsimd
        def _(po):
            run(po, 3, pch)

        @block.sync
        def _(sp):
            for dst, src in crows:
                sp.dma_start(dst, src).then_inc(cst, 16)
            with nc.allow_non_contiguous_dma(reason="512 positions, once"):
                sp.dma_start(posi[:, :].rearrange("p (t a) -> p t a", a=1),
                             I["positions"][0].rearrange("(t p a) -> p t a", p=P, a=1)).then_inc(cst, 16)
            sp.dma_start(x[:, :, :], I["x"][0].rearrange("(t p) d -> p t d", p=P)).then_inc(xin, 16)
            for c, (loads, kt, n, _) in enumerate(chunks):
                if c >= NS:
                    sp.wait_ge(w_lo, chunks[c - NS][3])
                v = ring[c % NS][:, :kt * n].rearrange("p (k c) -> p k c", c=n)
                for src, c0 in loads:
                    with nc.allow_non_contiguous_dma(reason="narrow weights: gates and router"):
                        sp.dma_start(v[:, :, c0:c0 + src.shape[2]], src).then_inc(w_full[c % NS], 16)
            if on(7):
                def load(e, j):
                    src = I[("w1_2", "w3_2", "w2_2")[j]][0, bass.ds(e, 1)].rearrange("o (k p) c -> p (o k) c", p=P)
                    sp.dma_start(matrix(j), src).then_inc(w_moe[j], 16)
                sp.wait_ge(w_lo, chunks[-1][3])
                for j in range(3):
                    load(0, j)
                with sp.Fori(0, NE - 1) as n:
                    for j in range(3):
                        sp.wait_ge(x_lo, n * NPC + PM * (j + 1))
                        load(n + 1, j)
                sp.wait_ge(phase, 4 * (moe_bar + 1))
                n_over = sp.value_load(ft[0:1, 0:1], min_val=0, max_val=NOVER)
                for q in range(NOVER):
                    with sp.If(n_over > q):
                        sp.wait_ge(x_lo, NPC * (NE + q))
                        e = expert_of(sp, q)
                        for j in range(3):
                            load(e, j)
                for t in range(NT):
                    sp.wait_ge(xsd, last_x[1] + t + 1)
                    sp.dma_start(out[0, t * P:(t + 1) * P, :], x[:, t, :]).then_inc(out_s, 16)
            else:
                sp.wait_ge(phase, 4 * len(stages))
                for t in range(NT):
                    sp.dma_start(out[0, t * P:(t + 1) * P, :], x[:, t, :]).then_inc(out_s, 16)
            sp.wait_ge(out_s, 16 * NT)


_INS = [
    "x", "positions", "l0_attn_norm", "l0_w_in", "l0_mla_q_a_norm", "l0_mla_w_q_up", "l0_mla_kv_a_norm",
    "l0_mla_w_kv_up", "l0_mla_q_norm", "l0_mla_k_norm", "l0_w_o", "l0_ffn_norm", "l0_w_gate", "l0_w_up",
    "l0_w_down", "l1_attn_norm", "l1_w_in", "l1_fox_f_bias", "l1_fox_q_norm", "l1_fox_k_norm", "l1_w_o",
    "l1_ffn_norm", "l1_w_gate", "l1_w_up", "l1_w_down", "mem_2", "norm_mix_g_2", "w_in_2", "b_gate_2", "b_if_2",
    "conv_w_2", "conv_b_2", "mh_norm_g_2", "sgu_norm_g_2", "w_s_2", "b_s_2", "w_out_2", "norm_x_g_2",
    "norm_mem_g_2", "w_xq_2", "w_xkv_2", "w_xo_2", "norm_moe_g_2", "w_rg_2", "b_rg_2", "w_re_2", "b_re_2", "w1_2",
    "w3_2", "w2_2", "norm_f_g_2",
]


def kernel(**inputs):
    import numpy as _np
    import concourse.bacc as _bacc
    from concourse import mybir as _mybir
    from concourse.bass_utils import run_bass_kernel_spmd as _run

    nc = _bacc.Bacc("TRN2", target_bir_lowering=False, num_devices=1)
    arrays, aps = {}, {}
    for name in _INS:
        a = _np.ascontiguousarray(inputs[name])
        arrays[f"in_{name}"] = a
        aps[name] = nc.dram_tensor(f"in_{name}", a.shape, _mybir.dt.from_np(a.dtype), kind="ExternalInput").ap()
    out = nc.dram_tensor("out", (1, S, D), _mybir.dt.float32, kind="ExternalOutput").ap()
    bass_two_blocks_kernel(nc, aps, out)
    r = _run(nc, [arrays], core_ids=[0])
    return r.results[0]["out"]
```
